# Optimizing a Trainium2 kernel written in Bass

```python
import math
import jax, jax.numpy as jnp
from jax import lax
import numpy as np

D_MODEL = 1024
BATCH = 1
SEQ = 1024
DEPTH = 1

CHUNK = 64

GDN_HEADS = 4
GDN_HEAD_DIM = 128
GDN_WIDTH = GDN_HEADS * GDN_HEAD_DIM
GDN_CONV = 4

SWA_HEADS = 8
SWA_KV_HEADS = 2
SWA_HEAD_DIM = 64
SWA_WIDTH = SWA_HEADS * SWA_HEAD_DIM
SWA_KV_WIDTH = SWA_KV_HEADS * SWA_HEAD_DIM
SWA_WINDOW = 128
SWA_WIN_CHUNKS = SWA_WINDOW // CHUNK

MIX_WIDTH = GDN_WIDTH + SWA_WIDTH
IN_SIZES = (3 * GDN_WIDTH, GDN_WIDTH, GDN_HEADS, GDN_HEADS, SWA_WIDTH, SWA_KV_WIDTH, SWA_KV_WIDTH)
IN_WIDTH = 4 * GDN_WIDTH + 2 * GDN_HEADS + SWA_WIDTH + 2 * SWA_KV_WIDTH

PEER_HEADS = 8
PEER_N_KEYS = 128
PEER_N_EXPERTS = PEER_N_KEYS * PEER_N_KEYS
PEER_QUERY_DIM = 256
PEER_HALF = PEER_QUERY_DIM // 2
PEER_TOPK = 16
PEER_TOKEN_BLOCK = 128

DEEPNORM_ALPHA = (2.0 * DEPTH) ** 0.25
DEEPNORM_BETA = (8.0 * DEPTH) ** -0.25

LN_EPS = 1e-5
RMS_EPS = 1e-6
L2_EPS = 1e-6

kernel_name = 'hybrid_gdn_swa_sink_peer_deepnorm'

def layer_norm(x, g, b):
    xf = x.astype(jnp.float32)
    mu = jnp.mean(xf, -1, keepdims=True)
    var = jnp.mean(jnp.square(xf - mu), -1, keepdims=True)
    y = (xf - mu) * lax.rsqrt(var + LN_EPS) * g.astype(jnp.float32) + b.astype(jnp.float32)
    return y.astype(x.dtype)

def l2_normalize(t):
    t = t.astype(jnp.float32)
    return t * lax.rsqrt(jnp.sum(t * t, -1, keepdims=True) + L2_EPS)

def causal_depthwise_conv(x, w):
    k = w.shape[0]
    return lax.conv_general_dilated(
        x, w[:, None, :].astype(x.dtype), window_strides=(1,), padding=[(k - 1, 0)],
        dimension_numbers=('NWC', 'WIO', 'NWC'), feature_group_count=x.shape[-1])

def gated_delta_rule_chunked(q, k, v, g, beta):
    B, H, S, Dk = q.shape
    Dv = v.shape[-1]
    nc = S // CHUNK
    q = q.reshape(B, H, nc, CHUNK, Dk)
    k = k.reshape(B, H, nc, CHUNK, Dk)
    v = v.reshape(B, H, nc, CHUNK, Dv)
    beta = beta.reshape(B, H, nc, CHUNK)
    gam = jnp.cumsum(g.reshape(B, H, nc, CHUNK), axis=-1)
    pos = jnp.arange(CHUNK)
    incl = pos[:, None] >= pos[None, :]
    decay = jnp.exp(jnp.where(incl, gam[..., :, None] - gam[..., None, :], -jnp.inf))
    strict_decay = jnp.where(pos[:, None] > pos[None, :], decay, 0.0)
    a_mat = beta[..., :, None] * strict_decay * jnp.einsum('bhnid,bhnjd->bhnij', k, k)
    rhs = jnp.concatenate([beta[..., None] * v, (beta * jnp.exp(gam))[..., None] * k], axis=-1)
    sol = lax.linalg.triangular_solve(a_mat, rhs, left_side=True, lower=True, unit_diagonal=True)
    u_v, w = sol[..., :Dv], sol[..., Dv:]
    qk = jnp.einsum('bhnid,bhnjd->bhnij', q, k) * decay
    q_dec = q * jnp.exp(gam)[..., None]
    k_dec = k * jnp.exp(gam[..., -1:] - gam)[..., None]
    chunk_decay = jnp.exp(gam[..., -1])

    def step(state, xs):
        u_v_c, w_c, qk_c, q_c, k_c, d_c = xs
        u = u_v_c - jnp.einsum('bhik,bhkv->bhiv', w_c, state)
        o = jnp.einsum('bhik,bhkv->bhiv', q_c, state) + jnp.einsum('bhij,bhjv->bhiv', qk_c, u)
        state = d_c[..., None, None] * state + jnp.einsum('bhik,bhiv->bhkv', k_c, u)
        return state, o

    xs = tuple(jnp.moveaxis(t, 2, 0) for t in (u_v, w, qk, q_dec, k_dec, chunk_decay))
    state0 = jnp.zeros((B, H, Dk, Dv), jnp.float32)
    _, o = lax.scan(step, state0, xs)
    return jnp.moveaxis(o, 0, 2).reshape(B, H, S, Dv)

def gated_deltanet(qkv, z, b_raw, a_raw, conv_w, a_log, dt_bias, norm_w):
    B, S, _ = qkv.shape
    f32 = jnp.float32
    qkv = jax.nn.silu(causal_depthwise_conv(qkv, conv_w))
    q, k, v = jnp.split(qkv, 3, axis=-1)
    heads = lambda t: t.reshape(B, S, GDN_HEADS, GDN_HEAD_DIM).transpose(0, 2, 1, 3)
    q = l2_normalize(heads(q)) * GDN_HEAD_DIM ** -0.5
    k = l2_normalize(heads(k))
    v = heads(v).astype(f32)
    beta = jax.nn.sigmoid(b_raw.astype(f32)).transpose(0, 2, 1)
    g = (-jnp.exp(a_log.astype(f32)) * jax.nn.softplus(a_raw.astype(f32) + dt_bias.astype(f32))).transpose(0, 2, 1)
    o = gated_delta_rule_chunked(q, k, v, g, beta).transpose(0, 2, 1, 3)
    o = o * lax.rsqrt(jnp.mean(o * o, -1, keepdims=True) + RMS_EPS) * norm_w.astype(f32)
    o = o * jax.nn.silu(z.astype(f32)).reshape(B, S, GDN_HEADS, GDN_HEAD_DIM)
    return o.reshape(B, S, GDN_WIDTH).astype(qkv.dtype)

def sliding_window_sink_attention(q, k, v, sinks):
    B, S, _, D = q.shape
    nc = S // CHUNK
    grp = SWA_HEADS // SWA_KV_HEADS
    qc = q.astype(jnp.float32).reshape(B, nc, CHUNK, SWA_KV_HEADS, grp, D)

    def band(t):
        t = t.astype(jnp.float32).reshape(B, nc, CHUNK, SWA_KV_HEADS, D)
        t = jnp.concatenate([jnp.zeros((B, SWA_WIN_CHUNKS - 1, CHUNK, SWA_KV_HEADS, D), t.dtype), t], axis=1)
        return jnp.concatenate([t[:, i:i + nc] for i in range(SWA_WIN_CHUNKS)], axis=2)

    kb, vb = band(k), band(v)
    key_chunk = jnp.arange(nc)[:, None] - (SWA_WIN_CHUNKS - 1) + jnp.arange(SWA_WIN_CHUNKS)[None, :]
    valid = jnp.repeat(key_chunk >= 0, CHUNK, axis=1)
    s = jnp.einsum('bnqhgd,bnkhd->bnhgqk', qc, kb) * D ** -0.5
    s = jnp.where(valid[None, :, None, None, None, :], s, -jnp.inf)
    sink = sinks.astype(jnp.float32).reshape(1, 1, SWA_KV_HEADS, grp, 1, 1)
    m = jnp.maximum(jnp.max(s, -1, keepdims=True), sink)
    p = jnp.exp(s - m)
    p = p / (jnp.sum(p, -1, keepdims=True) + jnp.exp(sink - m))
    o = jnp.einsum('bnhgqk,bnkhd->bnqhgd', p, vb)
    return o.reshape(B, S, SWA_HEADS * D).astype(q.dtype)

def token_mixer(x, w_in, conv_w, a_log, dt_bias, norm_w, sinks, w_out):
    B, S, _ = x.shape
    proj = x @ w_in
    split_at = np.cumsum(IN_SIZES)[:-1].tolist()
    qkv, z, b_raw, a_raw, sq, sk, sv = jnp.split(proj, split_at, axis=-1)
    gdn = gated_deltanet(qkv, z, b_raw, a_raw, conv_w, a_log, dt_bias, norm_w)
    swa = sliding_window_sink_attention(
        sq.reshape(B, S, SWA_HEADS, SWA_HEAD_DIM),
        sk.reshape(B, S, SWA_KV_HEADS, SWA_HEAD_DIM),
        sv.reshape(B, S, SWA_KV_HEADS, SWA_HEAD_DIM), sinks)
    return jnp.concatenate([gdn, swa], axis=-1) @ w_out

def peer_ffn(x, wq, k1, k2, u, v):
    B, S, D = x.shape
    f32 = jnp.float32
    xt = x.reshape(-1, D)
    n_tok = xt.shape[0]
    q = (xt @ wq).astype(f32).reshape(n_tok, PEER_HEADS, 2, PEER_HALF)
    s1 = jnp.einsum('thd,hnd->thn', q[:, :, 0], k1.astype(f32))
    s2 = jnp.einsum('thd,hnd->thn', q[:, :, 1], k2.astype(f32))
    t1, i1 = lax.top_k(s1, PEER_TOPK)
    t2, i2 = lax.top_k(s2, PEER_TOPK)
    n_cand = PEER_TOPK * PEER_TOPK
    cand_s = (t1[..., :, None] + t2[..., None, :]).reshape(n_tok, PEER_HEADS, n_cand)
    cand_i = (i1[..., :, None] * PEER_N_KEYS + i2[..., None, :]).reshape(n_tok, PEER_HEADS, n_cand)
    top_s, top_pos = lax.top_k(cand_s, PEER_TOPK)
    expert = jnp.take_along_axis(cand_i, top_pos, axis=-1)
    gate = jax.nn.softmax(top_s, axis=-1)
    n_sel = PEER_HEADS * PEER_TOPK
    n_blk = n_tok // PEER_TOKEN_BLOCK

    def expert_block(args):
        xb, eb, gb = args
        h = jnp.einsum('td,ted->te', xb.astype(f32), u[eb].astype(f32))
        a = jax.nn.gelu(h, approximate=False) * gb
        return jnp.einsum('te,ted->td', a, v[eb].astype(f32))

    y = lax.map(expert_block, (xt.reshape(n_blk, PEER_TOKEN_BLOCK, D),
                               expert.reshape(n_blk, PEER_TOKEN_BLOCK, n_sel),
                               gate.reshape(n_blk, PEER_TOKEN_BLOCK, n_sel)))
    return y.reshape(B, S, D).astype(x.dtype)

def setup_inputs(seed: int = 0) -> dict:
    key = jax.random.key(seed)
    ks = jax.random.split(key, 18)
    f32 = jnp.float32
    L = DEPTH
    nrm = lambda k, shape, s: jax.random.normal(k, shape, f32) * s
    x = jax.random.normal(ks[0], (BATCH, SEQ, D_MODEL), f32)
    w_in = nrm(ks[1], (L, D_MODEL, IN_WIDTH), D_MODEL ** -0.5)
    gdn_conv_w = nrm(ks[2], (L, GDN_CONV, 3 * GDN_WIDTH), GDN_CONV ** -0.5)
    gdn_a_log = jnp.log(jax.random.uniform(ks[3], (L, GDN_HEADS), f32, 1.0, 16.0))
    dt = jnp.exp(jax.random.uniform(ks[4], (L, GDN_HEADS), f32, math.log(1e-3), math.log(1e-1)))
    gdn_dt_bias = dt + jnp.log(-jnp.expm1(-dt))
    gdn_norm_w = 1.0 + nrm(ks[5], (L, GDN_HEAD_DIM), 0.02)
    swa_sinks = nrm(ks[6], (L, SWA_HEADS), 0.5)
    w_out = nrm(ks[7], (L, MIX_WIDTH, D_MODEL), DEEPNORM_BETA * MIX_WIDTH ** -0.5)
    ln1_g = 1.0 + nrm(ks[8], (L, D_MODEL), 0.02)
    ln1_b = nrm(ks[9], (L, D_MODEL), 0.02)
    peer_wq = nrm(ks[10], (L, D_MODEL, PEER_HEADS * PEER_QUERY_DIM), D_MODEL ** -0.5)
    peer_k1 = nrm(ks[11], (L, PEER_HEADS, PEER_N_KEYS, PEER_HALF), PEER_HALF ** -0.5)
    peer_k2 = nrm(ks[12], (L, PEER_HEADS, PEER_N_KEYS, PEER_HALF), PEER_HALF ** -0.5)
    peer_u = nrm(ks[13], (L, PEER_N_EXPERTS, D_MODEL), D_MODEL ** -0.5)
    peer_v = nrm(ks[14], (L, PEER_N_EXPERTS, D_MODEL), DEEPNORM_BETA)
    ln2_g = 1.0 + nrm(ks[15], (L, D_MODEL), 0.02)
    ln2_b = nrm(ks[16], (L, D_MODEL), 0.02)
    return {'x': x, 'w_in': w_in, 'gdn_conv_w': gdn_conv_w, 'gdn_a_log': gdn_a_log,
            'gdn_dt_bias': gdn_dt_bias, 'gdn_norm_w': gdn_norm_w, 'swa_sinks': swa_sinks,
            'w_out': w_out, 'ln1_g': ln1_g, 'ln1_b': ln1_b, 'peer_wq': peer_wq,
            'peer_k1': peer_k1, 'peer_k2': peer_k2, 'peer_u': peer_u, 'peer_v': peer_v,
            'ln2_g': ln2_g, 'ln2_b': ln2_b}

def reference(x, w_in, gdn_conv_w, gdn_a_log, gdn_dt_bias, gdn_norm_w, swa_sinks, w_out,
              ln1_g, ln1_b, peer_wq, peer_k1, peer_k2, peer_u, peer_v, ln2_g, ln2_b):
    h = x
    for l in range(DEPTH):
        mix = token_mixer(h, w_in[l], gdn_conv_w[l], gdn_a_log[l], gdn_dt_bias[l], gdn_norm_w[l],
                          swa_sinks[l], w_out[l])
        h = layer_norm(DEEPNORM_ALPHA * h + mix, ln1_g[l], ln1_b[l])
        ffn = peer_ffn(h, peer_wq[l], peer_k1[l], peer_k2[l], peer_u[l], peer_v[l])
        h = layer_norm(DEEPNORM_ALPHA * h + ffn, ln2_g[l], ln2_b[l])
    return h


_drawn_inputs = setup_inputs


def setup_inputs(seed=0):
    import zlib

    import numpy as np

    out = dict(_drawn_inputs(seed))
    spreads = {}
    factors = {'gdn_norm_w': 3.111, 'swa_sinks': 8.0, 'ln2_g': 2.864, 'ln2_b': 2.858}
    for name, (base, spread) in spreads.items():
        noise = np.random.default_rng([zlib.crc32(name.encode()), seed]).standard_normal(out[name].shape)
        drawn = base * np.exp(spread * noise) if base else spread * noise
        out[name] = __import__('jax').numpy.asarray(drawn.astype(out[name].dtype))
    for name, factor in factors.items():
        out[name] = (out[name] * factor).astype(out[name].dtype)
    return out
```

```python
from contextlib import ExitStack, contextmanager

import concourse.bass as bass
import numpy as np
from concourse import mybir

F32 = mybir.dt.float32
F32R = mybir.dt.float32r
U32 = mybir.dt.uint32
ALU = mybir.AluOpType
ACT = mybir.ActivationFunctionType
AX = mybir.AxisListType.X

P = 128
T = 1024
D = 1024
NT = T // P
KC = D // P
GH = 4
AH = 8
AD = 64
N_CH = 16
N_CONV = 12
PH = 8
TOPK = 16
NK = 128
HALF = 512
TG = 64
ALPHA = 2.0 ** 0.25
LN_EPS = 1e-5
RMS_EPS = 1e-6
L2_EPS = 1e-6
MASKED = -1e30
REPLACED = -3e38
LEVELS = 7

C_ID, C_TRIU, C_NEG, C_ONES, C_LEVEL = 0, 128, 256, 384, 512
C_IOTA = C_LEVEL + LEVELS * 128
C_IOTA16 = C_IOTA + 128
C_EPS = C_IOTA16 + 16
C_N = C_EPS + 4


def constants():
    c = np.zeros((P, C_N), np.float32)
    i, j = np.arange(P)[:, None], np.arange(P)[None, :]
    c[:, C_ID:C_ID + 128] = i == j
    c[:, C_TRIU:C_TRIU + 128] = i <= j
    c[:, C_NEG:C_NEG + 128] = np.where(j >= i, 0.0, MASKED)
    c[:, C_ONES:C_ONES + 128] = 1.0
    for n in range(LEVELS):
        bi, bj = i >> n, j >> n
        c[:, C_LEVEL + 128 * n:C_LEVEL + 128 * (n + 1)] = np.where((bi % 2 == 1) & (bj == bi - 1), -1.0, 0.0)
    c[:, C_IOTA:C_IOTA + 128] = j
    c[:, C_IOTA16:C_IOTA16 + 16] = np.arange(16)
    c[:, C_EPS + 0] = LN_EPS
    c[:, C_EPS + 1] = RMS_EPS
    c[:, C_EPS + 2] = L2_EPS
    c[:, C_EPS + 3] = L2_EPS * P
    return c


def window_masks():
    q = np.arange(P)[:, None] // 64
    k = np.arange(2 * P)[None, :] // 64
    m = np.where((k == q + 1) | (k == q + 2), 0.0, MASKED).astype(np.float32)
    out = np.stack([m] * NT)
    out[0, :, :P] = MASKED
    return out


def ts(start, size):
    return bass.ds(start, size)


def wait_apart(engine, tick, semaphore, value):
    engine.wait_ge(semaphore, value)
    engine.sem_inc(tick, 1)


@contextmanager
def stage_semaphores(nc):
    used = []

    def sem(name):
        used.append(nc.alloc_semaphore(name))
        return used[-1]

    yield sem
    nc.clear_and_free_semaphores(used)
    nc.all_engine_barrier()


def project(nc, sem, io, scr, ba, psum):
    with ExitStack() as ctx:
        def sb(name, shape, dt=F32):
            return ctx.enter_context(nc.sbuf_tensor(name, shape, dt))

        xT = sb("p_xT", [P, KC, T])
        w = [sb(f"p_w{s}", [P, KC, P]) for s in range(2)]
        wz = sb("p_wz", [P, KC, GH * P])
        ws = sb("p_ws", [P, KC, P + 8])
        convw = sb("p_convw", [P, N_CONV, 4])
        normw = sb("p_normw", [P, P])
        raw = [sb(f"p_raw{s}", [P, 3 + T]) for s in range(2)]
        cv = [sb(f"p_cv{s}", [P, T]) for s in range(2)]
        out = [sb(f"p_out{s}", [P, T]) for s in range(2)]
        zt = [sb(f"p_zt{s}", [P, GH * P]) for s in range(2)]
        svt = [sb(f"p_sv{s}", [P, P]) for s in range(2)]
        zero = sb("p_zero", [P, P])
        ps = [psum[:, 2 * s:2 * s + 2, :] for s in range(2)]

        x_in = sem("x_in")
        side_in = sem("side_in")
        tail_in = sem("tail_in")
        w_in = [sem(f"w_in{s}") for s in range(2)]
        mm = [sem(f"proj_mm{s}") for s in range(2)]
        evac = [sem(f"proj_evac{s}") for s in range(2)]
        zeroed = sem("proj_zeroed")
        conv_step = sem("conv_step")
        conv_done = [sem(f"conv_done{s}") for s in range(2)]
        silu = [sem(f"silu{s}") for s in range(2)]
        stored = [sem(f"ch_stored{s}") for s in range(2)]
        gated = [sem(f"z_gated{s}") for s in range(2)]
        tok_stored = [sem(f"tok_stored{s}") for s in range(2)]
        pad_stored = sem("pad_stored")
        N_BLK = N_CH + 1
        with nc.Block() as block:
            @block.sync
            def _(sp):
                sp.dma_start(w[0][:], io["w_ch"][0]).then_inc(w_in[0], 16)
                sp.dma_start(xT[:], io["xT"].rearrange("(k p) t -> p k t", p=P)).then_inc(x_in, 16)
                sp.dma_start(w[1][:], io["w_ch"][1]).then_inc(w_in[1], 16)
                sp.dma_start(convw[:], io["conv_w"]).then_inc(side_in, 16)
                sp.dma_start(normw[:], io["norm_w"].partition_broadcast(P)).then_inc(side_in, 16)
                with sp.Fori(1, N_CH // 2) as i:
                    for s in range(2):
                        sp.wait_ge(mm[s], i)
                        sp.dma_start(w[s][:], io["w_ch"][2 * i + s]).then_inc(w_in[s], 16)
                sp.wait_ge(mm[0], N_CH // 2)
                sp.dma_start(w[0][:], io["w_ch"][N_CH]).then_inc(w_in[0], 16)
                sp.dma_start(wz[:], io["w_z"]).then_inc(tail_in, 16)
                sp.dma_start(ws[:], io["w_s"]).then_inc(tail_in, 16)

            @block.tensor
            def _(pe):
                def channel_block(s, n):
                    pe.wait_ge(w_in[s], 16 * (n + 1))
                    pe.wait_ge(evac[s], n)
                    for h in range(2):
                        for k in range(KC):
                            last = nc.tensor.matmul(ps[s][:, h, :], w[s][:, k, :], xT[:, k, h * HALF:(h + 1) * HALF],
                                                    start=(k == 0), stop=(k == KC - 1))
                    last.then_inc(mm[s], 1)

                pe.wait_ge(x_in, 16)
                with pe.Fori(0, N_CH // 2) as i:
                    for s in range(2):
                        channel_block(s, i)
                channel_block(0, N_CH // 2)
                pe.wait_ge(tail_in, 32)
                for t in range(NT):
                    s = (t + 1) % 2
                    n = N_CH // 2 + (1 if s == 0 else 0) + t // 2
                    pe.wait_ge(evac[s], n)
                    for k in range(KC):
                        nc.tensor.matmul(ps[s][:, 0, :], xT[:, k, t * P:(t + 1) * P], wz[:, k, :],
                                         start=(k == 0), stop=(k == KC - 1))
                    for k in range(KC):
                        last = nc.tensor.matmul(ps[s][:, 1, 0:P + 8], xT[:, k, t * P:(t + 1) * P], ws[:, k, :],
                                                start=(k == 0), stop=(k == KC - 1))
                    last.then_inc(mm[s], 1)

            @block.scalar
            def _(act):
                act.wait_ge(zeroed, 3)
                with act.Fori(0, N_CONV // 2) as i:
                    for s in range(2):
                        act.wait_ge(mm[s], i + 1)
                        act.wait_ge(conv_done[s], i)
                        nc.scalar.activation(raw[s][:, 3:3 + T], ps[s].rearrange("p h t -> p (h t)"),
                                             ACT.Copy).then_inc(evac[s], 1)
                        act.wait_ge(conv_done[s], i + 1)
                        act.wait_ge(stored[s], 16 * i)
                        nc.scalar.activation(out[s][:], cv[s][:], ACT.Silu).then_inc(silu[s], 1)
                for b in range(N_CONV, N_BLK):
                    s, n = b % 2, b // 2
                    act.wait_ge(mm[s], n + 1)
                    act.wait_ge(stored[s], 16 * n)
                    nc.scalar.activation(out[s][:], ps[s].rearrange("p h t -> p (h t)"), ACT.Copy).then_inc(evac[s], 1)
                for t in range(NT):
                    s = (t + 1) % 2
                    n = N_CH // 2 + (1 if s == 0 else 0) + t // 2
                    act.wait_ge(mm[s], n + 1)
                    if t >= 2:
                        act.wait_ge(tok_stored[s], 32 * (t // 2))
                    nc.scalar.activation(zt[s][:], ps[s][:, 0, :], ACT.Silu).then_inc(gated[s], 1)
                    nc.scalar.activation(svt[s][:], ps[s][:, 1, 0:P], ACT.Copy)
                    nc.scalar.activation(ba[:, t, :], ps[s][:, 1, P:P + 8], ACT.Copy).then_inc(evac[s], 1)

            @block.vector
            def _(dve):
                nc.vector.memset(raw[0][:, 0:3], 0.0).then_inc(zeroed, 1)
                nc.vector.memset(raw[1][:, 0:3], 0.0).then_inc(zeroed, 1)
                nc.vector.memset(zero[:], 0.0).then_inc(zeroed, 1)
                dve.wait_ge(side_in, 32)
                with dve.Fori(0, N_CONV // 2) as i:
                    for s in range(2):
                        b = 2 * i + s
                        dve.wait_ge(evac[s], i + 1)
                        dve.wait_ge(silu[s], i)
                        nc.vector.tensor_scalar(cv[s][:], raw[s][:, 0:T], convw[:, ts(b, 1), 0], None,
                                                ALU.mult).then_inc(conv_step, 1)
                        for k in range(1, 4):
                            dve.wait_ge(conv_step, b * 3 + k)
                            step = nc.vector.scalar_tensor_tensor(cv[s][:], raw[s][:, k:k + T], convw[:, ts(b, 1), k],
                                                                  cv[s][:], ALU.mult, ALU.add)
                            step.then_inc(conv_step if k < 3 else conv_done[s], 1)
                for t in range(NT):
                    s = (t + 1) % 2
                    dve.wait_ge(gated[s], t // 2 + 1)
                    zv = zt[s].rearrange("p (h d) -> p h d", h=GH)
                    nc.vector.tensor_tensor(zv, zv, normw[:, :].unsqueeze(1).broadcast_to([P, GH, P]),
                                            ALU.mult).then_inc(silu[s], 1)

            @block.gpsimd
            def _(pool):
                pool.wait_ge(zeroed, 3)
                pool.dma_start(scr["sk"][:, 0:P], zero[:]).then_inc(pad_stored, 16)
                pool.dma_start(scr["sv"][0:P, :], zero[:]).then_inc(pad_stored, 16)
                with pool.Fori(0, N_CONV // 2) as i:
                    for s in range(2):
                        pool.wait_ge(silu[s], i + 1)
                        pool.dma_start(scr["ch"][2 * i + s], out[s][:]).then_inc(stored[s], 16)
                for b in range(N_CONV, N_CH):
                    s, n = b % 2, b // 2
                    pool.wait_ge(evac[s], n + 1)
                    pool.dma_start(scr["ch"][b], out[s][:]).then_inc(stored[s], 16)
                pool.wait_ge(evac[0], N_CH // 2 + 1)
                pool.dma_start(scr["sk"][:, P:P + T], out[0][:]).then_inc(stored[0], 16)
                for t in range(NT):
                    s = (t + 1) % 2
                    pool.wait_ge(silu[s], N_CONV // 2 + t // 2 + 1)
                    pool.dma_start(scr["z"][t * P:(t + 1) * P, :], zt[s][:]).then_inc(tok_stored[s], 16)
                    pool.wait_ge(evac[s], N_CH // 2 + (1 if s == 0 else 0) + t // 2 + 1)
                    pool.dma_start(scr["sv"][(t + 1) * P:(t + 2) * P, :], svt[s][:]).then_inc(tok_stored[s], 16)
                pool.wait_ge(pad_stored, 32)
                pool.wait_ge(stored[0], 16 * (N_CH // 2 + 1))
                pool.wait_ge(stored[1], 16 * (N_CH // 2))
                for s in range(2):
                    pool.wait_ge(tok_stored[s], 16 * NT)


def mix_tokens(nc, sem, io, scr, ba, cst, psum):
    with ExitStack() as ctx:
        def sb(name, shape, dt=F32):
            return ctx.enter_context(nc.sbuf_tensor(name, shape, dt))

        ident = cst[:, C_ID:C_ID + P]
        triu = cst[:, C_TRIU:C_TRIU + P]
        neg = cst[:, C_NEG:C_NEG + P]
        ones = cst[:, C_ONES:C_ONES + P]

        def heads(ap):
            return ap.unsqueeze(1).broadcast_to([P, GH, P])

        wout = sb("m_wout", [P, KC, D])
        lng = sb("m_lng", [P, D])
        lnb = sb("m_lnb", [P, D])
        sinks = sb("m_sinks", [P, AH])
        dtb = sb("m_dtb", [P, GH])
        alog = sb("m_alog", [P, GH])
        ch = [sb(f"m_ch{s}", [P, N_CH, P]) for s in range(2)]
        kw = [sb(f"m_kw{s}", [P, 2 * P]) for s in range(2)]
        vw = [sb(f"m_vw{s}", [P, 2, P]) for s in range(2)]
        zw = [sb(f"m_zw{s}", [P, GH, P]) for s in range(2)]
        wm = [sb(f"m_wm{s}", [P, 2 * P]) for s in range(2)]
        xt = [sb(f"m_xt{s}", [P, D]) for s in range(2)]
        small = {n: sb(f"m_{n}", [P, NT, GH]) for n in
                 ("beta", "soft", "mag", "g", "gam", "egam", "kdec", "nbeg", "decay", "tmp")}
        sq = sb("m_sq", [P, 2 * GH, P])
        rn = sb("m_rn", [P, 2 * GH, P])
        qk = sb("m_qk", [P, 2 * GH, P])
        kd = sb("m_kd", [P, GH, P])
        vb = sb("m_vb", [P, GH, P])
        gB = sb("m_gB", [P, GH, P])
        bB = sb("m_bB", [P, GH, P])
        dm = sb("m_dm", [P, GH, P])
        eg = sb("m_eg", [P, GH, P])
        qd = sb("m_qd", [P, GH, P])
        qkd = sb("m_qkd", [P, GH, P])
        at = sb("m_at", [P, GH, P])
        tu = sb("m_tu", [P, 2, GH, P])
        xs = sb("m_xs", [P, GH, P])
        uu = sb("m_uu", [P, GH, P])
        state = sb("m_state", [P, GH, P])
        og = sb("m_og", [P, GH, P])
        rms = sb("m_rms", [P, GH])
        mixT = sb("m_mixT", [P, KC, P])
        sc = sb("m_sc", [P, AH, 2 * P])
        pT = sb("m_pT", [P, AH, 2, P])
        on = sb("m_on", [P, AH, AD])
        mx = sb("m_mx", [P, 4, AH])
        h1 = sb("m_h1", [P, D])
        st = sb("m_st", [P, 2, 6])
        mv = sb("m_mv", [P, 3])

        A0, A1, B0, B1, C0, C1, D0, D1 = (psum[:, b, :].rearrange("p (h d) -> p h d", h=GH) for b in range(8))

        side_in = sem("mix_side_in")
        wout_in = sem("wout_in")
        tile_in = [[sem(f"tile_in{s}_{n}") for n in range(6)] for s in range(2)]
        prep = sem("prep_step")
        tile_read = sem("tile_read")
        x1_out = sem("x1_stored")
        names = ("sq ss root rn qk tr kd vb gB bB bc egx e_raw e_neg dmx qd kq qkd at0 at tu0 ks r2 u_mm u_ev o_ds "
                 "st_up osq osum oroot orec og ogT mg s_mm s_mask s_max s_mx s_nmx s_es s_p s_den s_rec p_tr p_ev "
                 "o_mm o_n onT ma proj h1 stat aggr root1 rec1 nrm nrm_g x1").split()
        S = {n: sem(f"m_{n}") for n in names}
        soft_done = sem("soft_done")
        tick = sem("m_tick")
        lx, lm, lt, le = sem("level_x"), sem("level_masked"), sem("level_t"), sem("level_evac")

        def load_tile(sp, c, s):
            for n, (dst, src) in enumerate((
                    (ch[s][:], scr["ch"][:, :, ts(c * P, P)].rearrange("b p t -> p b t")),
                    (kw[s][:], scr["sk"][:, ts(c * P, 2 * P)]),
                    (vw[s][:], scr["sv"][ts(c * P, 2 * P), :].rearrange("(a p) d -> p a d", a=2)),
                    (zw[s][:], scr["z"][ts(c * P, P), :].rearrange("p (h d) -> p h d", h=GH)),
                    (wm[s][:], io["wmask"][ts(c, 1)].rearrange("a p k -> (a p) k")),
                    (xt[s][:], io["x"][ts(c * P, P), :]))):
                sp.dma_start(dst, src).then_inc(tile_in[s][n], 16)

        with nc.Block() as block:
            @block.sync
            def _(sp):
                sp.dma_start(sinks[:], io["sinks"].partition_broadcast(P)).then_inc(side_in, 16)
                sp.dma_start(dtb[:], io["dt_bias"].partition_broadcast(P)).then_inc(side_in, 16)
                sp.dma_start(alog[:], io["a_log"].partition_broadcast(P)).then_inc(side_in, 16)
                sp.dma_start(lng[:], io["ln1_g"].partition_broadcast(P)).then_inc(side_in, 16)
                sp.dma_start(lnb[:], io["ln1_b"].partition_broadcast(P)).then_inc(side_in, 16)
                for s in range(2):
                    load_tile(sp, s, s)
                sp.dma_start(wout[:], io["w_out"].rearrange("(k p) n -> p k n", p=P)).then_inc(wout_in, 16)

                def store_x1(c):
                    sp.wait_ge(S["x1"], c + 1)
                    sp.dma_start(scr["x1"][ts(c * P, P), :], h1[:]).then_inc(x1_out, 16)

                with sp.Fori(0, NT // 2 - 1) as i:
                    for s in range(2):
                        store_x1(2 * i + s)
                        load_tile(sp, 2 * i + s + 2, s)
                for s in range(2):
                    store_x1(NT - 2 + s)
                sp.wait_ge(x1_out, 16 * NT)

            @block.tensor
            def _(pe):
                pe.wait_ge(prep, 8)
                nc.tensor.matmul(psum[:, 0, 0:NT * GH], triu, small["g"].rearrange("p t h -> p (t h)"),
                                 start=True, stop=True)
                nc.tensor.matmul(psum[:, 1, 0:NT * GH], ones, small["g"].rearrange("p t h -> p (t h)"),
                                 start=True, stop=True).then_inc(prep, 1)
                pe.wait_ge(prep, 14)
                pe.wait_ge(wout_in, 16)
                with pe.Fori(0, NT // 2) as i:
                    for s in range(2):
                        c = 2 * i + s
                        now = c + 1
                        pe.wait_ge(S["sq"], now)
                        for n in range(2):
                            last = nc.tensor.matmul(psum[:, n, :], ones,
                                                    sq[:, n * GH:(n + 1) * GH, :].rearrange("p h d -> p (h d)"),
                                                    start=True, stop=True)
                        last.then_inc(S["ss"], 1)
                        pe.wait_ge(S["qk"], now)
                        for h in range(GH):
                            nc.tensor.transpose(B0[:, h, :], qk[:, GH + h, :], ident)
                        for h in range(GH):
                            last = nc.tensor.transpose(B1[:, h, :], ch[s][:, 2 * GH + h, :], ident)
                        last.then_inc(S["tr"], 1)
                        pe.wait_ge(S["gB"], now)
                        pe.wait_ge(S["bB"], now)
                        for h in range(GH):
                            nc.tensor.matmul(C0[:, h, :], gB[:, h, :], triu, start=True, stop=True)
                        for h in range(GH):
                            last = nc.tensor.matmul(C1[:, h, :], bB[:, h, :], ident, start=True, stop=True)
                        last.then_inc(S["bc"], 1)
                        for h in range(GH):
                            nc.tensor.matmul(D0[:, h, :], qk[:, GH + h, :], qk[:, GH + h, :], start=True, stop=True)
                        for h in range(GH):
                            last = nc.tensor.matmul(D1[:, h, :], qk[:, GH + h, :], qk[:, h, :], start=True, stop=True)
                        last.then_inc(S["kq"], 1)
                        pe.wait_ge(S["at"], now)
                        for n in range(LEVELS):
                            if n == 0:
                                pe.wait_ge(S["tu0"], now)
                            else:
                                pe.wait_ge(le, c * LEVELS + n)
                            for h in range(GH):
                                last = nc.tensor.matmul(A0[:, h, :], at[:, h, :], tu[:, 0, h, :], start=True, stop=True)
                            last.then_inc(lx, 1)
                            pe.wait_ge(S["vb"], now)
                            pe.wait_ge(lm, c * LEVELS + n + 1)
                            for h in range(GH):
                                nc.tensor.matmul(B0[:, h, :], ident, tu[:, 0, h, :], start=True, stop=False)
                                nc.tensor.matmul(B0[:, h, :], tu[:, 1, h, :], xs[:, h, :], start=False, stop=True)
                            for h in range(GH):
                                nc.tensor.matmul(B1[:, h, :], ident, tu[:, 1, h, :], start=True, stop=False)
                                last = nc.tensor.matmul(B1[:, h, :], xs[:, h, :], tu[:, 1, h, :], start=False, stop=True)
                            last.then_inc(lt, 1)
                        pe.wait_ge(S["st_up"], c + 1)
                        for h in range(GH):
                            last = nc.tensor.matmul(C0[:, h, :], qk[:, GH + h, :], state[:, h, :], start=True, stop=True)
                        last.then_inc(S["ks"], 1)
                        pe.wait_ge(S["r2"], now)
                        pe.wait_ge(le, (c + 1) * LEVELS)
                        for h in range(GH):
                            last = nc.tensor.matmul(C1[:, h, :], tu[:, 1, h, :], vb[:, h, :], start=True, stop=True)
                        last.then_inc(S["u_mm"], 1)
                        pe.wait_ge(S["u_ev"], now)
                        for h in range(GH):
                            nc.tensor.matmul(D1[:, h, :], kd[:, h, :], uu[:, h, :], start=True, stop=True)
                        for h in range(GH):
                            nc.tensor.matmul(D0[:, h, :], qkd[:, h, :], uu[:, h, :], start=True, stop=False)
                            last = nc.tensor.matmul(D0[:, h, :], qd[:, h, :], state[:, h, :], start=False, stop=True)
                        last.then_inc(S["o_ds"], 1)
                        pe.wait_ge(S["og"], now)
                        for h in range(GH):
                            last = nc.tensor.transpose(A0[:, h, :], og[:, h, :], ident)
                        last.then_inc(S["ogT"], 1)
                        pe.wait_ge(tile_in[s][1], 16 * (i + 1))
                        pe.wait_ge(S["mg"], now)
                        for a in range(AH):
                            r, p = divmod(a, 4)
                            last = nc.tensor.matmul(psum[:, a // 2, (a % 2) * 256:(a % 2) * 256 + 256],
                                                    ch[s][64 * r:64 * r + 64, N_CONV + p, :],
                                                    kw[s][64 * r:64 * r + 64, :], start=True, stop=True)
                        last.then_inc(S["s_mm"], 1)
                        pe.wait_ge(S["s_p"], now)
                        pe.wait_ge(S["st_up"], c + 2)
                        for a in range(AH):
                            for k in range(2):
                                n = 2 * a + k
                                last = nc.tensor.transpose(psum[:, 4 + n // 4, (n % 4) * P:(n % 4) * P + P],
                                                           sc[:, a, k * P:(k + 1) * P], ident)
                        last.then_inc(S["p_tr"], 1)
                        pe.wait_ge(S["p_ev"], now)
                        for a in range(AH):
                            r = a // 4
                            for k in range(2):
                                last = nc.tensor.matmul(psum[:, 0, a * AD:(a + 1) * AD], pT[:, a, k, :],
                                                        vw[s][:, k, r * AD:(r + 1) * AD], start=(k == 0), stop=(k == 1))
                        last.then_inc(S["o_mm"], 1)
                        pe.wait_ge(S["o_n"], now)
                        for p in range(4):
                            last = nc.tensor.transpose(B0[:, p, :], on[:, 2 * p:2 * p + 2, :].rearrange("p a d -> p (a d)"),
                                                       ident)
                        last.then_inc(S["onT"], 1)
                        pe.wait_ge(S["ma"], now)
                        for n in range(2):
                            for k in range(KC):
                                last = nc.tensor.matmul(psum[:, 4 + n, :], mixT[:, k, :],
                                                        wout[:, k, n * HALF:(n + 1) * HALF],
                                                        start=(k == 0), stop=(k == KC - 1))
                        last.then_inc(S["proj"], 1)

            @block.scalar
            def _(act):
                act.wait_ge(side_in, 80)
                act.wait_ge(prep, 1)
                nc.scalar.activation(small["beta"][:], ba[:, :, 0:GH], ACT.Exp, scale=-1.0).then_inc(prep, 1)
                nc.scalar.activation(small["mag"][:], small["soft"][:], ACT.Abs).then_inc(prep, 1)
                act.wait_ge(prep, 3)
                nc.scalar.activation(small["mag"][:], small["mag"][:], ACT.Exp, scale=-1.0)
                nc.scalar.activation(alog[:], alog[:], ACT.Exp).then_inc(prep, 1)
                act.wait_ge(prep, 6)
                nc.scalar.activation(small["mag"][:], small["mag"][:], ACT.Ln).then_inc(prep, 1)
                act.wait_ge(prep, 9)
                nc.scalar.activation(small["egam"].rearrange("p t h -> p (t h)"), psum[:, 0, 0:NT * GH], ACT.Exp)
                nc.scalar.activation(small["decay"].rearrange("p t h -> p (t h)"), psum[:, 1, 0:NT * GH],
                                     ACT.Exp).then_inc(prep, 1)
                act.wait_ge(prep, 12)
                nc.scalar.activation(small["kdec"][:], small["tmp"][:], ACT.Exp).then_inc(prep, 1)
                with act.Fori(0, NT // 2) as i:
                    for s in range(2):
                        c = 2 * i + s
                        now = c + 1
                        act.wait_ge(tile_in[s][0], 16 * (i + 1))
                        nc.scalar.activation(sq[:], ch[s][:, 0:2 * GH, :], ACT.Square).then_inc(S["sq"], 1)
                        act.wait_ge(S["ss"], now)
                        nc.scalar.activation(rn[:, 0:GH, :], A0, ACT.Sqrt, scale=float(P), bias=cst[:, C_EPS + 3:C_EPS + 4])
                        nc.scalar.activation(rn[:, GH:, :], A1, ACT.Sqrt,
                                             bias=cst[:, C_EPS + 2:C_EPS + 3]).then_inc(S["root"], 1)
                        act.wait_ge(S["bc"], now)
                        nc.scalar.activation(eg[:], C0, ACT.Exp).then_inc(S["egx"], 1)
                        act.wait_ge(S["e_neg"], now)
                        nc.scalar.activation(dm[:], dm[:], ACT.Exp).then_inc(S["dmx"], 1)
                        for n in range(LEVELS):
                            act.wait_ge(lt, c * LEVELS + n + 1)
                            nc.scalar.activation(tu.rearrange("p a h d -> p a (h d)"), psum[:, 2:4, :],
                                                 ACT.Copy).then_inc(le, 1)
                        act.wait_ge(S["u_mm"], now)
                        nc.scalar.activation(uu[:], C1, ACT.Copy).then_inc(S["u_ev"], 1)
                        act.wait_ge(S["o_ds"], now)
                        nc.scalar.activation(og[:], D0, ACT.Square).then_inc(S["osq"], 1)
                        act.wait_ge(S["osum"], now)
                        nc.scalar.activation(rms[:], rms[:], ACT.Sqrt, scale=1.0 / P,
                                             bias=cst[:, C_EPS + 1:C_EPS + 2]).then_inc(S["oroot"], 1)
                        act.wait_ge(S["ogT"], now)
                        nc.scalar.activation(mixT[:, 0:GH, :], A0, ACT.Copy).then_inc(S["mg"], 1)
                        act.wait_ge(S["s_nmx"], now)
                        for a in range(AH):
                            nc.scalar.activation(sc[:, a, :], sc[:, a, :], ACT.Exp, bias=mx[:, 1, a:a + 1],
                                                 accum_out=mx[:, 3, a:a + 1])
                        nc.scalar.activation(mx[:, 2, :], mx[:, 2, :], ACT.Exp).then_inc(S["s_p"], 1)
                        act.wait_ge(S["p_tr"], now)
                        nc.scalar.activation(pT.rearrange("p a k q -> p (a k q)"),
                                             psum[:, 4:8, :].rearrange("p b q -> p (b q)"), ACT.Copy).then_inc(S["p_ev"], 1)
                        act.wait_ge(S["onT"], now)
                        nc.scalar.activation(mixT[:, GH:, :], B0, ACT.Copy).then_inc(S["ma"], 1)
                        act.wait_ge(S["aggr"], now)
                        nc.scalar.activation(mv[:, 2:3], mv[:, 1:2], ACT.Sqrt,
                                             bias=cst[:, C_EPS:C_EPS + 1]).then_inc(S["root1"], 1)

            @block.vector
            def _(dve):
                dve.wait_ge(side_in, 80)
                nc.vector.tensor_tensor(small["soft"][:], ba[:, :, GH:2 * GH],
                                        dtb[:, :].unsqueeze(1).broadcast_to([P, NT, GH]), ALU.add).then_inc(prep, 1)
                dve.wait_ge(prep, 4)
                nc.vector.tensor_scalar(small["beta"][:], small["beta"][:], 1.0, None, ALU.add)
                nc.vector.tensor_scalar(small["soft"][:], small["soft"][:], 0.0, None, ALU.max).then_inc(prep, 1)
                nc.vector.tensor_scalar(small["mag"][:], small["mag"][:], 1.0, None, ALU.add).then_inc(prep, 1)
                dve.wait_ge(prep, 7)
                nc.vector.reciprocal(small["beta"][:], small["beta"][:])
                nc.vector.tensor_tensor(small["soft"][:], small["soft"][:], small["mag"][:], ALU.add).then_inc(soft_done, 1)
                dve.wait_ge(soft_done, 1)
                nc.vector.scalar_tensor_tensor(small["g"][:], small["soft"][:], -1.0,
                                               alog[:, :].unsqueeze(1).broadcast_to([P, NT, GH]),
                                               ALU.mult, ALU.mult).then_inc(prep, 1)
                dve.wait_ge(prep, 10)
                nc.vector.tensor_copy(small["gam"].rearrange("p t h -> p (t h)"), psum[:, 0, 0:NT * GH]).then_inc(prep, 1)
                dve.wait_ge(prep, 11)
                nc.vector.tensor_tensor(small["tmp"].rearrange("p t h -> p (t h)"), psum[:, 1, 0:NT * GH],
                                        small["gam"].rearrange("p t h -> p (t h)"), ALU.subtract).then_inc(prep, 1)
                dve.wait_ge(prep, 13)
                nc.vector.scalar_tensor_tensor(small["nbeg"][:], small["egam"][:], -1.0, small["beta"][:],
                                               ALU.mult, ALU.mult)
                nc.vector.memset(state[:], 0.0).then_inc(S["st_up"], 1)
                nc.vector.tensor_copy(tu.rearrange("p a h d -> p (a h) d"),
                                      ident.unsqueeze(1).broadcast_to([P, 2 * GH, P])).then_inc(prep, 1)

                def per_head(name, c, n=P):
                    return small[name][:, ts(c, 1), :].rearrange("p t h -> p (t h)").unsqueeze(2).broadcast_to([P, GH, n])

                with dve.Fori(0, NT // 2) as i:
                    for s in range(2):
                        c = 2 * i + s
                        now = c + 1
                        nc.vector.tensor_copy(gB[:], per_head("g", c)).then_inc(S["gB"], 1)
                        nc.vector.tensor_copy(bB[:], per_head("beta", c)).then_inc(S["bB"], 1)
                        dve.wait_ge(S["root"], now)
                        nc.vector.reciprocal(rn[:], rn[:]).then_inc(S["rn"], 1)
                        dve.wait_ge(S["rn"], now)
                        nc.vector.tensor_tensor(qk[:], ch[s][:, 0:2 * GH, :], rn[:], ALU.mult).then_inc(S["qk"], 1)
                        dve.wait_ge(S["tr"], now)
                        nc.vector.tensor_tensor(kd[:], B0, per_head("kdec", c), ALU.mult).then_inc(S["kd"], 1)
                        nc.vector.tensor_tensor(vb[:], B1, per_head("beta", c), ALU.mult).then_inc(S["vb"], 1)
                        dve.wait_ge(S["bc"], now)
                        dve.wait_ge(S["egx"], now)
                        nc.vector.tensor_tensor(dm[:], C0, per_head("gam", c), ALU.subtract).then_inc(S["e_raw"], 1)
                        dve.wait_ge(S["e_raw"], now)
                        nc.vector.tensor_tensor(dm[:], dm[:], heads(neg), ALU.add).then_inc(S["e_neg"], 1)
                        nc.vector.tensor_tensor(qd[:], qk[:, 0:GH, :], eg[:], ALU.mult).then_inc(S["qd"], 1)
                        dve.wait_ge(S["dmx"], now)
                        dve.wait_ge(S["kq"], now)
                        nc.vector.tensor_tensor(at[:], D0, dm[:], ALU.mult).then_inc(S["at0"], 1)
                        nc.vector.tensor_tensor(qkd[:], D1, dm[:], ALU.mult).then_inc(S["qkd"], 1)
                        dve.wait_ge(S["at0"], now)
                        nc.vector.tensor_tensor(at[:], at[:], C1, ALU.mult).then_inc(S["at"], 1)
                        nc.vector.tensor_copy(tu.rearrange("p a h d -> p (a h) d"),
                                              ident.unsqueeze(1).broadcast_to([P, 2 * GH, P])).then_inc(S["tu0"], 1)
                        for n in range(LEVELS):
                            dve.wait_ge(lx, c * LEVELS + n + 1)
                            level = cst[:, C_LEVEL + n * P:C_LEVEL + (n + 1) * P]
                            nc.vector.tensor_tensor(xs[:], A0, heads(level), ALU.mult).then_inc(lm, 1)
                        dve.wait_ge(S["ks"], now)
                        nc.vector.tensor_tensor(xs[:], C0, per_head("nbeg", c), ALU.mult).then_inc(S["kd"], 1)
                        dve.wait_ge(S["kd"], 2 * now)
                        nc.vector.tensor_tensor(vb[:], vb[:], xs[:], ALU.add).then_inc(S["r2"], 1)
                        dve.wait_ge(S["o_ds"], now)
                        nc.vector.tensor_tensor(state[:], state[:], per_head("decay", c), ALU.mult).then_inc(S["qd"], 1)
                        dve.wait_ge(S["qd"], 2 * now)
                        nc.vector.tensor_tensor(state[:], state[:], D1, ALU.add).then_inc(S["st_up"], 1)
                        dve.wait_ge(S["osq"], now)
                        nc.vector.tensor_reduce(rms[:], og[:], AX, ALU.add).then_inc(S["osum"], 1)
                        dve.wait_ge(S["oroot"], now)
                        nc.vector.reciprocal(rms[:], rms[:]).then_inc(S["orec"], 1)
                        dve.wait_ge(S["orec"], now)
                        dve.wait_ge(tile_in[s][3], 16 * (i + 1))
                        for h in range(GH):
                            last = nc.vector.scalar_tensor_tensor(og[:, h, :], D0[:, h, :], rms[:, h:h + 1],
                                                                  zw[s][:, h, :], ALU.mult, ALU.mult)
                        last.then_inc(S["og"], 1)
                        dve.wait_ge(S["s_mm"], now)
                        dve.wait_ge(tile_in[s][4], 16 * (i + 1))
                        for b in range(4):
                            last = nc.vector.scalar_tensor_tensor(
                                sc[:, 2 * b:2 * b + 2, :], psum[:, b, :].rearrange("p (a k) -> p a k", a=2), AD ** -0.5,
                                wm[s][:, :].unsqueeze(1).broadcast_to([P, 2, 2 * P]), ALU.mult, ALU.add)
                        last.then_inc(S["s_mask"], 1)
                        dve.wait_ge(S["s_mask"], now)
                        nc.vector.tensor_reduce(mx[:, 0, :], sc[:], AX, ALU.max).then_inc(S["s_max"], 1)
                        dve.wait_ge(S["s_max"], now)
                        nc.vector.tensor_tensor(mx[:, 0, :], mx[:, 0, :], sinks[:], ALU.max).then_inc(S["s_mx"], 1)
                        dve.wait_ge(S["s_mx"], now)
                        nc.vector.tensor_tensor(mx[:, 2, :], sinks[:], mx[:, 0, :], ALU.subtract)
                        nc.vector.tensor_scalar(mx[:, 1, :], mx[:, 0, :], -1.0, None, ALU.mult).then_inc(S["s_nmx"], 1)
                        dve.wait_ge(S["s_p"], now)
                        nc.vector.tensor_tensor(mx[:, 3, :], mx[:, 3, :], mx[:, 2, :], ALU.add).then_inc(S["s_den"], 1)
                        dve.wait_ge(S["s_den"], now)
                        nc.vector.reciprocal(mx[:, 3, :], mx[:, 3, :]).then_inc(S["s_rec"], 1)
                        dve.wait_ge(S["s_rec"], now)
                        dve.wait_ge(S["o_mm"], now)
                        nc.vector.tensor_tensor(on[:], psum[:, 0, :].rearrange("p (a d) -> p a d", a=AH),
                                                mx[:, 3, :].unsqueeze(2).broadcast_to([P, AH, AD]),
                                                ALU.mult).then_inc(S["o_n"], 1)
                        dve.wait_ge(S["proj"], now)
                        dve.wait_ge(tile_in[s][5], 16 * (i + 1))
                        dve.wait_ge(x1_out, 16 * c)
                        for n in range(2):
                            nc.vector.scalar_tensor_tensor(h1[:, n * HALF:(n + 1) * HALF],
                                                           xt[s][:, n * HALF:(n + 1) * HALF], ALPHA, psum[:, 4 + n, :],
                                                           ALU.mult, ALU.add).then_inc(S["h1"], 1)
                        for n in range(2):
                            dve.wait_ge(S["h1"], 2 * c + n + 1)
                            nc.vector.bn_stats(st[:, n, :], h1[:, n * HALF:(n + 1) * HALF]).then_inc(S["stat"], 1)
                        wait_apart(dve, tick, S["stat"], 2 * now)
                        nc.vector.bn_aggr(mv[:, 0:2], st[:]).then_inc(S["aggr"], 1)
                        dve.wait_ge(S["root1"], now)
                        nc.vector.reciprocal(mv[:, 2:3], mv[:, 2:3]).then_inc(S["rec1"], 1)
                        dve.wait_ge(S["rec1"], now)
                        nc.vector.tensor_scalar(h1[:], h1[:], mv[:, 0:1], mv[:, 2:3], ALU.subtract,
                                                ALU.mult).then_inc(S["nrm"], 1)
                        dve.wait_ge(S["nrm"], now)
                        nc.vector.tensor_tensor(h1[:], h1[:], lng[:], ALU.mult).then_inc(S["nrm_g"], 1)
                        dve.wait_ge(S["nrm_g"], now)
                        nc.vector.tensor_tensor(h1[:], h1[:], lnb[:], ALU.add).then_inc(S["x1"], 1)


def split_x1(nc, sem, scr, cst, psum, x1h, x1l):
    with ExitStack() as ctx:
        xt = [ctx.enter_context(nc.sbuf_tensor(f"t_x{s}", [P, D], F32)) for s in range(2)]
        x_in = [sem(f"t_in{s}") for s in range(2)]
        tr = [sem(f"t_tr{s}") for s in range(2)]
        hi = [sem(f"t_hi{s}") for s in range(2)]
        lo = [sem(f"t_lo{s}") for s in range(2)]
        ps = [psum[:, 2 * s:2 * s + 2, :].rearrange("p b (k t) -> p (b k) t", t=P) for s in range(2)]
        with nc.Block() as block:
            @block.sync
            def _(sp):
                with sp.Fori(0, NT // 2) as i:
                    for s in range(2):
                        sp.wait_ge(tr[s], i)
                        sp.dma_start(xt[s][:], scr["x1"][ts((2 * i + s) * P, P), :]).then_inc(x_in[s], 16)

            @block.tensor
            def _(pe):
                with pe.Fori(0, NT // 2) as i:
                    for s in range(2):
                        pe.wait_ge(x_in[s], 16 * (i + 1))
                        pe.wait_ge(lo[s], i)
                        for k in range(KC):
                            last = nc.tensor.transpose(ps[s][:, k, :], xt[s][:, k * P:(k + 1) * P],
                                                       cst[:, C_ID:C_ID + P])
                        last.then_inc(tr[s], 1)

            @block.scalar
            def _(act):
                with act.Fori(0, NT // 2) as i:
                    for s in range(2):
                        act.wait_ge(tr[s], i + 1)
                        nc.scalar.activation(x1h[:, :, ts((2 * i + s) * P, P)], ps[s], ACT.Copy).then_inc(hi[s], 1)

            @block.vector
            def _(dve):
                with dve.Fori(0, NT // 2) as i:
                    for s in range(2):
                        dve.wait_ge(hi[s], i + 1)
                        nc.vector.tensor_tensor(x1l[:, :, ts((2 * i + s) * P, P)], ps[s],
                                                x1h[:, :, ts((2 * i + s) * P, P)].bitcast(F32),
                                                ALU.subtract).then_inc(lo[s], 1)


def retrieve(nc, sem, io, cst, psum, x1h, x1l, key1, key2, gate):
    with ExitStack() as ctx:
        def sb(name, shape, dt=F32):
            return ctx.enter_context(nc.sbuf_tensor(name, shape, dt))

        wr = [sb(f"r_w{s}", [P, KC, P]) for s in range(2)]
        wh = [sb(f"r_wh{s}", [P, KC, P], F32R) for s in range(2)]
        wl = [sb(f"r_wl{s}", [P, KC, P], F32R) for s in range(2)]
        keys = sb("r_keys", [P, 2 * PH, NK])
        qT = [sb(f"r_qT{s}", [P, T]) for s in range(2)]
        kk = [sb(f"r_kk{s}", [P, NK]) for s in range(2)]
        sc = [sb(f"r_sc{s}", [P, NT, NK]) for s in range(2)]
        rest = sb("r_rest", [P, NT, NK])
        top = [sb(f"r_top{s}", [P, NT, TOPK]) for s in range(2)]
        idx = [sb(f"r_idx{s}", [P, NT, TOPK], U32) for s in range(2)]
        idf = [[sb(f"r_idf{v}{s}", [P, NT, TOPK]) for s in range(2)] for v in range(2)]
        cand = sb("r_cand", [P, NT, TOPK * TOPK])
        crest = sb("r_crest", [P, NT, TOPK * TOPK])
        best = sb("r_best", [P, NT, TOPK])
        ex = sb("r_ex", [P, NT, TOPK])
        pos = sb("r_pos", [P, NT, TOPK], U32)
        pab = [sb(f"r_pab{s}", [P, NT, TOPK], U32) for s in range(2)]
        pf = [[sb(f"r_pf{v}{s}", [P, NT, TOPK]) for s in range(2)] for v in range(2)]
        gsum = sb("r_gsum", [P, NT])
        pick = [sb(f"r_pick{s}", [P, NT, TOPK, TOPK]) for s in range(2)]
        q_ps = [psum[:, 2 * s:2 * s + 2, :] for s in range(2)]
        s_ps = [psum[:, 4 + 2 * s:6 + 2 * s, :] for s in range(2)]

        tick = sem("r_tick")
        w_in = [sem(f"r_w_in{s}") for s in range(2)]
        w_hi = [sem(f"r_w_hi{s}") for s in range(2)]
        w_lo = [sem(f"r_w_lo{s}") for s in range(2)]
        q_mm = [sem(f"r_q_mm{s}") for s in range(2)]
        q_ev = [sem(f"r_q_ev{s}") for s in range(2)]
        s_mm = [sem(f"r_s_mm{s}") for s in range(2)]
        s_ev = [sem(f"r_s_ev{s}") for s in range(2)]
        kk_in = [sem(f"r_kk{s}") for s in range(2)]
        half_done = [sem(f"r_half{s}") for s in range(2)]
        mx1, mi1, mr, mx2 = sem("r_max1"), sem("r_index1"), sem("r_replace"), sem("r_max2")
        c_new, c1, c2, c3, c4, c5 = (sem(f"r_cand{n}") for n in range(6))
        g_sub, g_exp, g_sum, g_rec, g_out = (sem(f"r_gate{n}") for n in range(5))
        p_bits = sem("r_bits")
        p_ready = [sem(f"r_pos_ready{v}") for v in range(2)]
        pool_step = sem("r_pick_step")
        p_square = sem("r_pick_square")
        p_diff = [sem(f"r_pick_diff{s}") for s in range(2)]
        p_match = [sem(f"r_pick_match{s}") for s in range(2)]
        picked_all = [sem(f"r_picked{v}") for v in range(2)]

        with nc.Block() as block:
            @block.sync
            def _(sp):
                with sp.Fori(0, PH) as h:
                    for s in range(2):
                        sp.wait_ge(w_lo[s], h)
                        sp.dma_start(wr[s][:], io["wq"][2 * h + s]).then_inc(w_in[s], 16)
                        sp.wait_ge(s_mm[s], h)
                        sp.dma_start(kk[s][:], io["keysT"][2 * h + s]).then_inc(kk_in[s], 16)

            @block.tensor
            def _(pe):
                with pe.Fori(0, PH) as h:
                    for s in range(2):
                        pe.wait_ge(w_hi[s], h + 1)
                        pe.wait_ge(w_lo[s], h + 1)
                        pe.wait_ge(q_ev[s], h)
                        for n in range(2):
                            for k in range(KC):
                                c = slice(n * HALF, (n + 1) * HALF)
                                nc.tensor.matmul(q_ps[s][:, n, :], wh[s][:, k, :], x1h[:, k, c],
                                                 start=(k == 0), stop=False)
                                nc.tensor.matmul(q_ps[s][:, n, :], wh[s][:, k, :], x1l[:, k, c],
                                                 start=False, stop=False)
                                last = nc.tensor.matmul(q_ps[s][:, n, :], wl[s][:, k, :], x1h[:, k, c],
                                                        start=False, stop=(k == KC - 1))
                        last.then_inc(q_mm[s], 1)
                    for s in range(2):
                        pe.wait_ge(q_ev[s], h + 1)
                        pe.wait_ge(kk_in[s], 16 * (h + 1))
                        pe.wait_ge(s_ev[s], h)
                        for t in range(NT):
                            last = nc.tensor.matmul(s_ps[s][:, t // 4, (t % 4) * P:(t % 4 + 1) * P],
                                                    qT[s][:, t * P:(t + 1) * P], kk[s][:], start=True, stop=True)
                        last.then_inc(s_mm[s], 1)

            @block.scalar
            def _(act):
                def weights(h):
                    for s in range(2):
                        act.wait_ge(w_in[s], 16 * (h + 1))
                        act.wait_ge(q_mm[s], h)
                        nc.scalar.activation(wh[s][:], wr[s][:], ACT.Copy).then_inc(w_hi[s], 1)

                def scores(h):
                    for s in range(2):
                        act.wait_ge(q_mm[s], h + 1)
                        act.wait_ge(s_mm[s], h)
                        nc.scalar.activation(qT[s][:], q_ps[s].rearrange("p b t -> p (b t)"), ACT.Copy).then_inc(q_ev[s], 1)
                    for s in range(2):
                        act.wait_ge(s_mm[s], h + 1)
                        act.wait_ge(half_done[s], h)
                        nc.scalar.activation(sc[s].rearrange("p t n -> p (t n)"),
                                             s_ps[s].rearrange("p b n -> p (b n)"), ACT.Copy).then_inc(s_ev[s], 1)

                def picks(h):
                    for s in range(2):
                        act.wait_ge(p_diff[s], h + 1)
                        nc.scalar.activation(pick[s][:], pick[s][:], ACT.Square).then_inc(p_square, 1)
                        act.wait_ge(p_square, 2 * h + s + 1)
                        nc.scalar.activation(pick[s][:], pick[s][:], ACT.Relu, scale=-1.0,
                                             bias=cst[:, C_ONES:C_ONES + 1]).then_inc(p_match[s], 1)

                def gates(h):
                    act.wait_ge(g_sub, h + 1)
                    nc.scalar.activation(ex[:], ex[:], ACT.Exp).then_inc(g_exp, 1)

                weights(0)
                scores(0)
                weights(1)
                scores(1)
                gates(0)
                with act.Fori(1, PH - 1) as h:
                    weights(h + 1)
                    picks(h - 1)
                    scores(h + 1)
                    gates(h)
                picks(PH - 2)
                gates(PH - 1)
                picks(PH - 1)

            @block.vector
            def _(dve):
                with dve.Fori(0, PH // 2) as i:
                    for v in range(2):
                        h = 2 * i + v
                        for s in range(2):
                            n = 2 * h + s
                            wait_apart(dve, tick, s_ev[s], h + 1)
                            for t in range(NT):
                                last = nc.vector.max(top[s][:, t, 0:8], sc[s][:, t, :])
                            last.then_inc(mx1, 1)
                            wait_apart(dve, tick, mx1, n + 1)
                            for t in range(NT):
                                last = nc.vector.match_replace(rest[:, t, :], top[s][:, t, 0:8], sc[s][:, t, :], REPLACED)
                            last.then_inc(mr, 1)
                            for t in range(NT):
                                last = nc.vector.max_index(idx[s][:, t, 0:8], top[s][:, t, 0:8], sc[s][:, t, :])
                            last.then_inc(half_done[s], 1)
                            wait_apart(dve, tick, mr, n + 1)
                            for t in range(NT):
                                last = nc.vector.max(top[s][:, t, 8:16], rest[:, t, :])
                            last.then_inc(mx2, 1)
                            wait_apart(dve, tick, mx2, n + 1)
                            for t in range(NT):
                                last = nc.vector.max_index(idx[s][:, t, 8:16], top[s][:, t, 8:16], rest[:, t, :])
                            last.then_inc(mi1, 1)
                        dve.wait_ge(mi1, 2 * h + 2)
                        dve.wait_ge(picked_all[v], i)
                        for s in range(2):
                            nc.vector.tensor_copy(idf[v][s][:], idx[s][:])
                        nc.vector.tensor_tensor(cand.rearrange("p t (a b) -> p t a b", a=TOPK),
                                                top[0][:, :, :].unsqueeze(3).broadcast_to([P, NT, TOPK, TOPK]),
                                                top[1][:, :, :].unsqueeze(2).broadcast_to([P, NT, TOPK, TOPK]),
                                                ALU.add).then_inc(c_new, 1)
                        dve.wait_ge(c_new, h + 1)
                        wait_apart(dve, tick, g_out, h)
                        for t in range(NT):
                            last = nc.vector.max(best[:, t, 0:8], cand[:, t, :])
                        last.then_inc(c1, 1)
                        wait_apart(dve, tick, c1, h + 1)
                        for t in range(NT):
                            last = nc.vector.match_replace(crest[:, t, :], best[:, t, 0:8], cand[:, t, :], REPLACED)
                        last.then_inc(c2, 1)
                        for t in range(NT):
                            nc.vector.max_index(pos[:, t, 0:8], best[:, t, 0:8], cand[:, t, :])
                        wait_apart(dve, tick, c2, h + 1)
                        for t in range(NT):
                            last = nc.vector.max(best[:, t, 8:16], crest[:, t, :])
                        last.then_inc(c3, 1)
                        wait_apart(dve, tick, c3, h + 1)
                        for t in range(NT):
                            last = nc.vector.max_index(pos[:, t, 8:16], best[:, t, 8:16], crest[:, t, :])
                        last.then_inc(c4, 1)
                        dve.wait_ge(c4, h + 1)
                        nc.vector.tensor_scalar(pab[0][:], pos[:], 4, None, ALU.logical_shift_right)
                        nc.vector.tensor_scalar(pab[1][:], pos[:], 15, None, ALU.bitwise_and).then_inc(p_bits, 1)
                        nc.vector.tensor_tensor(ex[:], best[:], best[:, :, 0:1].broadcast_to([P, NT, TOPK]),
                                                ALU.subtract).then_inc(g_sub, 1)
                        dve.wait_ge(p_bits, h + 1)
                        nc.vector.tensor_copy(pf[v][0][:], pab[0][:])
                        nc.vector.tensor_copy(pf[v][1][:], pab[1][:]).then_inc(p_ready[v], 1)
                        dve.wait_ge(g_exp, h + 1)
                        nc.vector.tensor_reduce(gsum[:], ex[:], AX, ALU.add).then_inc(g_sum, 1)
                        dve.wait_ge(g_sum, h + 1)
                        nc.vector.reciprocal(gsum[:], gsum[:]).then_inc(g_rec, 1)
                        dve.wait_ge(g_rec, h + 1)
                        nc.vector.tensor_tensor(gate[:, :, ts(h * TOPK, TOPK)], ex[:],
                                                gsum[:, :].unsqueeze(2).broadcast_to([P, NT, TOPK]),
                                                ALU.mult).then_inc(g_out, 1)

            @block.gpsimd
            def _(pool):
                def weights(h):
                    for s in range(2):
                        pool.wait_ge(w_hi[s], h + 1)
                        nc.gpsimd.tensor_tensor(wl[s][:], wr[s][:], wh[s][:].bitcast(F32), ALU.subtract).then_inc(w_lo[s], 1)

                def picks(h, v, i):
                    ranks = cst[:, C_IOTA16:C_IOTA16 + TOPK].unsqueeze(1).broadcast_to([P, NT * TOPK, TOPK])
                    pool.wait_ge(p_ready[v], i + 1)
                    pool.wait_ge(pool_step, 10 * h)
                    for s in range(2):
                        nc.gpsimd.tensor_tensor(
                            pick[s].rearrange("p t k j -> p (t k) j"),
                            pf[v][s].rearrange("p t k -> p (t k)").unsqueeze(2).broadcast_to([P, NT * TOPK, TOPK]),
                            ranks, ALU.subtract).then_inc(p_diff[s], 1)
                    for s, dst in enumerate((key1, key2)):
                        n = 10 * h + 5 * s
                        flat = pick[s].rearrange("p t k j -> p (t k) j")
                        pool.wait_ge(p_match[s], h + 1)
                        nc.gpsimd.tensor_tensor(pick[s][:], pick[s][:],
                                                idf[v][s][:, :, :].unsqueeze(2).broadcast_to([P, NT, TOPK, TOPK]),
                                                ALU.mult).then_inc(pool_step, 1)
                        pool.wait_ge(pool_step, n + 1)
                        for step, m in enumerate((8, 4, 2)):
                            nc.gpsimd.tensor_tensor(flat[:, :, 0:m], flat[:, :, 0:m], flat[:, :, m:2 * m],
                                                    ALU.add).then_inc(pool_step, 1)
                            pool.wait_ge(pool_step, n + 2 + step)
                        nc.gpsimd.tensor_tensor(dst[:, :, ts(h * TOPK, TOPK)], pick[s][:, :, :, 0],
                                                pick[s][:, :, :, 1], ALU.add).then_inc(pool_step, 1)
                    pool.wait_ge(pool_step, 10 * (h + 1))
                    pool.sem_inc(picked_all[v], 1)

                weights(0)
                weights(1)
                with pool.Fori(0, PH // 2 - 1) as i:
                    for v in range(2):
                        weights(2 * i + v + 2)
                        picks(2 * i + v, v, i)
                picks(PH - 2, 0, PH // 2 - 1)
                picks(PH - 1, 1, PH // 2 - 1)


def build_gates(nc, sem, scr, cst, psum, key1, key2, gate):
    with ExitStack() as ctx:
        def sb(name, shape, dt=F32):
            return ctx.enter_context(nc.sbuf_tensor(name, shape, dt))

        R = 16
        pickT = sb("g_pickT", [P, 3, T])
        one1 = [sb(f"g_one{s}", [P, R, NK]) for s in range(2)]
        one2 = [sb(f"g_two{s}", [P, R, NK]) for s in range(2)]
        gt = [sb(f"g_tile{s}", [P, NK, TG]) for s in range(2)]
        iota = cst[:, C_IOTA:C_IOTA + NK].unsqueeze(1).broadcast_to([P, R, NK])
        tr, tr_ev = sem("g_tr"), sem("g_tr_ev")
        hot1 = [sem(f"g_hot1{s}") for s in range(2)]
        hot2 = [sem(f"g_hot2{s}") for s in range(2)]
        gated = [sem(f"g_gated{s}") for s in range(2)]
        mm = [sem(f"g_mm{s}") for s in range(2)]
        evac = [sem(f"g_evac{s}") for s in range(2)]
        stored = [sem(f"g_stored{s}") for s in range(2)]

        def picks_of(n, t):
            return pickT[:, n, ts(t, R)].unsqueeze(2).broadcast_to([P, R, NK])

        with nc.Block() as block:
            @block.tensor
            def _(pe):
                for t in range(NT):
                    if t >= 2:
                        pe.wait_ge(tr_ev, t - 1)
                    for n, src in enumerate((key1, key2, gate)):
                        last = nc.tensor.transpose(psum[:, t % 2, n * P:(n + 1) * P], src[:, t, :], cst[:, C_ID:C_ID + P])
                    last.then_inc(tr, 1)
                pe.wait_ge(tr_ev, NT)
                with pe.Fori(0, T // R // 2) as i:
                    for s in range(2):
                        pe.wait_ge(hot1[s], i + 1)
                        pe.wait_ge(gated[s], i + 1)
                        pe.wait_ge(evac[s], 4 * i)
                        for n in range(R):
                            last = nc.tensor.matmul(psum[:, 4 * s + n // 4, (n % 4) * NK:(n % 4 + 1) * NK],
                                                    one2[s][:, n, :], one1[s][:, n, :], start=True, stop=True)
                            if n % 4 == 3:
                                last.then_inc(mm[s], 1)

            @block.vector
            def _(dve):
                dve.wait_ge(tr_ev, NT)
                with dve.Fori(0, T // R // 2) as i:
                    for s in range(2):
                        t = (2 * i + s) * R
                        dve.wait_ge(mm[s], 4 * i)
                        nc.vector.tensor_tensor(one2[s][:], iota, picks_of(1, t), ALU.is_equal).then_inc(hot2[s], 1)
                        nc.vector.tensor_tensor(one1[s][:], iota, picks_of(0, t), ALU.is_equal).then_inc(hot1[s], 1)

            @block.gpsimd
            def _(pool):
                with pool.Fori(0, T // R // 2) as i:
                    for s in range(2):
                        pool.wait_ge(hot2[s], i + 1)
                        nc.gpsimd.tensor_tensor(one2[s][:], one2[s][:], picks_of(2, (2 * i + s) * R),
                                                ALU.mult).then_inc(gated[s], 1)

            @block.scalar
            def _(act):
                for t in range(NT):
                    act.wait_ge(tr, t + 1)
                    nc.scalar.activation(pickT[:, :, t * P:(t + 1) * P],
                                         psum[:, t % 2, 0:3 * P].rearrange("p (n t) -> p n t", n=3),
                                         ACT.Copy).then_inc(tr_ev, 1)
                with act.Fori(0, T // TG // 2) as i:
                    for b in range(2):
                        act.wait_ge(stored[b], 16 * i)
                        for r in range(TG // R):
                            s = r % 2
                            for n in range(4):
                                act.wait_ge(mm[s], ((2 * i + b) * (TG // R // 2) + r // 2) * 4 + n + 1)
                                nc.scalar.activation(gt[b][:, :, r * R + 4 * n:r * R + 4 * n + 4].rearrange("p k t -> p t k"),
                                                     psum[:, 4 * s + n, :].rearrange("p (t k) -> p t k", t=4),
                                                     ACT.Copy).then_inc(evac[s], 1)

            @block.sync
            def _(sp):
                with sp.Fori(0, T // TG // 2) as i:
                    for b in range(2):
                        sp.wait_ge(evac[1], (2 * i + b + 1) * (TG // 8))
                        sp.dma_start(scr["G"][ts(2 * i + b, 1)].rearrange("a p k t -> (a p) k t"),
                                     gt[b][:]).then_inc(stored[b], 16)
                for b in range(2):
                    sp.wait_ge(stored[b], 16 * (T // TG // 2))


def experts(nc, sem, io, scr, psum, x1h, x1l, y):
    with ExitStack() as ctx:
        def sb(name, shape, dt=F32):
            return ctx.enter_context(nc.sbuf_tensor(name, shape, dt))

        NG = NK // 2
        ur = [sb(f"e_ur{j}", [P, KC, P]) for j in range(2)]
        vr = sb("e_vr", [P, D])
        uh = [sb(f"e_uh{j}", [P, KC, P], F32R) for j in range(2)]
        ul = [sb(f"e_ul{j}", [P, KC, P], F32R) for j in range(2)]
        vh = [[sb(f"e_vh{s}{j}", [P, D], F32R) for j in range(2)] for s in range(2)]
        vl = [[sb(f"e_vl{s}{j}", [P, D], F32R) for j in range(2)] for s in range(2)]
        ah = [[sb(f"e_ah{s}{j}", [P, T], F32R) for j in range(2)] for s in range(2)]
        al = [[sb(f"e_al{s}{j}", [P, T], F32R) for j in range(2)] for s in range(2)]
        gt = [sb(f"e_g{j}", [P, T // TG, TG]) for j in range(2)]
        av = [sb(f"e_a{n}", [P, HALF]) for n in range(2)]

        u_in = [sem(f"u_in{j}") for j in range(2)]
        v_in = [sem(f"v_in{j}") for j in range(2)]
        g_in = [sem(f"g_in{j}") for j in range(2)]
        u_hi = [sem(f"u_hi{j}") for j in range(2)]
        u_lo = [sem(f"u_lo{j}") for j in range(2)]
        v_hi = [sem(f"v_hi{j}") for j in range(2)]
        v_lo = [sem(f"v_lo{j}") for j in range(2)]
        h_mm = [[sem(f"h_mm{j}{n}") for n in range(2)] for j in range(2)]
        gelu = [[sem(f"gelu{j}{n}") for n in range(2)] for j in range(2)]
        a_mul = [[sem(f"a_mul{j}{n}") for n in range(2)] for j in range(2)]
        a_hi = [[sem(f"a_hi{j}{n}") for n in range(2)] for j in range(2)]
        a_lo = [[sem(f"a_lo{j}{n}") for n in range(2)] for j in range(2)]
        y_mm = sem("y_mm")
        y_add = [sem(f"y_add{b}") for b in range(4)]
        y_zero = sem("y_zero")

        with nc.Block() as block:
            @block.sync
            def _(sp):
                with sp.Fori(0, NG) as g:
                    for j in range(2):
                        sp.wait_ge(u_lo[j], g)
                        sp.dma_start(ur[j][:], io["uT"][2 * g + j]).then_inc(u_in[j], 16)
                        sp.wait_ge(v_lo[1 - j], g + j)
                        sp.dma_start(vr[:], io["v"][ts((2 * g + j) * NK, NK), :]).then_inc(v_in[j], 16)
                        sp.wait_ge(a_mul[j][1], g)
                        sp.dma_start(gt[j][:], scr["G"][:, :, 2 * g + j, :].rearrange("t p q -> p t q")).then_inc(g_in[j], 16)

            @block.tensor
            def _(pe):
                def hidden(g):
                    for j in range(2):
                        pe.wait_ge(u_hi[j], g + 1)
                        pe.wait_ge(u_lo[j], g + 1)
                        for n in range(2):
                            pe.wait_ge(gelu[j][n], g)
                            out = psum[:, 2 * j + n, :]
                            c = slice(n * HALF, (n + 1) * HALF)
                            for k in range(KC):
                                nc.tensor.matmul(out, uh[j][:, k, :], x1h[:, k, c], start=(k == 0), stop=False)
                                nc.tensor.matmul(out, uh[j][:, k, :], x1l[:, k, c], start=False, stop=False)
                                last = nc.tensor.matmul(out, ul[j][:, k, :], x1h[:, k, c], start=False,
                                                        stop=(k == KC - 1))
                            last.then_inc(h_mm[j][n], 1)

                def values(g, s):
                    for j in range(2):
                        pe.wait_ge(v_hi[j], g + 1)
                        pe.wait_ge(v_lo[j], g + 1)
                        for n in range(2):
                            pe.wait_ge(a_lo[j][n], g + 1)
                    for q in range(2 * NT):
                        t, n = divmod(q, 2)
                        pe.wait_ge(y_add[q % 4], 4 * g + q // 4)
                        out = psum[:, 4 + q % 4, :]
                        c = slice(n * HALF, (n + 1) * HALF)
                        r = slice(t * P, (t + 1) * P)
                        for j in range(2):
                            nc.tensor.matmul(out, ah[s][j][:, r], vh[s][j][:, c], start=(j == 0), stop=False)
                            nc.tensor.matmul(out, ah[s][j][:, r], vl[s][j][:, c], start=False, stop=False)
                            last = nc.tensor.matmul(out, al[s][j][:, r], vh[s][j][:, c], start=False, stop=(j == 1))
                        last.then_inc(y_mm, 1)

                pe.wait_ge(y_zero, 1)
                hidden(0)
                with pe.Fori(0, (NG - 2) // 2) as i:
                    hidden(2 * i + 1)
                    values(2 * i, 0)
                    hidden(2 * i + 2)
                    values(2 * i + 1, 1)
                hidden(NG - 1)
                values(NG - 2, 0)
                values(NG - 1, 1)

            @block.scalar
            def _(act):
                def split_u(g, j):
                    act.wait_ge(u_in[j], 16 * (g + 1))
                    act.wait_ge(h_mm[j][1], g)
                    nc.scalar.activation(uh[j][:], ur[j][:], ACT.Copy).then_inc(u_hi[j], 1)

                def split_v(g, s, j, used):
                    act.wait_ge(v_in[j], 16 * (g + 1))
                    act.wait_ge(y_mm, used)
                    nc.scalar.activation(vh[s][j][:], vr[:], ACT.Copy).then_inc(v_hi[j], 1)

                def activate(g, s, j, used):
                    for n in range(2):
                        act.wait_ge(h_mm[j][n], g + 1)
                        if j == 1:
                            act.wait_ge(a_lo[0][n], g + 1)
                        else:
                            act.wait_ge(a_lo[1][n], g)
                        nc.scalar.activation(av[n][:], psum[:, 2 * j + n, :], ACT.Gelu).then_inc(gelu[j][n], 1)
                    act.wait_ge(y_mm, used)
                    for n in range(2):
                        act.wait_ge(a_mul[j][n], g + 1)
                        nc.scalar.activation(ah[s][j][:, n * HALF:(n + 1) * HALF], av[n][:], ACT.Copy).then_inc(a_hi[j][n], 1)

                def group(g, s, used, used_next, more=True):
                    for j in range(2):
                        activate(g, s, j, used)
                        if more:
                            split_u(g + 1, j)
                    if more:
                        for j in range(2):
                            split_v(g + 1, 1 - s, j, used_next)

                for j in range(2):
                    split_u(0, j)
                    split_v(0, 0, j, 0)
                group(0, 0, 0, 0)
                with act.Fori(0, (NG - 2) // 2) as i:
                    group(2 * i + 1, 1, 32 * i, 32 * i + 16)
                    group(2 * i + 2, 0, 32 * i + 16, 32 * i + 32)
                group(NG - 1, 1, 16 * (NG - 2), 0, more=False)

            @block.vector
            def _(dve):
                def split_u(g, j):
                    dve.wait_ge(u_hi[j], g + 1)
                    nc.vector.tensor_tensor(ul[j][:], ur[j][:], uh[j][:].bitcast(F32), ALU.subtract).then_inc(u_lo[j], 1)

                def split_v(g, s, j):
                    dve.wait_ge(v_hi[j], g + 1)
                    nc.vector.tensor_tensor(vl[s][j][:], vr[:], vh[s][j][:].bitcast(F32),
                                            ALU.subtract).then_inc(v_lo[j], 1)

                def weigh(g, s, j):
                    dve.wait_ge(g_in[j], 16 * (g + 1))
                    for n in range(2):
                        dve.wait_ge(gelu[j][n], g + 1)
                        nc.vector.tensor_tensor(av[n][:], av[n][:],
                                                gt[j][:, n * HALF // TG:(n + 1) * HALF // TG, :].rearrange("p t q -> p (t q)"),
                                                ALU.mult).then_inc(a_mul[j][n], 1)
                    for n in range(2):
                        dve.wait_ge(a_hi[j][n], g + 1)
                        c = slice(n * HALF, (n + 1) * HALF)
                        nc.vector.tensor_tensor(al[s][j][:, c], av[n][:], ah[s][j][:, c].bitcast(F32),
                                                ALU.subtract).then_inc(a_lo[j][n], 1)

                def gather(g, q0, q1):
                    for q in range(q0, q1):
                        t, n = divmod(q, 2)
                        c = slice(n * HALF, (n + 1) * HALF)
                        dve.wait_ge(y_mm, 16 * g + q + 1)
                        nc.vector.tensor_tensor(y[:, t, c], y[:, t, c], psum[:, 4 + q % 4, :], ALU.add).then_inc(y_add[q % 4], 1)

                def group(g, s, more=True, before=True):
                    weigh(g, s, 0)
                    if more:
                        split_u(g + 1, 0)
                    weigh(g, s, 1)
                    if before:
                        gather(g - 1, 0, 4)
                    if more:
                        split_u(g + 1, 1)
                    if before:
                        gather(g - 1, 4, 2 * NT)
                    if more:
                        for j in range(2):
                            split_v(g + 1, 1 - s, j)

                nc.vector.memset(y[:], 0.0).then_inc(y_zero, 1)
                for j in range(2):
                    split_u(0, j)
                    split_v(0, 0, j)
                group(0, 0, before=False)
                with dve.Fori(0, (NG - 2) // 2) as i:
                    group(2 * i + 1, 1)
                    group(2 * i + 2, 0)
                group(NG - 1, 1, more=False)
                gather(NG - 1, 0, 2 * NT)


def finish(nc, sem, io, scr, cst, y, out):
    with ExitStack() as ctx:
        def sb(name, shape, dt=F32):
            return ctx.enter_context(nc.sbuf_tensor(name, shape, dt))

        x1 = [sb(f"f_x{s}", [P, D]) for s in range(2)]
        lng = sb("f_g", [P, D])
        lnb = sb("f_b", [P, D])
        st = sb("f_st", [P, 2, 6])
        mv = [sb(f"f_mv{s}", [P, 3]) for s in range(2)]
        side = sem("f_side")
        tick = sem("f_tick")
        x_in = [sem(f"f_in{s}") for s in range(2)]
        stored = [sem(f"f_out{s}") for s in range(2)]
        h, stat, aggr, root, rec, nrm, nrm_g, done = (sem(f"f_{n}") for n in "h stat aggr root rec nrm nrm_g done".split())
        with nc.Block() as block:
            @block.sync
            def _(sp):
                sp.dma_start(lng[:], io["ln2_g"].partition_broadcast(P)).then_inc(side, 16)
                sp.dma_start(lnb[:], io["ln2_b"].partition_broadcast(P)).then_inc(side, 16)
                with sp.Fori(0, NT // 2) as i:
                    for s in range(2):
                        sp.wait_ge(stored[s], 16 * i)
                        sp.dma_start(x1[s][:], scr["x1"][ts((2 * i + s) * P, P), :]).then_inc(x_in[s], 16)

            @block.scalar
            def _(act):
                with act.Fori(0, NT // 2) as i:
                    for s in range(2):
                        c = 2 * i + s
                        act.wait_ge(aggr, c + 1)
                        nc.scalar.activation(mv[s][:, 2:3], mv[s][:, 1:2], ACT.Sqrt,
                                             bias=cst[:, C_EPS:C_EPS + 1]).then_inc(root, 1)
                        act.wait_ge(done, c + 1)
                        act.dma_start(out[0, ts(c * P, P), :], x1[s][:]).then_inc(stored[s], 16)
                for s in range(2):
                    act.wait_ge(stored[s], 16 * (NT // 2))

            @block.vector
            def _(dve):
                dve.wait_ge(side, 32)
                with dve.Fori(0, NT // 2) as i:
                    for s in range(2):
                        c = 2 * i + s
                        now = c + 1
                        dve.wait_ge(x_in[s], 16 * (i + 1))
                        nc.vector.scalar_tensor_tensor(x1[s][:], x1[s][:], ALPHA,
                                                       y[:, ts(c, 1), :].rearrange("p t d -> p (t d)"),
                                                       ALU.mult, ALU.add).then_inc(h, 1)
                        dve.wait_ge(h, now)
                        for n in range(2):
                            nc.vector.bn_stats(st[:, n, :], x1[s][:, n * HALF:(n + 1) * HALF]).then_inc(stat, 1)
                        wait_apart(dve, tick, stat, 2 * now)
                        nc.vector.bn_aggr(mv[s][:, 0:2], st[:]).then_inc(aggr, 1)
                        dve.wait_ge(root, now)
                        nc.vector.reciprocal(mv[s][:, 2:3], mv[s][:, 2:3]).then_inc(rec, 1)
                        dve.wait_ge(rec, now)
                        nc.vector.tensor_scalar(x1[s][:], x1[s][:], mv[s][:, 0:1], mv[s][:, 2:3], ALU.subtract,
                                                ALU.mult).then_inc(nrm, 1)
                        dve.wait_ge(nrm, now)
                        nc.vector.tensor_tensor(x1[s][:], x1[s][:], lng[:], ALU.mult).then_inc(nrm_g, 1)
                        dve.wait_ge(nrm_g, now)
                        nc.vector.tensor_tensor(x1[s][:], x1[s][:], lnb[:], ALU.add).then_inc(done, 1)


def build(nc, io, out):
    with ExitStack() as ctx:
        scr = {
            "ch": nc.dram_tensor("s_ch", (N_CH, P, T), F32).ap(),
            "sk": nc.dram_tensor("s_sk", (P, P + T), F32).ap(),
            "sv": nc.dram_tensor("s_sv", (P + T, P), F32).ap(),
            "z": nc.dram_tensor("s_z", (T, GH * P), F32).ap(),
            "x1": nc.dram_tensor("s_x1", (T, D), F32).ap(),
            "G": nc.dram_tensor("s_G", (T // TG, P, NK, TG), F32).ap(),
        }
        psum = ctx.enter_context(nc.psum_tensor("psum", [P, 8, HALF], F32))
        cst = ctx.enter_context(nc.sbuf_tensor("cst", [P, C_N], F32))
        cst_in = ctx.enter_context(nc.semaphore("cst_in"))
        with nc.Block() as block:
            @block.sync
            def _(sp):
                sp.dma_start(cst[:], io["consts"]).then_inc(cst_in, 16)
                sp.wait_ge(cst_in, 16)
        with ExitStack() as mixer:
            ba = mixer.enter_context(nc.sbuf_tensor("ba", [P, NT, 2 * GH], F32))
            with stage_semaphores(nc) as sem:
                project(nc, sem, io, scr, ba, psum)
            with stage_semaphores(nc) as sem:
                mix_tokens(nc, sem, io, scr, ba, cst, psum)
        x1h = ctx.enter_context(nc.sbuf_tensor("x1h", [P, KC, T], F32R))
        x1l = ctx.enter_context(nc.sbuf_tensor("x1l", [P, KC, T], F32R))
        with stage_semaphores(nc) as sem:
            split_x1(nc, sem, scr, cst, psum, x1h, x1l)
        with ExitStack() as picks:
            key1, key2, gate = (picks.enter_context(nc.sbuf_tensor(n, [P, NT, PH * TOPK], F32))
                                for n in ("key1", "key2", "gate"))
            with stage_semaphores(nc) as sem:
                retrieve(nc, sem, io, cst, psum, x1h, x1l, key1, key2, gate)
            with stage_semaphores(nc) as sem:
                build_gates(nc, sem, scr, cst, psum, key1, key2, gate)
        with ExitStack() as sums:
            y = sums.enter_context(nc.sbuf_tensor("y", [P, NT, D], F32))
            with stage_semaphores(nc) as sem:
                experts(nc, sem, io, scr, psum, x1h, x1l, y)
            with stage_semaphores(nc) as sem:
                finish(nc, sem, io, scr, cst, y, out)


def layout(inputs):
    a = {k: np.asarray(v) for k, v in inputs.items()}

    def blocks(w):
        return np.ascontiguousarray(w.reshape(KC, P, -1, P).transpose(2, 1, 0, 3))

    def rows(w):
        return np.ascontiguousarray(w.reshape(KC, P, -1).transpose(1, 0, 2))

    w = a["w_in"][0]
    q0 = 4 * GH * P + 2 * GH
    k0, v0 = q0 + AH * AD, q0 + AH * AD + 2 * AD
    order = np.concatenate([np.arange(AD) + (r * 4 + p) * AD for p in range(4) for r in range(2)])
    channels = np.concatenate([w[:, 0:3 * GH * P], w[:, q0 + order], w[:, k0:v0]], axis=1)
    keys = np.stack([a["peer_k1"][0], a["peer_k2"][0]], axis=1).transpose(0, 1, 3, 2).reshape(2 * PH, P, NK)
    return {
        "x": a["x"][0], "xT": np.ascontiguousarray(a["x"][0].T), "w_ch": blocks(channels),
        "w_z": rows(w[:, 3 * GH * P:4 * GH * P]),
        "w_s": rows(np.concatenate([w[:, v0:], w[:, 4 * GH * P:q0]], axis=1)),
        "conv_w": np.ascontiguousarray(a["gdn_conv_w"][0].reshape(4, N_CONV, P).transpose(2, 1, 0)),
        "a_log": a["gdn_a_log"][0], "dt_bias": a["gdn_dt_bias"][0], "norm_w": a["gdn_norm_w"][0],
        "sinks": a["swa_sinks"][0], "w_out": a["w_out"][0], "ln1_g": a["ln1_g"][0], "ln1_b": a["ln1_b"][0],
        "wq": blocks(a["peer_wq"][0]), "keysT": np.ascontiguousarray(keys),
        "uT": np.ascontiguousarray(a["peer_u"][0].reshape(NK, NK, KC, P).transpose(0, 3, 2, 1)),
        "v": a["peer_v"][0], "ln2_g": a["ln2_g"][0], "ln2_b": a["ln2_b"][0],
        "consts": constants(), "wmask": window_masks(),
    }


def kernel(**inputs):
    import concourse.bacc as bacc
    from concourse.bass_utils import run_bass_kernel_spmd

    nc = bacc.Bacc("TRN2", target_bir_lowering=False, num_devices=1)
    arrays = {f"in_{k}": v for k, v in layout(inputs).items()}
    io = {k[3:]: nc.dram_tensor(k, v.shape, mybir.dt.from_np(v.dtype), kind="ExternalInput").ap()
          for k, v in arrays.items()}
    out = nc.dram_tensor("out", (1, T, D), F32, kind="ExternalOutput").ap()
    build(nc, io, out)
    result = run_bass_kernel_spmd(nc, [arrays], core_ids=[0])
    return result.results[0]["out"]
```

```python
from contextlib import ExitStack, contextmanager

import concourse.bass as bass
import numpy as np
from concourse import mybir

F32 = mybir.dt.float32
F32R = mybir.dt.float32r
U32 = mybir.dt.uint32
ALU = mybir.AluOpType
ACT = mybir.ActivationFunctionType
AX = mybir.AxisListType.X

P = 128
T = 1024
D = 1024
NT = T // P
KC = D // P
GH = 4
AH = 8
AD = 64
N_CH = 16
N_CONV = 12
PH = 8
TOPK = 16
NK = 128
HALF = 512
TG = 64
ALPHA = 2.0 ** 0.25
LN_EPS = 1e-5
RMS_EPS = 1e-6
L2_EPS = 1e-6
MASKED = -1e30
REPLACED = -3e38
TAIL = 4
AHEAD_R = PH + TAIL
AHEAD_G = T // (2 * TG)
AHEAD = AHEAD_R + AHEAD_G
LEVELS = 7

C_ID, C_TRIU, C_NEG, C_ONES, C_LEVEL = 0, 128, 256, 384, 512
C_IOTA = C_LEVEL + LEVELS * 128
C_IOTA16 = C_IOTA + 128
C_EPS = C_IOTA16 + 16
C_N = C_EPS + 4


def constants():
    c = np.zeros((P, C_N), np.float32)
    i, j = np.arange(P)[:, None], np.arange(P)[None, :]
    c[:, C_ID:C_ID + 128] = i == j
    c[:, C_TRIU:C_TRIU + 128] = i <= j
    c[:, C_NEG:C_NEG + 128] = np.where(j >= i, 0.0, MASKED)
    c[:, C_ONES:C_ONES + 128] = 1.0
    for n in range(LEVELS):
        bi, bj = i >> n, j >> n
        c[:, C_LEVEL + 128 * n:C_LEVEL + 128 * (n + 1)] = np.where((bi % 2 == 1) & (bj == bi - 1), -1.0, 0.0)
    c[:, C_IOTA:C_IOTA + 128] = j
    c[:, C_IOTA16:C_IOTA16 + 16] = np.arange(16)
    c[:, C_EPS + 0] = LN_EPS
    c[:, C_EPS + 1] = RMS_EPS
    c[:, C_EPS + 2] = L2_EPS
    c[:, C_EPS + 3] = L2_EPS * P
    return c


def window_masks():
    q = np.arange(P)[:, None] // 64
    k = np.arange(2 * P)[None, :] // 64
    m = np.where((k == q + 1) | (k == q + 2), 0.0, MASKED).astype(np.float32)
    out = np.stack([m] * NT)
    out[0, :, :P] = MASKED
    return out


def ts(start, size):
    return bass.ds(start, size)


def wait_apart(engine, tick, semaphore, value):
    engine.wait_ge(semaphore, value)
    engine.sem_inc(tick, 1)


@contextmanager
def stage_semaphores(nc):
    used = []

    def sem(name):
        used.append(nc.alloc_semaphore(name))
        return used[-1]

    yield sem
    nc.clear_and_free_semaphores(used)
    nc.all_engine_barrier()


def project(nc, sem, io, scr, ba, cst, psum):
    with ExitStack() as ctx:
        def sb(name, shape, dt=F32):
            return ctx.enter_context(nc.sbuf_tensor(name, shape, dt))

        TOK = GH * P + P + 2 * GH
        xh = sb("p_xh", [P, KC, T], F32R)
        xl = sb("p_xl", [P, KC, T], F32R)
        part = [sb(f"p_part{s}", [P, T]) for s in range(2)]
        wr = [sb(f"p_wr{s}", [P, KC, P]) for s in range(2)]
        wh = [sb(f"p_wh{s}", [P, KC, P], F32R) for s in range(2)]
        wl = [sb(f"p_wl{s}", [P, KC, P], F32R) for s in range(2)]
        toh = sb("p_toh", [P, KC, TOK], F32R)
        tol = sb("p_tol", [P, KC, TOK], F32R)
        convw = sb("p_convw", [P, N_CONV, 4])
        normw = sb("p_normw", [P, P])
        raw = [sb(f"p_raw{s}", [P, 3 + T]) for s in range(2)]
        cv = [sb(f"p_cv{s}", [P, T]) for s in range(2)]
        out = [sb(f"p_out{s}", [P, T]) for s in range(2)]
        zt = [sb(f"p_zt{s}", [P, GH * P]) for s in range(2)]
        svt = [sb(f"p_sv{s}", [P, P]) for s in range(2)]
        zero = sb("p_zero", [P, P])
        squares = sb("p_squares", [P, 2 * GH, T])
        ps = [psum[:, 2 * s:2 * s + 2, :] for s in range(2)]

        part_in = [sem(f"part_in{s}") for s in range(2)]
        part_hi, part_lo = sem("part_hi"), sem("part_lo")
        w_hi = [sem(f"w_hi{s}") for s in range(2)]
        w_lo = [sem(f"w_lo{s}") for s in range(2)]
        side_in = sem("side_in")
        w_in = [sem(f"w_in{s}") for s in range(2)]
        mm = [sem(f"proj_mm{s}") for s in range(2)]
        evac = [sem(f"proj_evac{s}") for s in range(2)]
        zeroed = sem("proj_zeroed")
        squared = sem("squared")
        conv_step = sem("conv_step")
        conv_done = [sem(f"conv_done{s}") for s in range(2)]
        silu = [sem(f"silu{s}") for s in range(2)]
        stored = [sem(f"ch_stored{s}") for s in range(2)]
        gated = [sem(f"z_gated{s}") for s in range(2)]
        tok_stored = [sem(f"tok_stored{s}") for s in range(2)]
        pad_stored = sem("pad_stored")
        N_BLK = N_CH + 1
        with nc.Block() as block:
            @block.sync
            def _(sp):
                def load_w(n, s, b):
                    sp.wait_ge(w_lo[s], n)
                    sp.dma_start(wr[s][:], io["w_ch"][b]).then_inc(w_in[s], 16)

                load_w(0, 0, 0)
                for k in range(KC):
                    if k >= 2:
                        sp.wait_ge(part_lo, k - 1)
                    sp.dma_start(part[k % 2][:], io["xT"][k * P:(k + 1) * P, :]).then_inc(part_in[k % 2], 16)
                    if k == 2:
                        load_w(0, 1, 1)
                sp.dma_start(convw[:], io["conv_w"]).then_inc(side_in, 16)
                sp.dma_start(normw[:], io["norm_w"].partition_broadcast(P)).then_inc(side_in, 16)
                with sp.Fori(1, N_CH // 2) as i:
                    for s in range(2):
                        load_w(i, s, 2 * i + s)
                load_w(N_CH // 2, 0, N_CH)
                for k in range(KC):
                    sp.wait_ge(part_lo, KC + k - 1)
                    sp.dma_start(part[k % 2][:, 0:TOK], io["w_tok"][:, k, :]).then_inc(part_in[k % 2], 16)

            @block.tensor
            def _(pe):
                def channel_block(s, n, first=False):
                    pe.wait_ge(w_hi[s], n + 1)
                    pe.wait_ge(w_lo[s], n + 1)
                    pe.wait_ge(evac[s], n)
                    for k in range(KC):
                        if first:
                            pe.wait_ge(part_lo, k + 1)
                        for h in range(2):
                            c = slice(h * HALF, (h + 1) * HALF)
                            nc.tensor.matmul(ps[s][:, h, :], wh[s][:, k, :], xh[:, k, c], start=(k == 0), stop=False)
                            nc.tensor.matmul(ps[s][:, h, :], wh[s][:, k, :], xl[:, k, c], start=False, stop=False)
                            last = nc.tensor.matmul(ps[s][:, h, :], wl[s][:, k, :], xh[:, k, c], start=False,
                                                    stop=(k == KC - 1))
                    last.then_inc(mm[s], 1)

                channel_block(0, 0, first=True)
                channel_block(1, 0)
                with pe.Fori(1, N_CH // 2) as i:
                    for s in range(2):
                        channel_block(s, i)
                channel_block(0, N_CH // 2)
                pe.wait_ge(squared, 2 * GH)
                for t in range(NT):
                    for b in range(2 * GH):
                        nc.tensor.matmul(psum[:, 4, t * 2 * GH + b:t * 2 * GH + b + 1], squares[:, b, t * P:(t + 1) * P],
                                         cst[:, C_ONES:C_ONES + 1], start=True, stop=True)
                pe.wait_ge(part_lo, 2 * KC)
                for t in range(NT):
                    s = (t + 1) % 2
                    n = N_CH // 2 + (1 if s == 0 else 0) + t // 2
                    r = slice(t * P, (t + 1) * P)
                    pe.wait_ge(evac[s], n)
                    for k in range(KC):
                        for h in range(2):
                            c = slice(h * TOK // 2, (h + 1) * TOK // 2)
                            dst = ps[s][:, h, 0:TOK // 2]
                            nc.tensor.matmul(dst, xh[:, k, r], toh[:, k, c], start=(k == 0), stop=False)
                            nc.tensor.matmul(dst, xh[:, k, r], tol[:, k, c], start=False, stop=False)
                            last = nc.tensor.matmul(dst, xl[:, k, r], toh[:, k, c], start=False, stop=(k == KC - 1))
                    last.then_inc(mm[s], 1)

            @block.scalar
            def _(act):
                act.wait_ge(zeroed, 3)

                def split_w(n, s):
                    act.wait_ge(w_in[s], 16 * (n + 1))
                    act.wait_ge(mm[s], n)
                    nc.scalar.activation(wh[s][:], wr[s][:], ACT.Copy).then_inc(w_hi[s], 1)

                def split_part(q, dst):
                    act.wait_ge(part_in[q % 2], 16 * (q // 2 + 1))
                    nc.scalar.activation(dst, part[q % 2][:, 0:dst.shape[-1]], ACT.Copy).then_inc(part_hi, 1)

                split_w(0, 0)
                for k in range(KC):
                    split_part(k, xh[:, k, :])
                    if k == 3:
                        split_w(0, 1)

                def channels(i, s):
                    act.wait_ge(mm[s], i + 1)
                    act.wait_ge(conv_done[s], i)
                    nc.scalar.activation(raw[s][:, 3:3 + T], ps[s].rearrange("p h t -> p (h t)"),
                                         ACT.Copy).then_inc(evac[s], 1)
                    split_w(i + 1, s)
                    act.wait_ge(conv_done[s], i + 1)
                    act.wait_ge(stored[s], 16 * i)
                    nc.scalar.activation(out[s][:], cv[s][:], ACT.Silu).then_inc(silu[s], 1)

                with act.Fori(0, GH) as i:
                    for s in range(2):
                        channels(i, s)
                        act.wait_ge(silu[s], i + 1)
                        nc.scalar.activation(squares[:, ts(2 * i + s, 1), :].rearrange("p b t -> p (b t)"), out[s][:],
                                             ACT.Square).then_inc(squared, 1)
                with act.Fori(GH, N_CONV // 2) as i:
                    for s in range(2):
                        channels(i, s)
                for b in range(N_CONV, N_BLK):
                    s, n = b % 2, b // 2
                    act.wait_ge(mm[s], n + 1)
                    act.wait_ge(stored[s], 16 * n)
                    nc.scalar.activation(out[s][:], ps[s].rearrange("p h t -> p (h t)"), ACT.Copy).then_inc(evac[s], 1)
                    if b + 2 < N_BLK:
                        split_w(n + 1, s)
                    if b < N_CH:
                        for k in (2 * (b - N_CONV), 2 * (b - N_CONV) + 1):
                            split_part(KC + k, toh[:, k, :])
                for t in range(NT):
                    s = (t + 1) % 2
                    n = N_CH // 2 + (1 if s == 0 else 0) + t // 2
                    act.wait_ge(mm[s], n + 1)
                    if t >= 2:
                        act.wait_ge(tok_stored[s], 32 * (t // 2))
                    nc.scalar.activation(zt[s][:, 0:TOK // 2], ps[s][:, 0, 0:TOK // 2], ACT.Silu)
                    z1 = GH * P - TOK // 2
                    nc.scalar.activation(zt[s][:, TOK // 2:], ps[s][:, 1, 0:z1], ACT.Silu).then_inc(gated[s], 1)
                    nc.scalar.activation(svt[s][:], ps[s][:, 1, z1:z1 + P], ACT.Copy)
                    nc.scalar.activation(ba[:, t, :], ps[s][:, 1, z1 + P:TOK // 2], ACT.Copy).then_inc(evac[s], 1)

            @block.vector
            def _(dve):
                nc.vector.memset(raw[0][:, 0:3], 0.0).then_inc(zeroed, 1)
                nc.vector.memset(raw[1][:, 0:3], 0.0).then_inc(zeroed, 1)
                nc.vector.memset(zero[:], 0.0).then_inc(zeroed, 1)

                def split_w(n, s):
                    dve.wait_ge(w_hi[s], n + 1)
                    nc.vector.tensor_tensor(wl[s][:], wr[s][:], wh[s][:].bitcast(F32), ALU.subtract).then_inc(w_lo[s], 1)

                def split_part(q, hi, lo):
                    dve.wait_ge(part_hi, q + 1)
                    nc.vector.tensor_tensor(lo, part[q % 2][:, 0:hi.shape[-1]], hi.bitcast(F32),
                                            ALU.subtract).then_inc(part_lo, 1)

                split_w(0, 0)
                for k in range(KC):
                    split_part(k, xh[:, k, :], xl[:, k, :])
                    if k == 3:
                        split_w(0, 1)
                dve.wait_ge(side_in, 32)
                with dve.Fori(0, N_CONV // 2) as i:
                    for s in range(2):
                        b = 2 * i + s
                        dve.wait_ge(evac[s], i + 1)
                        dve.wait_ge(silu[s], i)
                        nc.vector.tensor_scalar(cv[s][:], raw[s][:, 0:T], convw[:, ts(b, 1), 0], None,
                                                ALU.mult).then_inc(conv_step, 1)
                        for k in range(1, 4):
                            dve.wait_ge(conv_step, b * 3 + k)
                            step = nc.vector.scalar_tensor_tensor(cv[s][:], raw[s][:, k:k + T], convw[:, ts(b, 1), k],
                                                                  cv[s][:], ALU.mult, ALU.add)
                            step.then_inc(conv_step if k < 3 else conv_done[s], 1)
                        split_w(i + 1, s)
                for b in range(N_CONV, N_CH):
                    if b + 2 <= N_CH:
                        split_w(b // 2 + 1, b % 2)
                    for k in (2 * (b - N_CONV), 2 * (b - N_CONV) + 1):
                        split_part(KC + k, toh[:, k, :], tol[:, k, :])
                for t in range(NT):
                    s = (t + 1) % 2
                    dve.wait_ge(gated[s], t // 2 + 1)
                    zv = zt[s].rearrange("p (h d) -> p h d", h=GH)
                    nc.vector.tensor_tensor(zv, zv, normw[:, :].unsqueeze(1).broadcast_to([P, GH, P]),
                                            ALU.mult).then_inc(silu[s], 1)

            @block.gpsimd
            def _(pool):
                pool.wait_ge(zeroed, 3)
                pool.dma_start(scr["sk"][:, 0:P], zero[:]).then_inc(pad_stored, 16)
                pool.dma_start(scr["sv"][0:P, :], zero[:]).then_inc(pad_stored, 16)
                with pool.Fori(0, N_CONV // 2) as i:
                    for s in range(2):
                        pool.wait_ge(silu[s], i + 1)
                        pool.dma_start(scr["ch"][2 * i + s], out[s][:]).then_inc(stored[s], 16)
                for b in range(N_CONV, N_CH):
                    s, n = b % 2, b // 2
                    pool.wait_ge(evac[s], n + 1)
                    pool.dma_start(scr["ch"][b], out[s][:]).then_inc(stored[s], 16)
                pool.wait_ge(evac[0], N_CH // 2 + 1)
                pool.dma_start(scr["sk"][:, P:P + T], out[0][:]).then_inc(stored[0], 16)
                for t in range(NT):
                    s = (t + 1) % 2
                    pool.wait_ge(silu[s], N_CONV // 2 + t // 2 + 1)
                    pool.dma_start(scr["z"][t * P:(t + 1) * P, :], zt[s][:]).then_inc(tok_stored[s], 16)
                    pool.wait_ge(evac[s], N_CH // 2 + (1 if s == 0 else 0) + t // 2 + 1)
                    pool.dma_start(scr["sv"][(t + 1) * P:(t + 2) * P, :], svt[s][:]).then_inc(tok_stored[s], 16)
                pool.wait_ge(pad_stored, 32)
                pool.wait_ge(stored[0], 16 * (N_CH // 2 + 1))
                pool.wait_ge(stored[1], 16 * (N_CH // 2))
                for s in range(2):
                    pool.wait_ge(tok_stored[s], 16 * NT)


def mix_tokens(nc, sem, io, scr, ba, cst, psum):
    with ExitStack() as ctx:
        def sb(name, shape, dt=F32):
            return ctx.enter_context(nc.sbuf_tensor(name, shape, dt))

        ident = cst[:, C_ID:C_ID + P]
        triu = cst[:, C_TRIU:C_TRIU + P]
        neg = cst[:, C_NEG:C_NEG + P]
        ones = cst[:, C_ONES:C_ONES + P]

        def heads(ap):
            return ap.unsqueeze(1).broadcast_to([P, GH, P])

        wout = sb("m_wout", [P, KC, D])
        lng = sb("m_lng", [P, D])
        lnb = sb("m_lnb", [P, D])
        sinks = sb("m_sinks", [P, AH])
        dtb = sb("m_dtb", [P, GH])
        alog = sb("m_alog", [P, GH])
        ch = [sb(f"m_ch{s}", [P, N_CH, P]) for s in range(2)]
        kw = [sb(f"m_kw{s}", [P, 2 * P]) for s in range(2)]
        vw = [sb(f"m_vw{s}", [P, 2, P]) for s in range(2)]
        zw = [sb(f"m_zw{s}", [P, GH, P]) for s in range(2)]
        wm = [sb(f"m_wm{s}", [P, 2 * P]) for s in range(2)]
        xt = [sb(f"m_xt{s}", [P, D]) for s in range(2)]
        mag = sb("m_mag", [P, NT, 2 * GH])
        clip = sb("m_clip", [P, NT, 2 * GH])
        lr = sb("m_lr", [P, NT, 2 * GH])
        small = {n: sb(f"m_{n}", [P, NT, GH]) for n in ("lnbeta", "g", "gam", "nkey", "kdl", "kdec", "nbeg", "decay", "beta")}
        rows = sb("m_rows", [P, NT, 2, GH])
        gB = sb("m_gB", [P, 2 * GH, P])
        e0 = sb("m_e0", [P, GH, P])
        dm = sb("m_dm", [P, 2, GH, P])
        eg = sb("m_eg", [P, GH, P])
        aq = sb("m_aq", [P, 2, GH, P])
        qd = sb("m_qd", [P, GH, P])
        kd = sb("m_kd", [P, GH, P])
        vb = sb("m_vb", [P, GH, P])
        tu = sb("m_tu", [P, 2, GH, P])
        xs = sb("m_xs", [P, GH, P])
        uu = sb("m_uu", [P, GH, P])
        state = sb("m_state", [P, GH, P])
        faded = sb("m_faded", [P, GH, P])
        og = sb("m_og", [P, GH, P])
        rms = sb("m_rms", [P, GH])
        mixT = [sb(f"m_mixT{s}", [P, KC, P]) for s in range(2)]
        sc = sb("m_sc", [P, AH, 2 * P])
        pT = sb("m_pT", [P, AH, 2, P])
        on = sb("m_on", [P, AH, AD])
        mx = sb("m_mx", [P, 4, AH])
        h1 = sb("m_h1", [P, D])
        st = sb("m_st", [P, 2, 6])
        mv = sb("m_mv", [P, 3])

        def bank(b):
            return psum[:, b, :].rearrange("p (h d) -> p h d", h=GH)

        KKQ = psum[:, 0:2, :].rearrange("p b (h d) -> p b h d", h=GH)
        ROW = psum[:, 2:4, :].rearrange("p b (h d) -> p b h d", h=GH)
        ATT = psum[:, 4:6, :].rearrange("p b k -> p (b k)")

        side_in = sem("mix_side_in")
        ln_in = sem("ln_in")
        wout_in = sem("wout_in")
        tile_in = [[sem(f"tile_in{s}_{n}") for n in range(6)] for s in range(2)]
        x1_out = sem("x1_stored")
        tick = sem("m_tick")
        prep = {n: sem(f"prep_{n}") for n in "bias abs exp one ln g0 g sums gam kdl rows exps done".split()}
        names = ("gB e0 row eg e_add dmx kq aq qd tr kd xt0 xs0 t1 t1T u1 decayed ks kb r2 u_mm u_ev ods st_up "
                 "osq osum oln orms og ogT mg mask max mx nmx prob p_tr p_ev s_mm den rec o_mm o_n onT ma "
                 "proj h1 stat aggr ln1 rstd nrm nrm_g x1").split()
        S = {n: sem(f"m_{n}") for n in names}
        lx, lm, lt, lu, la, lb = (sem(f"level_{n}") for n in ("x", "masked", "t", "u", "t_add", "u_add"))
        LV = LEVELS - 1
        last_tile = NT - 1

        def load(sp, c, s):
            for n, (dst, src) in enumerate((
                    (ch[s][:], scr["ch"][:, :, ts(c * P, P)].rearrange("b p t -> p b t")),
                    (kw[s][:], scr["sk"][:, ts(c * P, 2 * P)]),
                    (vw[s][:], scr["sv"][ts(c * P, 2 * P), :].rearrange("(a p) d -> p a d", a=2)),
                    (zw[s][:], scr["z"][ts(c * P, P), :].rearrange("p (h d) -> p h d", h=GH)),
                    (wm[s][:], io["wmask"][ts(c, 1)].rearrange("a p k -> (a p) k")))):
                sp.dma_start(dst, src).then_inc(tile_in[s][n], 16)

        def load_x(sp, c, s):
            sp.dma_start(xt[s][:], io["x"][ts(c * P, P), :]).then_inc(tile_in[s][5], 16)

        def tiles(engine, body):
            body(0, 0, 0, False)
            body(1, 0, 1, True)
            with engine.Fori(1, NT // 2) as i:
                body(2 * i, i, 0, True)
                body(2 * i + 1, i, 1, True)

        with nc.Block() as block:
            @block.sync
            def _(sp):
                sp.dma_start(sinks[:], io["sinks"].partition_broadcast(P)).then_inc(side_in, 16)
                sp.dma_start(dtb[:], io["dt_bias"].partition_broadcast(P)).then_inc(side_in, 16)
                sp.dma_start(alog[:], io["a_log"].partition_broadcast(P)).then_inc(side_in, 16)
                for s in range(2):
                    load(sp, s, s)
                    load_x(sp, s, s)
                sp.dma_start(wout[:], io["w_out"].rearrange("(k p) n -> p k n", p=P)).then_inc(wout_in, 16)
                sp.dma_start(lng[:], io["ln1_g"].partition_broadcast(P)).then_inc(ln_in, 16)
                sp.dma_start(lnb[:], io["ln1_b"].partition_broadcast(P)).then_inc(ln_in, 16)

                def refill(c, s):
                    sp.wait_ge(S["og"], c + 1)
                    sp.wait_ge(S["o_mm"], c + 1)
                    load(sp, c + 2, s)

                def store(c, s, more=True):
                    sp.wait_ge(S["x1"], c + 1)
                    sp.dma_start(scr["x1"][ts(c * P, P), :], h1[:]).then_inc(x1_out, 16)
                    if more:
                        load_x(sp, c + 2, s)

                refill(0, 0)
                with sp.Fori(0, NT // 2 - 2) as i:
                    refill(2 * i + 1, 1)
                    store(2 * i, 0)
                    refill(2 * i + 2, 0)
                    store(2 * i + 1, 1)
                refill(NT - 3, 1)
                store(NT - 4, 0)
                store(NT - 3, 1)
                for s in range(2):
                    store(NT - 2 + s, s, more=False)
                sp.wait_ge(x1_out, 16 * NT)

            @block.tensor
            def _(pe):
                pe.wait_ge(prep["g"], 1)
                nc.tensor.matmul(psum[:, 0, 0:NT * GH], triu, small["g"].rearrange("p t h -> p (t h)"),
                                 start=True, stop=True)
                nc.tensor.matmul(psum[:, 0, NT * GH:2 * NT * GH], ones, small["g"].rearrange("p t h -> p (t h)"),
                                 start=True, stop=True).then_inc(prep["sums"], 1)
                pe.wait_ge(prep["done"], 1)
                pe.wait_ge(wout_in, 16)

                def project_out(s, first, n):
                    for m in range(first, first + n):
                        half, k = divmod(m, KC)
                        last = nc.tensor.matmul(psum[:, 6 + half, :], mixT[s][:, k, :],
                                                wout[:, k, half * HALF:(half + 1) * HALF],
                                                start=(k == 0), stop=(k == KC - 1))
                    return last

                def scores(s, half):
                    for n in range(4):
                        last = nc.tensor.matmul(ATT[:, n * 2 * P:(n + 1) * 2 * P],
                                                ch[s][64 * half:64 * half + 64, N_CONV + n, :],
                                                kw[s][64 * half:64 * half + 64, :], start=True, stop=True)
                    last.then_inc(S["s_mm"], 1)

                def transpose_probs(half):
                    for n in range(8):
                        last = nc.tensor.transpose(ATT[:, n * P:(n + 1) * P],
                                                   sc[:, 4 * half + n // 2, (n % 2) * P:(n % 2 + 1) * P], ident)
                    last.then_inc(S["p_tr"], 1)

                def body(c, i, s, before):
                    now = c + 1
                    pe.wait_ge(tile_in[s][0], 16 * (i + 1))
                    for n in range(2):
                        for h in range(GH):
                            last = nc.tensor.matmul(KKQ[:, n, h, :], ch[s][:, GH + h, :], ch[s][:, (1 - n) * GH + h, :],
                                                    start=True, stop=True)
                    last.then_inc(S["kq"], 1)
                    pe.wait_ge(S["gB"], now)
                    for h in range(2 * GH):
                        last = nc.tensor.matmul(ROW[:, h // GH, h % GH, :], gB[:, h, :], ident, start=True, stop=True)
                    last.then_inc(S["row"], 1)
                    pe.wait_ge(tile_in[s][1], 16 * (i + 1))
                    if before:
                        pe.wait_ge(S["ma"], c)
                    scores(s, 0)
                    pe.wait_ge(S["e_add"], now)
                    for h in range(GH):
                        nc.tensor.transpose(bank(2)[:, h, :], ch[s][:, GH + h, :], ident)
                    for h in range(GH):
                        last = nc.tensor.transpose(bank(3)[:, h, :], ch[s][:, 2 * GH + h, :], ident)
                    last.then_inc(S["tr"], 1)
                    pe.wait_ge(S["aq"], now)
                    for h in range(GH):
                        last = nc.tensor.transpose(bank(0)[:, h, :], aq[:, 0, h, :], ident)
                    last.then_inc(S["xt0"], 1)
                    pe.wait_ge(S["kd"], now)
                    pe.wait_ge(S["t1"], now)
                    for h in range(GH):
                        last = nc.tensor.transpose(bank(3)[:, h, :], tu[:, 0, h, :], ident)
                    last.then_inc(S["t1T"], 1)
                    for n in range(LV):
                        at_level = c * LV + n + 1
                        if n:
                            pe.wait_ge(la, c * (LV - 1) + n)
                        for h in range(GH):
                            last = nc.tensor.matmul(bank(0)[:, h, :], aq[:, 0, h, :], tu[:, 0, h, :], start=True, stop=True)
                        last.then_inc(lx, 1)
                        if before:
                            project_out(1 - s, 2 * n, 2)
                        if n == 2:
                            pe.wait_ge(S["prob"], 2 * c + 1)
                            transpose_probs(0)
                        if n == 3:
                            pe.wait_ge(S["p_ev"], 2 * c + 1)
                            scores(s, 1)
                        pe.wait_ge(lm, at_level)
                        if n == 0:
                            pe.wait_ge(S["u1"], now)
                        else:
                            pe.wait_ge(lb, c * LV + n)
                        if n < LV - 1:
                            for h in range(GH):
                                last = nc.tensor.matmul(bank(2)[:, h, :], tu[:, 1, h, :], xs[:, h, :], start=True, stop=True)
                            last.then_inc(lt, 1)
                        for h in range(GH):
                            last = nc.tensor.matmul(bank(3)[:, h, :], xs[:, h, :], tu[:, 1, h, :], start=True, stop=True)
                        last.then_inc(lu, 1)
                    if before:
                        pe.wait_ge(S["st_up"], c)
                    for h in range(GH):
                        last = nc.tensor.matmul(bank(0)[:, h, :], ch[s][:, GH + h, :], state[:, h, :], start=True, stop=True)
                    last.then_inc(S["ks"], 1)
                    if before:
                        project_out(1 - s, 12, 2)
                    pe.wait_ge(S["r2"], now)
                    pe.wait_ge(lb, now * LV)
                    for h in range(GH):
                        last = nc.tensor.matmul(bank(1)[:, h, :], tu[:, 1, h, :], vb[:, h, :], start=True, stop=True)
                    last.then_inc(S["u_mm"], 1)
                    if before:
                        project_out(1 - s, 14, 2).then_inc(S["proj"], 1)
                    pe.wait_ge(S["u_ev"], now)
                    for h in range(GH):
                        nc.tensor.matmul(bank(3)[:, h, :], kd[:, h, :], uu[:, h, :], start=True, stop=True)
                    for h in range(GH):
                        nc.tensor.matmul(bank(2)[:, h, :], aq[:, 1, h, :], uu[:, h, :], start=True, stop=False)
                        last = nc.tensor.matmul(bank(2)[:, h, :], qd[:, h, :], state[:, h, :], start=False, stop=True)
                    last.then_inc(S["ods"], 1)
                    pe.wait_ge(S["prob"], 2 * now)
                    transpose_probs(1)
                    pe.wait_ge(S["p_ev"], 2 * now)
                    pe.wait_ge(tile_in[s][2], 16 * (i + 1))
                    for a in range(AH):
                        r = a // 4
                        for k in range(2):
                            last = nc.tensor.matmul(psum[:, 4, a * AD:(a + 1) * AD], pT[:, a, k, :],
                                                    vw[s][:, k, r * AD:(r + 1) * AD], start=(k == 0), stop=(k == 1))
                    last.then_inc(S["o_mm"], 1)
                    pe.wait_ge(S["og"], now)
                    for h in range(GH):
                        last = nc.tensor.transpose(bank(1)[:, h, :], og[:, h, :], ident)
                    last.then_inc(S["ogT"], 1)
                    pe.wait_ge(S["o_n"], now)
                    for p in range(4):
                        last = nc.tensor.transpose(bank(5)[:, p, :], on[:, 2 * p:2 * p + 2, :].rearrange("p a d -> p (a d)"),
                                                   ident)
                    last.then_inc(S["onT"], 1)
                    pe.wait_ge(S["mg"], now)
                    pe.wait_ge(S["ma"], now)
                    if before:
                        pe.wait_ge(S["h1"], 2 * c)

                tiles(pe, body)
                project_out(last_tile % 2, 0, 2 * KC).then_inc(S["proj"], 1)

            @block.scalar
            def _(act):
                act.wait_ge(side_in, 48)
                act.wait_ge(prep["bias"], 1)
                nc.scalar.activation(mag[:], ba[:], ACT.Abs).then_inc(prep["abs"], 1)
                act.wait_ge(prep["abs"], 1)
                nc.scalar.activation(mag[:], mag[:], ACT.Exp, scale=-1.0).then_inc(prep["exp"], 1)
                nc.scalar.activation(alog[:], alog[:], ACT.Exp)
                lrv = lr.rearrange("p t (a h) -> p t a h", a=2)
                ss = psum[:, 4, 0:NT * 2 * GH].rearrange("p (t a h) -> p t a h", t=NT, a=2)
                nc.scalar.activation(lrv[:, :, 0, :], ss[:, :, 0, :], ACT.Ln, scale=float(P), bias=cst[:, C_EPS + 3:C_EPS + 4])
                nc.scalar.activation(lrv[:, :, 1, :], ss[:, :, 1, :], ACT.Ln, bias=cst[:, C_EPS + 2:C_EPS + 3])
                act.wait_ge(prep["one"], 1)
                nc.scalar.activation(mag[:], mag[:], ACT.Ln).then_inc(prep["ln"], 1)
                act.wait_ge(prep["rows"], 1)
                nc.scalar.activation(small["beta"][:], small["lnbeta"][:], ACT.Exp)
                nc.scalar.activation(small["kdec"][:], small["kdl"][:], ACT.Exp)
                nc.scalar.activation(small["nbeg"][:], rows[:, :, 0, :], ACT.Exp)
                nc.scalar.activation(small["decay"].rearrange("p t h -> p (t h)"), psum[:, 0, NT * GH:2 * NT * GH],
                                     ACT.Exp).then_inc(prep["exps"], 1)

                def exps(c, half):
                    act.wait_ge(S["nmx"], 2 * c + half + 1)
                    for a in range(4 * half, 4 * half + 4):
                        nc.scalar.activation(sc[:, a, :], sc[:, a, :], ACT.Exp, bias=mx[:, 1, a:a + 1],
                                             accum_out=mx[:, 3, a:a + 1])
                    a = slice(4 * half, 4 * half + 4)
                    nc.scalar.activation(mx[:, 2, a], mx[:, 2, a], ACT.Exp).then_inc(S["prob"], 1)

                def evacuate_probs(c, half):
                    act.wait_ge(S["p_tr"], 2 * c + half + 1)
                    nc.scalar.activation(pT[:, 4 * half:4 * half + 4].rearrange("p a k q -> p (a k q)"), ATT,
                                         ACT.Copy).then_inc(S["p_ev"], 1)

                def rstd(c):
                    act.wait_ge(S["aggr"], c + 1)
                    nc.scalar.activation(mv[:, 2:3], mv[:, 1:2], ACT.Ln, bias=cst[:, C_EPS:C_EPS + 1]).then_inc(S["ln1"], 1)
                    act.wait_ge(S["ln1"], c + 1)
                    nc.scalar.activation(mv[:, 2:3], mv[:, 2:3], ACT.Exp, scale=-0.5).then_inc(S["rstd"], 1)

                def body(c, i, s, before):
                    now = c + 1
                    act.wait_ge(S["row"], now)
                    nc.scalar.activation(eg[:], bank(3), ACT.Exp).then_inc(S["eg"], 1)
                    act.wait_ge(S["e_add"], now)
                    nc.scalar.activation(dm[:], dm[:], ACT.Exp).then_inc(S["dmx"], 1)
                    act.wait_ge(S["t1T"], now)
                    nc.scalar.activation(tu[:, 1], bank(3), ACT.Copy).then_inc(S["u1"], 1)
                    exps(c, 0)
                    evacuate_probs(c, 0)
                    exps(c, 1)
                    act.wait_ge(S["u_mm"], now)
                    nc.scalar.activation(uu[:], bank(1), ACT.Copy).then_inc(S["u_ev"], 1)
                    act.wait_ge(S["ods"], now)
                    nc.scalar.activation(og[:], bank(2), ACT.Square).then_inc(S["osq"], 1)
                    evacuate_probs(c, 1)
                    act.wait_ge(S["osum"], now)
                    nc.scalar.activation(rms[:], rms[:], ACT.Ln, scale=1.0 / P,
                                         bias=cst[:, C_EPS + 1:C_EPS + 2]).then_inc(S["oln"], 1)
                    act.wait_ge(S["oln"], now)
                    nc.scalar.activation(rms[:], rms[:], ACT.Exp, scale=-0.5).then_inc(S["orms"], 1)
                    act.wait_ge(S["ogT"], now)
                    nc.scalar.activation(mixT[s][:, 0:GH, :], bank(1), ACT.Copy).then_inc(S["mg"], 1)
                    act.wait_ge(S["onT"], now)
                    nc.scalar.activation(mixT[s][:, GH:, :], bank(5), ACT.Copy).then_inc(S["ma"], 1)
                    if before:
                        rstd(c - 1)

                act.wait_ge(prep["done"], 1)
                tiles(act, body)
                rstd(last_tile)

            @block.vector
            def _(dve):
                dve.wait_ge(side_in, 48)
                nc.vector.tensor_tensor(ba[:, :, GH:2 * GH], ba[:, :, GH:2 * GH],
                                        dtb[:, :].unsqueeze(1).broadcast_to([P, NT, GH]), ALU.add).then_inc(prep["bias"], 1)
                dve.wait_ge(prep["exp"], 1)
                nc.vector.tensor_scalar(mag[:], mag[:], 1.0, None, ALU.add).then_inc(prep["one"], 1)
                nc.vector.tensor_scalar(clip[:, :, 0:GH], ba[:, :, 0:GH], 0.0, None, ALU.min)
                nc.vector.tensor_scalar(clip[:, :, GH:], ba[:, :, GH:], 0.0, None, ALU.max).then_inc(prep["g0"], 1)
                dve.wait_ge(prep["ln"], 1)
                dve.wait_ge(prep["g0"], 1)
                nc.vector.tensor_tensor(clip[:, :, GH:], clip[:, :, GH:], mag[:, :, GH:], ALU.add).then_inc(prep["g0"], 1)
                nc.vector.tensor_tensor(small["lnbeta"][:], clip[:, :, 0:GH], mag[:, :, 0:GH], ALU.subtract)
                nc.vector.tensor_scalar(lr[:], lr[:], -0.5, None, ALU.mult)
                dve.wait_ge(prep["g0"], 2)
                nc.vector.scalar_tensor_tensor(small["g"][:], clip[:, :, GH:], -1.0,
                                               alog[:, :].unsqueeze(1).broadcast_to([P, NT, GH]),
                                               ALU.mult, ALU.mult).then_inc(prep["g"], 1)
                dve.wait_ge(prep["g"], 1)
                dve.wait_ge(prep["sums"], 1)
                nc.vector.tensor_copy(small["gam"].rearrange("p t h -> p (t h)"),
                                      psum[:, 0, 0:NT * GH]).then_inc(prep["gam"], 1)
                dve.wait_ge(prep["gam"], 1)
                nc.vector.tensor_tensor(small["nkey"][:], lr[:, :, GH:], small["gam"][:], ALU.subtract).then_inc(prep["gam"], 1)
                nc.vector.tensor_tensor(rows[:, :, 1, :], small["gam"][:], lr[:, :, 0:GH], ALU.add)
                nc.vector.tensor_tensor(rows[:, :, 0, :], small["gam"][:], lr[:, :, GH:], ALU.add).then_inc(prep["kdl"], 1)
                dve.wait_ge(prep["gam"], 2)
                nc.vector.tensor_tensor(small["kdl"].rearrange("p t h -> p (t h)"), psum[:, 0, NT * GH:2 * NT * GH],
                                        small["nkey"].rearrange("p t h -> p (t h)"), ALU.add)
                dve.wait_ge(prep["kdl"], 1)
                nc.vector.tensor_tensor(rows[:, :, 0, :], rows[:, :, 0, :], small["lnbeta"][:],
                                        ALU.add).then_inc(prep["rows"], 1)
                nc.vector.memset(state[:], 0.0)
                dve.wait_ge(prep["rows"], 1)
                dve.wait_ge(prep["exps"], 1)
                nc.vector.tensor_scalar(small["nbeg"][:], small["nbeg"][:], -1.0, None, ALU.mult).then_inc(prep["done"], 1)
                dve.wait_ge(prep["done"], 1)

                def per_head(name, c):
                    return small[name][:, ts(c, 1), :].rearrange("p t h -> p (t h)").unsqueeze(2).broadcast_to([P, GH, P])

                def expand(c):
                    nc.vector.tensor_copy(gB[:], rows[:, ts(c, 1)].rearrange("p t a h -> p (t a h)").unsqueeze(2)
                                          .broadcast_to([P, 2 * GH, P])).then_inc(S["gB"], 1)
                    nc.vector.tensor_tensor(e0[:], heads(neg), per_head("nkey", c), ALU.add).then_inc(S["e0"], 1)

                def softmax_scores(c, s, half):
                    n = 2 * c + half + 1
                    a = slice(4 * half, 4 * half + 4)
                    dve.wait_ge(S["s_mm"], n)
                    nc.vector.scalar_tensor_tensor(sc[:, a, :], ATT.rearrange("p (a k) -> p a k", a=4), AD ** -0.5,
                                                   wm[s][:, :].unsqueeze(1).broadcast_to([P, 4, 2 * P]),
                                                   ALU.mult, ALU.add).then_inc(S["mask"], 1)

                def softmax_max(c, half):
                    n = 2 * c + half + 1
                    a = slice(4 * half, 4 * half + 4)
                    dve.wait_ge(S["mask"], n)
                    nc.vector.tensor_reduce(mx[:, 0, a], sc[:, a, :], AX, ALU.max).then_inc(S["max"], 1)
                    dve.wait_ge(S["max"], n)
                    nc.vector.tensor_tensor(mx[:, 0, a], mx[:, 0, a], sinks[:, a], ALU.max).then_inc(S["mx"], 1)
                    dve.wait_ge(S["mx"], n)
                    nc.vector.tensor_tensor(mx[:, 2, a], sinks[:, a], mx[:, 0, a], ALU.subtract)
                    nc.vector.tensor_scalar(mx[:, 1, a], mx[:, 0, a], -1.0, None, ALU.mult).then_inc(S["nmx"], 1)

                def layer_norm(c, i, s):
                    dve.wait_ge(S["proj"], c + 1)
                    dve.wait_ge(tile_in[s][5], 16 * (i + 1))
                    dve.wait_ge(x1_out, 16 * c)
                    for n in range(2):
                        nc.vector.scalar_tensor_tensor(h1[:, n * HALF:(n + 1) * HALF],
                                                       xt[s][:, n * HALF:(n + 1) * HALF], ALPHA, psum[:, 6 + n, :],
                                                       ALU.mult, ALU.add).then_inc(S["h1"], 1)
                    for n in range(2):
                        dve.wait_ge(S["h1"], 2 * c + n + 1)
                        nc.vector.bn_stats(st[:, n, :], h1[:, n * HALF:(n + 1) * HALF]).then_inc(S["stat"], 1)
                    wait_apart(dve, tick, S["stat"], 2 * (c + 1))
                    nc.vector.bn_aggr(mv[:, 0:2], st[:]).then_inc(S["aggr"], 1)
                    dve.wait_ge(S["rstd"], c + 1)
                    nc.vector.tensor_scalar(h1[:], h1[:], mv[:, 0:1], mv[:, 2:3], ALU.subtract,
                                            ALU.mult).then_inc(S["nrm"], 1)

                def body(c, i, s, before):
                    now = c + 1
                    expand(c)
                    dve.wait_ge(tile_in[s][4], 16 * (i + 1))
                    dve.wait_ge(S["e0"], now)
                    dve.wait_ge(S["eg"], now)
                    nc.vector.tensor_tensor(dm[:], ROW, e0[:, :, :].unsqueeze(1).broadcast_to([P, 2, GH, P]),
                                            ALU.add).then_inc(S["e_add"], 1)
                    nc.vector.tensor_tensor(qd[:], ch[s][:, 0:GH, :], eg[:], ALU.mult).then_inc(S["qd"], 1)
                    dve.wait_ge(S["dmx"], now)
                    dve.wait_ge(S["kq"], now)
                    nc.vector.tensor_tensor(aq[:], KKQ, dm[:], ALU.mult).then_inc(S["aq"], 1)
                    softmax_scores(c, s, 0)
                    dve.wait_ge(S["tr"], now)
                    nc.vector.tensor_tensor(kd[:], bank(2), per_head("kdec", c), ALU.mult)
                    nc.vector.tensor_tensor(vb[:], bank(3), per_head("beta", c), ALU.mult).then_inc(S["kd"], 1)
                    dve.wait_ge(S["xt0"], now)
                    nc.vector.tensor_tensor(xs[:], bank(0), heads(cst[:, C_LEVEL:C_LEVEL + P]), ALU.mult).then_inc(S["xs0"], 1)
                    dve.wait_ge(S["xs0"], now)
                    nc.vector.tensor_tensor(tu[:, 0], xs[:], heads(ident), ALU.add).then_inc(S["t1"], 1)
                    softmax_max(c, 0)
                    for n in range(LV):
                        dve.wait_ge(lx, c * LV + n + 1)
                        level = cst[:, C_LEVEL + (n + 1) * P:C_LEVEL + (n + 2) * P]
                        nc.vector.tensor_tensor(xs[:], bank(0), heads(level), ALU.mult).then_inc(lm, 1)
                        if n < LV - 1:
                            dve.wait_ge(lt, c * (LV - 1) + n + 1)
                            nc.vector.tensor_tensor(tu[:, 0], tu[:, 0], bank(2), ALU.add).then_inc(la, 1)
                        if n == 4:
                            softmax_max(c, 1)
                        if n == 5:
                            dve.wait_ge(S["st_up"], c)
                            nc.vector.tensor_tensor(faded[:], state[:], per_head("decay", c),
                                                    ALU.mult).then_inc(S["decayed"], 1)
                        dve.wait_ge(lu, c * LV + n + 1)
                        if n == 0:
                            dve.wait_ge(S["u1"], now)
                        nc.vector.tensor_tensor(tu[:, 1], tu[:, 1], bank(3), ALU.add).then_inc(lb, 1)
                        if n == 3:
                            softmax_scores(c, s, 1)
                    dve.wait_ge(S["ks"], now)
                    nc.vector.tensor_tensor(xs[:], bank(0), per_head("nbeg", c), ALU.mult).then_inc(S["kb"], 1)
                    dve.wait_ge(S["kb"], now)
                    nc.vector.tensor_tensor(vb[:], vb[:], xs[:], ALU.add).then_inc(S["r2"], 1)
                    dve.wait_ge(S["ods"], now)
                    dve.wait_ge(S["decayed"], now)
                    nc.vector.tensor_tensor(state[:], faded[:], bank(3), ALU.add).then_inc(S["st_up"], 1)
                    dve.wait_ge(S["osq"], now)
                    nc.vector.tensor_reduce(rms[:], og[:], AX, ALU.add).then_inc(S["osum"], 1)
                    nc.vector.tensor_tensor(mx[:, 3, :], mx[:, 3, :], mx[:, 2, :], ALU.add).then_inc(S["den"], 1)
                    dve.wait_ge(S["den"], now)
                    nc.vector.reciprocal(mx[:, 3, :], mx[:, 3, :]).then_inc(S["rec"], 1)
                    dve.wait_ge(S["orms"], now)
                    dve.wait_ge(tile_in[s][3], 16 * (i + 1))
                    for h in range(GH):
                        last = nc.vector.scalar_tensor_tensor(og[:, h, :], bank(2)[:, h, :], rms[:, h:h + 1],
                                                              zw[s][:, h, :], ALU.mult, ALU.mult)
                    last.then_inc(S["og"], 1)
                    dve.wait_ge(S["rec"], now)
                    dve.wait_ge(S["o_mm"], now)
                    nc.vector.tensor_tensor(on[:], psum[:, 4, :].rearrange("p (a d) -> p a d", a=AH),
                                            mx[:, 3, :].unsqueeze(2).broadcast_to([P, AH, AD]),
                                            ALU.mult).then_inc(S["o_n"], 1)
                    if before:
                        layer_norm(c - 1, i - 1 + s if not isinstance(c, int) else 0, 1 - s)

                tiles(dve, body)
                layer_norm(last_tile, NT // 2 - 1, last_tile % 2)

            @block.gpsimd
            def _(pool):
                pool.wait_ge(ln_in, 32)
                with pool.Fori(0, NT) as c:
                    pool.wait_ge(S["nrm"], c + 1)
                    nc.gpsimd.tensor_tensor(h1[:], h1[:], lng[:], ALU.mult).then_inc(S["nrm_g"], 1)
                    pool.wait_ge(S["nrm_g"], c + 1)
                    nc.gpsimd.tensor_tensor(h1[:], h1[:], lnb[:], ALU.add).then_inc(S["x1"], 1)


def split_x1(nc, sem, scr, cst, psum, x1h, x1l):
    with ExitStack() as ctx:
        xt = [ctx.enter_context(nc.sbuf_tensor(f"t_x{s}", [P, D], F32)) for s in range(2)]
        x_in = [sem(f"t_in{s}") for s in range(2)]
        tr = [sem(f"t_tr{s}") for s in range(2)]
        hi = [sem(f"t_hi{s}") for s in range(2)]
        lo = [sem(f"t_lo{s}") for s in range(2)]
        ps = [psum[:, 2 * s:2 * s + 2, :].rearrange("p b (k t) -> p (b k) t", t=P) for s in range(2)]
        with nc.Block() as block:
            @block.sync
            def _(sp):
                with sp.Fori(0, NT // 2) as i:
                    for s in range(2):
                        sp.wait_ge(tr[s], i)
                        sp.dma_start(xt[s][:], scr["x1"][ts((2 * i + s) * P, P), :]).then_inc(x_in[s], 16)

            @block.tensor
            def _(pe):
                with pe.Fori(0, NT // 2) as i:
                    for s in range(2):
                        pe.wait_ge(x_in[s], 16 * (i + 1))
                        pe.wait_ge(lo[s], i)
                        for k in range(KC):
                            last = nc.tensor.transpose(ps[s][:, k, :], xt[s][:, k * P:(k + 1) * P],
                                                       cst[:, C_ID:C_ID + P])
                        last.then_inc(tr[s], 1)

            @block.scalar
            def _(act):
                with act.Fori(0, NT // 2) as i:
                    for s in range(2):
                        act.wait_ge(tr[s], i + 1)
                        nc.scalar.activation(x1h[:, :, ts((2 * i + s) * P, P)], ps[s], ACT.Copy).then_inc(hi[s], 1)

            @block.vector
            def _(dve):
                with dve.Fori(0, NT // 2) as i:
                    for s in range(2):
                        dve.wait_ge(hi[s], i + 1)
                        nc.vector.tensor_tensor(x1l[:, :, ts((2 * i + s) * P, P)], ps[s],
                                                x1h[:, :, ts((2 * i + s) * P, P)].bitcast(F32),
                                                ALU.subtract).then_inc(lo[s], 1)


def retrieve(nc, sem, io, scr, cst, psum, x1h, x1l, key1, key2, gate):
    with ExitStack() as ctx:
        def sb(name, shape, dt=F32):
            return ctx.enter_context(nc.sbuf_tensor(name, shape, dt))

        wr = [sb(f"r_w{s}", [P, KC, P]) for s in range(2)]
        wh = [sb(f"r_wh{s}", [P, KC, P], F32R) for s in range(2)]
        wl = [sb(f"r_wl{s}", [P, KC, P], F32R) for s in range(2)]
        qT = [sb(f"r_qT{s}", [P, T]) for s in range(2)]
        kk = [sb(f"r_kk{s}", [P, NK]) for s in range(2)]
        sc = [sb(f"r_sc{s}", [P, NT, NK]) for s in range(2)]
        rest = sb("r_rest", [P, NT, NK])
        top = [sb(f"r_top{s}", [P, NT, TOPK]) for s in range(2)]
        idx = [sb(f"r_idx{s}", [P, NT, TOPK], U32) for s in range(2)]
        idf = [[sb(f"r_idf{v}{s}", [P, NT, TOPK]) for s in range(2)] for v in range(2)]
        cand = sb("r_cand", [P, NT, TOPK * TOPK])
        crest = sb("r_crest", [P, NT, TOPK * TOPK])
        best = sb("r_best", [P, NT, TOPK])
        ex = sb("r_ex", [P, NT, TOPK])
        pos = sb("r_pos", [P, NT, TOPK], U32)
        pab = [sb(f"r_pab{s}", [P, NT, TOPK], U32) for s in range(2)]
        pf = [[sb(f"r_pf{v}{s}", [P, NT, TOPK]) for s in range(2)] for v in range(2)]
        gsum = sb("r_gsum", [P, NT])
        pick = [sb(f"r_pick{s}", [P, NT, TOPK, TOPK]) for s in range(2)]
        ur = sb("r_ur", [P, KC, P])
        uh = [sb(f"r_uh{v}", [P, KC, P], F32R) for v in range(2)]
        ul = [sb(f"r_ul{v}", [P, KC, P], F32R) for v in range(2)]
        act_out = [sb(f"r_gelu{n}", [P, HALF]) for n in range(2)]
        q_ps = [psum[:, 2 * s:2 * s + 2, :] for s in range(2)]
        s_ps = psum[:, 4:6, :]

        tick = sem("r_tick")
        w_in = [sem(f"r_w_in{s}") for s in range(2)]
        w_hi = [sem(f"r_w_hi{s}") for s in range(2)]
        w_lo = [sem(f"r_w_lo{s}") for s in range(2)]
        q_mm = [sem(f"r_q_mm{s}") for s in range(2)]
        q_ev = [sem(f"r_q_ev{s}") for s in range(2)]
        s_mm = [sem(f"r_s_mm{s}") for s in range(2)]
        s_ev = [sem(f"r_s_ev{s}") for s in range(2)]
        u_in, u_hi, u_lo = sem("r_u_in"), sem("r_u_hi"), sem("r_u_lo")
        h_mm = [sem(f"r_h_mm{n}") for n in range(2)]
        gelu = [sem(f"r_gelu{n}") for n in range(2)]
        h_out = [sem(f"r_h_out{n}") for n in range(2)]
        kk_in = [sem(f"r_kk{s}") for s in range(2)]
        half_done = [sem(f"r_half{s}") for s in range(2)]
        mx1, mi1, mr, mx2 = sem("r_max1"), sem("r_index1"), sem("r_replace"), sem("r_max2")
        c_new, c1, c2, c3, c4, c5 = (sem(f"r_cand{n}") for n in range(6))
        g_sub, g_exp, g_sum, g_rec, g_out = (sem(f"r_gate{n}") for n in range(5))
        p_bits = sem("r_bits")
        p_ready = [sem(f"r_pos_ready{v}") for v in range(2)]
        pool_step = sem("r_pick_step")
        p_square = sem("r_pick_square")
        p_diff = [sem(f"r_pick_diff{s}") for s in range(2)]
        p_match = [sem(f"r_pick_match{s}") for s in range(2)]
        picked_all = [sem(f"r_picked{v}") for v in range(2)]

        with nc.Block() as block:
            @block.sync
            def _(sp):
                def load_u(b):
                    sp.wait_ge(u_lo, b)
                    sp.dma_start(ur[:], io["uT"][b]).then_inc(u_in, 16)

                def store_hidden(b):
                    for n in range(2):
                        sp.wait_ge(gelu[n], b + 1)
                        sp.dma_start(scr["hidden"][ts(b, 1), :, n * HALF:(n + 1) * HALF].rearrange("a p t -> (a p) t"),
                                     act_out[n][:]).then_inc(h_out[n], 16)

                def head(h):
                    for s in range(2):
                        sp.wait_ge(w_lo[s], h)
                        sp.dma_start(wr[s][:], io["wq"][2 * h + s]).then_inc(w_in[s], 16)
                    load_u(h)
                    for s in range(2):
                        sp.wait_ge(s_mm[s], h)
                        sp.dma_start(kk[s][:], io["keysT"][2 * h + s]).then_inc(kk_in[s], 16)

                head(0)
                with sp.Fori(1, PH) as h:
                    head(h)
                    store_hidden(h - 1)
                load_u(PH)
                store_hidden(PH - 1)
                for b in range(PH + 1, AHEAD_R):
                    load_u(b)
                    if b > PH + 1:
                        store_hidden(b - 2)
                for b in range(AHEAD_R - 2, AHEAD_R):
                    store_hidden(b)
                for n in range(2):
                    sp.wait_ge(h_out[n], 16 * AHEAD_R)

            @block.tensor
            def _(pe):
                def query(h, s):
                    pe.wait_ge(w_hi[s], h + 1)
                    pe.wait_ge(w_lo[s], h + 1)
                    pe.wait_ge(q_ev[s], h)
                    for n in range(2):
                        for k in range(KC):
                            c = slice(n * HALF, (n + 1) * HALF)
                            nc.tensor.matmul(q_ps[s][:, n, :], wh[s][:, k, :], x1h[:, k, c],
                                             start=(k == 0), stop=False)
                            nc.tensor.matmul(q_ps[s][:, n, :], wh[s][:, k, :], x1l[:, k, c],
                                             start=False, stop=False)
                            last = nc.tensor.matmul(q_ps[s][:, n, :], wl[s][:, k, :], x1h[:, k, c],
                                                    start=False, stop=(k == KC - 1))
                    last.then_inc(q_mm[s], 1)

                def hidden(b, v, n):
                    pe.wait_ge(u_hi, b + 1)
                    pe.wait_ge(u_lo, b + 1)
                    pe.wait_ge(gelu[n], b)
                    c = slice(n * HALF, (n + 1) * HALF)
                    for k in range(KC):
                        nc.tensor.matmul(psum[:, 6 + n, :], uh[v][:, k, :], x1h[:, k, c], start=(k == 0), stop=False)
                        nc.tensor.matmul(psum[:, 6 + n, :], uh[v][:, k, :], x1l[:, k, c], start=False, stop=False)
                        last = nc.tensor.matmul(psum[:, 6 + n, :], ul[v][:, k, :], x1h[:, k, c], start=False,
                                                stop=(k == KC - 1))
                    last.then_inc(h_mm[n], 1)

                def score(h, s):
                    pe.wait_ge(q_ev[s], h + 1)
                    pe.wait_ge(kk_in[s], 16 * (h + 1))
                    pe.wait_ge(s_ev[1 - s], h + s)
                    for t in range(NT):
                        last = nc.tensor.matmul(s_ps[:, t // 4, (t % 4) * P:(t % 4 + 1) * P],
                                                qT[s][:, t * P:(t + 1) * P], kk[s][:], start=True, stop=True)
                    last.then_inc(s_mm[s], 1)

                with pe.Fori(0, PH // 2) as i:
                    for v in range(2):
                        h = 2 * i + v
                        query(h, 0)
                        query(h, 1)
                        hidden(h, v, 0)
                        score(h, 0)
                        hidden(h, v, 1)
                        score(h, 1)
                for b in range(PH, AHEAD_R):
                    for n in range(2):
                        hidden(b, b % 2, n)

            @block.scalar
            def _(act):
                def weights(h):
                    for s in range(2):
                        act.wait_ge(w_in[s], 16 * (h + 1))
                        act.wait_ge(q_mm[s], h)
                        nc.scalar.activation(wh[s][:], wr[s][:], ACT.Copy).then_inc(w_hi[s], 1)

                def split_u(b, v):
                    act.wait_ge(u_in, 16 * (b + 1))
                    if not isinstance(b, int) or b >= 2:
                        act.wait_ge(h_mm[1], b - 1)
                    nc.scalar.activation(uh[v][:], ur[:], ACT.Copy).then_inc(u_hi, 1)

                def activate(b, n):
                    act.wait_ge(h_mm[n], b + 1)
                    act.wait_ge(h_out[n], 16 * b)
                    nc.scalar.activation(act_out[n][:], psum[:, 6 + n, :], ACT.Gelu).then_inc(gelu[n], 1)

                def scores(h, v, more=True):
                    for s in range(2):
                        act.wait_ge(q_mm[s], h + 1)
                        act.wait_ge(s_mm[s], h)
                        nc.scalar.activation(qT[s][:], q_ps[s].rearrange("p b t -> p (b t)"), ACT.Copy).then_inc(q_ev[s], 1)
                    if more:
                        weights(h + 1)
                    split_u(h + 1, 1 - v)
                    for s in range(2):
                        activate(h, s)
                        act.wait_ge(s_mm[s], h + 1)
                        act.wait_ge(half_done[s], h)
                        nc.scalar.activation(sc[s].rearrange("p t n -> p (t n)"),
                                             s_ps.rearrange("p b n -> p (b n)"), ACT.Copy).then_inc(s_ev[s], 1)

                def picks(h):
                    for s in range(2):
                        act.wait_ge(p_diff[s], h + 1)
                        nc.scalar.activation(pick[s][:], pick[s][:], ACT.Square).then_inc(p_square, 1)
                        act.wait_ge(p_square, 2 * h + s + 1)
                        nc.scalar.activation(pick[s][:], pick[s][:], ACT.Relu, scale=-1.0,
                                             bias=cst[:, C_ONES:C_ONES + 1]).then_inc(p_match[s], 1)

                def gates(h):
                    act.wait_ge(g_sub, h + 1)
                    nc.scalar.activation(ex[:], ex[:], ACT.Exp).then_inc(g_exp, 1)

                weights(0)
                split_u(0, 0)
                scores(0, 0)
                scores(1, 1)
                gates(0)

                def steady(h, v, more=True):
                    picks(h - 1)
                    scores(h + 1, v, more)
                    gates(h)

                with act.Fori(0, PH // 2 - 2) as i:
                    steady(2 * i + 1, 0)
                    steady(2 * i + 2, 1)
                steady(PH - 3, 0)
                steady(PH - 2, 1, more=False)
                split_u(PH + 1, 1)
                picks(PH - 2)
                for n in range(2):
                    activate(PH, n)
                split_u(PH + 2, 0)
                for n in range(2):
                    activate(PH + 1, n)
                gates(PH - 1)
                split_u(PH + 3, 1)
                for n in range(2):
                    activate(PH + 2, n)
                picks(PH - 1)
                for n in range(2):
                    activate(PH + 3, n)

            @block.vector
            def _(dve):
                def split_u(b, v):
                    dve.wait_ge(u_hi, b + 1)
                    nc.vector.tensor_tensor(ul[v][:], ur[:], uh[v][:].bitcast(F32), ALU.subtract).then_inc(u_lo, 1)

                with dve.Fori(0, PH // 2) as i:
                    for v in range(2):
                        h = 2 * i + v
                        split_u(h + 1, 1 - v)
                        for s in range(2):
                            n = 2 * h + s
                            wait_apart(dve, tick, s_ev[s], h + 1)
                            for t in range(NT):
                                last = nc.vector.max(top[s][:, t, 0:8], sc[s][:, t, :])
                            last.then_inc(mx1, 1)
                            wait_apart(dve, tick, mx1, n + 1)
                            for t in range(NT):
                                last = nc.vector.match_replace(rest[:, t, :], top[s][:, t, 0:8], sc[s][:, t, :], REPLACED)
                            last.then_inc(mr, 1)
                            for t in range(NT):
                                last = nc.vector.max_index(idx[s][:, t, 0:8], top[s][:, t, 0:8], sc[s][:, t, :])
                            last.then_inc(half_done[s], 1)
                            wait_apart(dve, tick, mr, n + 1)
                            for t in range(NT):
                                last = nc.vector.max(top[s][:, t, 8:16], rest[:, t, :])
                            last.then_inc(mx2, 1)
                            wait_apart(dve, tick, mx2, n + 1)
                            for t in range(NT):
                                last = nc.vector.max_index(idx[s][:, t, 8:16], top[s][:, t, 8:16], rest[:, t, :])
                            last.then_inc(mi1, 1)
                        dve.wait_ge(mi1, 2 * h + 2)
                        dve.wait_ge(picked_all[v], i)
                        for s in range(2):
                            nc.vector.tensor_copy(idf[v][s][:], idx[s][:])
                        nc.vector.tensor_tensor(cand.rearrange("p t (a b) -> p t a b", a=TOPK),
                                                top[0][:, :, :].unsqueeze(3).broadcast_to([P, NT, TOPK, TOPK]),
                                                top[1][:, :, :].unsqueeze(2).broadcast_to([P, NT, TOPK, TOPK]),
                                                ALU.add).then_inc(c_new, 1)
                        dve.wait_ge(c_new, h + 1)
                        wait_apart(dve, tick, g_out, h)
                        for t in range(NT):
                            last = nc.vector.max(best[:, t, 0:8], cand[:, t, :])
                        last.then_inc(c1, 1)
                        wait_apart(dve, tick, c1, h + 1)
                        for t in range(NT):
                            last = nc.vector.match_replace(crest[:, t, :], best[:, t, 0:8], cand[:, t, :], REPLACED)
                        last.then_inc(c2, 1)
                        for t in range(NT):
                            nc.vector.max_index(pos[:, t, 0:8], best[:, t, 0:8], cand[:, t, :])
                        wait_apart(dve, tick, c2, h + 1)
                        for t in range(NT):
                            last = nc.vector.max(best[:, t, 8:16], crest[:, t, :])
                        last.then_inc(c3, 1)
                        wait_apart(dve, tick, c3, h + 1)
                        for t in range(NT):
                            last = nc.vector.max_index(pos[:, t, 8:16], best[:, t, 8:16], crest[:, t, :])
                        last.then_inc(c4, 1)
                        dve.wait_ge(c4, h + 1)
                        nc.vector.tensor_scalar(pab[0][:], pos[:], 4, None, ALU.logical_shift_right)
                        nc.vector.tensor_scalar(pab[1][:], pos[:], 15, None, ALU.bitwise_and).then_inc(p_bits, 1)
                        nc.vector.tensor_tensor(ex[:], best[:], best[:, :, 0:1].broadcast_to([P, NT, TOPK]),
                                                ALU.subtract).then_inc(g_sub, 1)
                        dve.wait_ge(p_bits, h + 1)
                        nc.vector.tensor_copy(pf[v][0][:], pab[0][:])
                        nc.vector.tensor_copy(pf[v][1][:], pab[1][:]).then_inc(p_ready[v], 1)
                        dve.wait_ge(g_exp, h + 1)
                        nc.vector.tensor_reduce(gsum[:], ex[:], AX, ALU.add).then_inc(g_sum, 1)
                        dve.wait_ge(g_sum, h + 1)
                        nc.vector.reciprocal(gsum[:], gsum[:]).then_inc(g_rec, 1)
                        dve.wait_ge(g_rec, h + 1)
                        nc.vector.tensor_tensor(gate[:, :, ts(h * TOPK, TOPK)], ex[:],
                                                gsum[:, :].unsqueeze(2).broadcast_to([P, NT, TOPK]),
                                                ALU.mult).then_inc(g_out, 1)
                split_u(AHEAD_R - 1, 1)

            @block.gpsimd
            def _(pool):
                def weights(h):
                    for s in range(2):
                        pool.wait_ge(w_hi[s], h + 1)
                        nc.gpsimd.tensor_tensor(wl[s][:], wr[s][:], wh[s][:].bitcast(F32), ALU.subtract).then_inc(w_lo[s], 1)

                def split_u(b, v):
                    pool.wait_ge(u_hi, b + 1)
                    nc.gpsimd.tensor_tensor(ul[v][:], ur[:], uh[v][:].bitcast(F32), ALU.subtract).then_inc(u_lo, 1)

                def picks(h, v, i):
                    ranks = cst[:, C_IOTA16:C_IOTA16 + TOPK].unsqueeze(1).broadcast_to([P, NT * TOPK, TOPK])
                    pool.wait_ge(p_ready[v], i + 1)
                    pool.wait_ge(pool_step, 10 * h)
                    for s in range(2):
                        nc.gpsimd.tensor_tensor(
                            pick[s].rearrange("p t k j -> p (t k) j"),
                            pf[v][s].rearrange("p t k -> p (t k)").unsqueeze(2).broadcast_to([P, NT * TOPK, TOPK]),
                            ranks, ALU.subtract).then_inc(p_diff[s], 1)
                    for s, dst in enumerate((key1, key2)):
                        n = 10 * h + 5 * s
                        flat = pick[s].rearrange("p t k j -> p (t k) j")
                        pool.wait_ge(p_match[s], h + 1)
                        nc.gpsimd.tensor_tensor(pick[s][:], pick[s][:],
                                                idf[v][s][:, :, :].unsqueeze(2).broadcast_to([P, NT, TOPK, TOPK]),
                                                ALU.mult).then_inc(pool_step, 1)
                        pool.wait_ge(pool_step, n + 1)
                        for step, m in enumerate((8, 4, 2)):
                            nc.gpsimd.tensor_tensor(flat[:, :, 0:m], flat[:, :, 0:m], flat[:, :, m:2 * m],
                                                    ALU.add).then_inc(pool_step, 1)
                            pool.wait_ge(pool_step, n + 2 + step)
                        nc.gpsimd.tensor_tensor(dst[:, :, ts(h * TOPK, TOPK)], pick[s][:, :, :, 0],
                                                pick[s][:, :, :, 1], ALU.add).then_inc(pool_step, 1)
                    pool.wait_ge(pool_step, 10 * (h + 1))
                    pool.sem_inc(picked_all[v], 1)

                weights(0)
                split_u(0, 0)
                weights(1)
                with pool.Fori(0, PH // 2 - 1) as i:
                    for v in range(2):
                        weights(2 * i + v + 2)
                        picks(2 * i + v, v, i)
                split_u(PH + 1, 1)
                picks(PH - 2, 0, PH // 2 - 1)
                split_u(PH + 2, 0)
                picks(PH - 1, 1, PH // 2 - 1)


def build_gates(nc, sem, io, scr, cst, psum, x1h, x1l, key1, key2, gate):
    with ExitStack() as ctx:
        def sb(name, shape, dt=F32):
            return ctx.enter_context(nc.sbuf_tensor(name, shape, dt))

        R = 16
        pickT = sb("g_pickT", [P, 3, T])
        one1 = [sb(f"g_one{s}", [P, R, NK]) for s in range(2)]
        one2 = [sb(f"g_two{s}", [P, R, NK]) for s in range(2)]
        gt = [sb(f"g_tile{s}", [P, NK, TG]) for s in range(2)]
        iota = cst[:, C_IOTA:C_IOTA + NK].unsqueeze(1).broadcast_to([P, R, NK])
        ur = sb("g_ur", [P, KC, P])
        uh = sb("g_uh", [P, KC, P], F32R)
        ul = sb("g_ul", [P, KC, P], F32R)
        act_out = [sb(f"g_gelu{n}", [P, HALF]) for n in range(2)]
        u_in, u_hi, u_lo = sem("g_u_in"), sem("g_u_hi"), sem("g_u_lo")
        h_mm = [sem(f"g_h_mm{n}") for n in range(2)]
        gelu = [sem(f"g_gelu{n}") for n in range(2)]
        h_out = [sem(f"g_h_out{n}") for n in range(2)]
        PAIRS = 2 * TG // (2 * R)
        tr, tr_ev = sem("g_tr"), sem("g_tr_ev")
        hot1 = [sem(f"g_hot1{s}") for s in range(2)]
        hot2 = [sem(f"g_hot2{s}") for s in range(2)]
        gated = [sem(f"g_gated{s}") for s in range(2)]
        mm = [sem(f"g_mm{s}") for s in range(2)]
        evac = [sem(f"g_evac{n}") for n in range(4)]
        stored = [sem(f"g_stored{s}") for s in range(2)]

        def picks_of(n, t):
            return pickT[:, n, ts(t, R)].unsqueeze(2).broadcast_to([P, R, NK])

        with nc.Block() as block:
            @block.tensor
            def _(pe):
                for t in range(NT):
                    if t >= 2:
                        pe.wait_ge(tr_ev, t - 1)
                    for n, src in enumerate((key1, key2, gate)):
                        last = nc.tensor.transpose(psum[:, t % 2, n * P:(n + 1) * P], src[:, t, :], cst[:, C_ID:C_ID + P])
                    last.then_inc(tr, 1)
                pe.wait_ge(tr_ev, NT)
                with pe.Fori(0, AHEAD_G) as i:
                    for r in range(PAIRS):
                        for s in range(2):
                            pair = PAIRS * i + r
                            pe.wait_ge(hot1[s], pair + 1)
                            pe.wait_ge(gated[s], pair + 1)
                            for n in range(R):
                                if n % 4 == 0:
                                    pe.wait_ge(evac[n // 4], 2 * pair + s)
                                last = nc.tensor.matmul(psum[:, n // 4, (n % 4) * NK:(n % 4 + 1) * NK],
                                                        one2[s][:, n, :], one1[s][:, n, :], start=True, stop=True)
                                if n % 4 == 3:
                                    last.then_inc(mm[s], 1)
                        n, first = r // 2, r % 2 * (KC // 2)
                        if r == 0:
                            pe.wait_ge(u_hi, i + 1)
                            pe.wait_ge(u_lo, i + 1)
                        if first == 0:
                            pe.wait_ge(gelu[n], i)
                        c = slice(n * HALF, (n + 1) * HALF)
                        for k in range(first, first + KC // 2):
                            nc.tensor.matmul(psum[:, 6 + n, :], uh[:, k, :], x1h[:, k, c], start=(k == 0), stop=False)
                            nc.tensor.matmul(psum[:, 6 + n, :], uh[:, k, :], x1l[:, k, c], start=False, stop=False)
                            last = nc.tensor.matmul(psum[:, 6 + n, :], ul[:, k, :], x1h[:, k, c], start=False,
                                                    stop=(k == KC - 1))
                        if first:
                            last.then_inc(h_mm[n], 1)

            @block.vector
            def _(dve):
                dve.wait_ge(tr_ev, NT)
                with dve.Fori(0, T // R // 2) as i:
                    for s in range(2):
                        t = (2 * i + s) * R
                        dve.wait_ge(mm[s], 4 * i)
                        nc.vector.tensor_tensor(one2[s][:], iota, picks_of(1, t), ALU.is_equal).then_inc(hot2[s], 1)
                        nc.vector.tensor_tensor(one1[s][:], iota, picks_of(0, t), ALU.is_equal).then_inc(hot1[s], 1)

            @block.gpsimd
            def _(pool):
                with pool.Fori(0, AHEAD_G) as i:
                    for r in range(PAIRS):
                        for s in range(2):
                            pair = PAIRS * i + r
                            pool.wait_ge(hot2[s], pair + 1)
                            nc.gpsimd.tensor_tensor(one2[s][:], one2[s][:], picks_of(2, (2 * pair + s) * R),
                                                    ALU.mult).then_inc(gated[s], 1)
                        if r == 0:
                            pool.wait_ge(u_hi, i + 1)
                            nc.gpsimd.tensor_tensor(ul[:], ur[:], uh[:].bitcast(F32), ALU.subtract).then_inc(u_lo, 1)

            @block.scalar
            def _(act):
                for t in range(NT):
                    act.wait_ge(tr, t + 1)
                    nc.scalar.activation(pickT[:, :, t * P:(t + 1) * P],
                                         psum[:, t % 2, 0:3 * P].rearrange("p (n t) -> p n t", n=3),
                                         ACT.Copy).then_inc(tr_ev, 1)
                with act.Fori(0, T // TG // 2) as i:
                    act.wait_ge(u_in, 16 * (i + 1))
                    act.wait_ge(h_mm[1], i)
                    nc.scalar.activation(uh[:], ur[:], ACT.Copy).then_inc(u_hi, 1)
                    for b in range(2):
                        act.wait_ge(stored[b], 16 * i)
                        for r in range(TG // R):
                            s = r % 2
                            for n in range(4):
                                act.wait_ge(mm[s], ((2 * i + b) * (TG // R // 2) + r // 2) * 4 + n + 1)
                                nc.scalar.activation(gt[b][:, :, r * R + 4 * n:r * R + 4 * n + 4].rearrange("p k t -> p t k"),
                                                     psum[:, n, :].rearrange("p (t k) -> p t k", t=4),
                                                     ACT.Copy).then_inc(evac[n], 1)
                        act.wait_ge(h_mm[b], i + 1)
                        act.wait_ge(h_out[b], 16 * i)
                        nc.scalar.activation(act_out[b][:], psum[:, 6 + b, :], ACT.Gelu).then_inc(gelu[b], 1)

            @block.sync
            def _(sp):
                def stores(i, more):
                    if more:
                        sp.wait_ge(u_lo, i + 1)
                        sp.dma_start(ur[:], io["uT"][i + (AHEAD_R + 1)]).then_inc(u_in, 16)
                    for b in range(2):
                        sp.wait_ge(evac[3], (2 * i + b + 1) * (TG // R))
                        sp.dma_start(scr["G"][ts(2 * i + b, 1)].rearrange("a p k t -> (a p) k t"),
                                     gt[b][:]).then_inc(stored[b], 16)
                        sp.wait_ge(gelu[b], i + 1)
                        sp.dma_start(scr["hidden"][ts(i + AHEAD_R, 1), :, b * HALF:(b + 1) * HALF]
                                     .rearrange("a p t -> (a p) t"), act_out[b][:]).then_inc(h_out[b], 16)

                sp.dma_start(ur[:], io["uT"][AHEAD_R]).then_inc(u_in, 16)
                with sp.Fori(0, AHEAD_G - 1) as i:
                    stores(i, True)
                stores(AHEAD_G - 1, False)
                for b in range(2):
                    sp.wait_ge(stored[b], 16 * (T // TG // 2))
                    sp.wait_ge(h_out[b], 16 * AHEAD_G)


def experts(nc, sem, io, scr, psum, x1h, x1l, y):
    with ExitStack() as ctx:
        def sb(name, shape, dt=F32):
            return ctx.enter_context(nc.sbuf_tensor(name, shape, dt))

        NG = NK // 2
        SHORT = AHEAD // 2
        ur = [sb(f"e_ur{j}", [P, KC, P]) for j in range(2)]
        vr = sb("e_vr", [P, D])
        uh = [sb(f"e_uh{j}", [P, KC, P], F32R) for j in range(2)]
        ul = [sb(f"e_ul{j}", [P, KC, P], F32R) for j in range(2)]
        vh = [[sb(f"e_vh{s}{j}", [P, D], F32R) for j in range(2)] for s in range(2)]
        vl = [[sb(f"e_vl{s}{j}", [P, D], F32R) for j in range(2)] for s in range(2)]
        ah = [[sb(f"e_ah{s}{j}", [P, T], F32R) for j in range(2)] for s in range(2)]
        al = [[sb(f"e_al{s}{j}", [P, T], F32R) for j in range(2)] for s in range(2)]
        gt = [sb(f"e_g{j}", [P, T // TG, TG]) for j in range(2)]
        av = [sb(f"e_a{n}", [P, HALF]) for n in range(2)]

        u_in = [sem(f"u_in{j}") for j in range(2)]
        v_in = [sem(f"v_in{j}") for j in range(2)]
        g_in = [sem(f"g_in{j}") for j in range(2)]
        u_hi = [sem(f"u_hi{j}") for j in range(2)]
        u_lo = [sem(f"u_lo{j}") for j in range(2)]
        v_hi = [sem(f"v_hi{j}") for j in range(2)]
        v_lo = [sem(f"v_lo{j}") for j in range(2)]
        h_mm = [[sem(f"h_mm{j}{n}") for n in range(2)] for j in range(2)]
        gelu = [[sem(f"gelu{j}{n}") for n in range(2)] for j in range(2)]
        a_mul = [[sem(f"a_mul{j}{n}") for n in range(2)] for j in range(2)]
        a_hi = [[sem(f"a_hi{j}{n}") for n in range(2)] for j in range(2)]
        a_lo = [[sem(f"a_lo{j}{n}") for n in range(2)] for j in range(2)]
        y_mm = sem("y_mm")
        y_add = [sem(f"y_add{b}") for b in range(4)]
        x1_in = sem("x1_in")
        y_ready = sem("y_ready")

        with nc.Block() as block:
            @block.sync
            def _(sp):
                def load_v(g, j):
                    sp.wait_ge(v_lo[1 - j], g + j)
                    sp.dma_start(vr[:], io["v"][ts((2 * g + j) * NK, NK), :]).then_inc(v_in[j], 16)

                def load_gates(g, j):
                    sp.wait_ge(a_mul[j][1], g)
                    sp.dma_start(gt[j][:], scr["G"][:, :, 2 * g + j, :].rearrange("t p q -> p t q")).then_inc(g_in[j], 16)

                def short_group(g):
                    for j in range(2):
                        load_gates(g, j)
                        sp.dma_start(ur[j].rearrange("p k e -> p (k e)"),
                                     scr["hidden"][2 * g + j]).then_inc(u_in[j], 16)
                    for j in range(2):
                        load_v(g, j)
                short_group(0)
                for t in range(NT):
                    sp.dma_start(y[:, t, :], scr["x1"][t * P:(t + 1) * P, :]).then_inc(x1_in, 16)
                with sp.Fori(1, SHORT) as g:
                    short_group(g)
                with sp.Fori(SHORT, NG) as g:
                    for j in range(2):
                        sp.wait_ge(u_lo[j], g - SHORT)
                        sp.wait_ge(a_mul[j][1], SHORT)
                        sp.dma_start(ur[j][:], io["uT"][2 * g + j]).then_inc(u_in[j], 16)
                        load_v(g, j)
                        load_gates(g, j)

            @block.tensor
            def _(pe):
                def hidden(g):
                    for j in range(2):
                        pe.wait_ge(u_hi[j], g - SHORT + 1)
                        pe.wait_ge(u_lo[j], g - SHORT + 1)
                        for n in range(2):
                            pe.wait_ge(gelu[j][n], g - SHORT)
                            out = psum[:, 2 * j + n, :]
                            c = slice(n * HALF, (n + 1) * HALF)
                            for k in range(KC):
                                nc.tensor.matmul(out, uh[j][:, k, :], x1h[:, k, c], start=(k == 0), stop=False)
                                nc.tensor.matmul(out, uh[j][:, k, :], x1l[:, k, c], start=False, stop=False)
                                last = nc.tensor.matmul(out, ul[j][:, k, :], x1h[:, k, c], start=False,
                                                        stop=(k == KC - 1))
                            last.then_inc(h_mm[j][n], 1)

                def values(g, s):
                    for j in range(2):
                        pe.wait_ge(v_hi[j], g + 1)
                        pe.wait_ge(v_lo[j], g + 1)
                        for n in range(2):
                            pe.wait_ge(a_lo[j][n], g + 1)
                    for q in range(2 * NT):
                        t, n = divmod(q, 2)
                        pe.wait_ge(y_add[q % 4], 4 * g + q // 4)
                        out = psum[:, 4 + q % 4, :]
                        c = slice(n * HALF, (n + 1) * HALF)
                        r = slice(t * P, (t + 1) * P)
                        for j in range(2):
                            nc.tensor.matmul(out, ah[s][j][:, r], vh[s][j][:, c], start=(j == 0), stop=False)
                            nc.tensor.matmul(out, ah[s][j][:, r], vl[s][j][:, c], start=False, stop=False)
                            last = nc.tensor.matmul(out, al[s][j][:, r], vh[s][j][:, c], start=False, stop=(j == 1))
                        last.then_inc(y_mm, 1)

                with pe.Fori(0, SHORT // 2) as i:
                    values(2 * i, 0)
                    values(2 * i + 1, 1)
                hidden(SHORT)
                with pe.Fori(SHORT // 2, (NG - 2) // 2) as i:
                    hidden(2 * i + 1)
                    values(2 * i, 0)
                    hidden(2 * i + 2)
                    values(2 * i + 1, 1)
                hidden(NG - 1)
                values(NG - 2, 0)
                values(NG - 1, 1)

            @block.scalar
            def _(act):
                def split_u(g, j):
                    act.wait_ge(u_in[j], 16 * (g + 1))
                    act.wait_ge(h_mm[j][1], g - SHORT)
                    nc.scalar.activation(uh[j][:], ur[j][:], ACT.Copy).then_inc(u_hi[j], 1)

                def split_v(g, s, j, used):
                    act.wait_ge(v_in[j], 16 * (g + 1))
                    act.wait_ge(y_mm, used)
                    nc.scalar.activation(vh[s][j][:], vr[:], ACT.Copy).then_inc(v_hi[j], 1)

                def split_a(g, s, j, used):
                    act.wait_ge(y_mm, used)
                    for n in range(2):
                        act.wait_ge(a_mul[j][n], g + 1)
                        nc.scalar.activation(ah[s][j][:, n * HALF:(n + 1) * HALF], av[n][:], ACT.Copy).then_inc(a_hi[j][n], 1)

                def activate(g, j):
                    for n in range(2):
                        act.wait_ge(h_mm[j][n], g - SHORT + 1)
                        if j == 1:
                            act.wait_ge(a_lo[0][n], g + 1)
                        else:
                            act.wait_ge(a_lo[1][n], g)
                        nc.scalar.activation(av[n][:], psum[:, 2 * j + n, :], ACT.Gelu).then_inc(gelu[j][n], 1)

                def short_group(g, s, used):
                    for j in range(2):
                        split_a(g, s, j, used)
                    for j in range(2):
                        split_v(g, s, j, used)

                def group(g, s, used, used_next, more=True):
                    for j in range(2):
                        activate(g, j)
                        split_a(g, s, j, used)
                        if more:
                            split_u(g + 1, j)
                    if more:
                        for j in range(2):
                            split_v(g + 1, 1 - s, j, used_next)

                short_group(0, 0, 0)
                with act.Fori(0, SHORT // 2 - 1) as i:
                    short_group(2 * i + 1, 1, 32 * i)
                    short_group(2 * i + 2, 0, 32 * i + 16)
                short_group(SHORT - 1, 1, 16 * (SHORT - 2))
                for j in range(2):
                    split_u(SHORT, j)
                for j in range(2):
                    split_v(SHORT, 0, j, 16 * (SHORT - 1))
                group(SHORT, 0, 16 * (SHORT - 1), 16 * SHORT)
                with act.Fori(SHORT // 2, (NG - 2) // 2) as i:
                    group(2 * i + 1, 1, 32 * i, 32 * i + 16)
                    group(2 * i + 2, 0, 32 * i + 16, 32 * i + 32)
                group(NG - 1, 1, 16 * (NG - 2), 0, more=False)

            @block.vector
            def _(dve):
                def split_u(g, j):
                    dve.wait_ge(u_hi[j], g - SHORT + 1)
                    nc.vector.tensor_tensor(ul[j][:], ur[j][:], uh[j][:].bitcast(F32), ALU.subtract).then_inc(u_lo[j], 1)

                def split_v(g, s, j):
                    dve.wait_ge(v_hi[j], g + 1)
                    nc.vector.tensor_tensor(vl[s][j][:], vr[:], vh[s][j][:].bitcast(F32),
                                            ALU.subtract).then_inc(v_lo[j], 1)

                def weigh(g, s, j, short=True):
                    dve.wait_ge(g_in[j], 16 * (g + 1))
                    if short:
                        dve.wait_ge(u_in[j], 16 * (g + 1))
                    for n in range(2):
                        if short:
                            dve.wait_ge(a_lo[1 - j][n], g + j)
                            src = ur[j].rearrange("p k e -> p (k e)")[:, n * HALF:(n + 1) * HALF]
                        else:
                            dve.wait_ge(gelu[j][n], g - SHORT + 1)
                            src = av[n][:]
                        nc.vector.tensor_tensor(av[n][:], src,
                                                gt[j][:, n * HALF // TG:(n + 1) * HALF // TG, :].rearrange("p t q -> p (t q)"),
                                                ALU.mult).then_inc(a_mul[j][n], 1)
                    for n in range(2):
                        dve.wait_ge(a_hi[j][n], g + 1)
                        c = slice(n * HALF, (n + 1) * HALF)
                        nc.vector.tensor_tensor(al[s][j][:, c], av[n][:], ah[s][j][:, c].bitcast(F32),
                                                ALU.subtract).then_inc(a_lo[j][n], 1)

                def gather(g, q0, q1, first=False):
                    for q in range(q0, q1):
                        t, n = divmod(q, 2)
                        c = slice(n * HALF, (n + 1) * HALF)
                        dve.wait_ge(y_mm, 16 * g + q + 1)
                        if first:
                            dve.wait_ge(y_ready, t + 1)
                        nc.vector.tensor_tensor(y[:, t, c], y[:, t, c], psum[:, 4 + q % 4, :], ALU.add).then_inc(y_add[q % 4], 1)

                def short_group(g, s, before=True, first=False):
                    for n, prepare in enumerate((weigh, weigh, split_v, split_v)):
                        prepare(g, s, n % 2)
                        if before:
                            gather(g - 1, 4 * n, 4 * n + 4, first)

                def group(g, s, more=True, before=True):
                    weigh(g, s, 0, short=False)
                    if more:
                        split_u(g + 1, 0)
                    weigh(g, s, 1, short=False)
                    if before:
                        gather(g - 1, 0, 4)
                    if more:
                        split_u(g + 1, 1)
                    if before:
                        gather(g - 1, 4, 2 * NT)
                    if more:
                        for j in range(2):
                            split_v(g + 1, 1 - s, j)

                short_group(0, 0, before=False)
                short_group(1, 1, first=True)
                short_group(2, 0)
                with dve.Fori(1, SHORT // 2 - 1) as i:
                    short_group(2 * i + 1, 1)
                    short_group(2 * i + 2, 0)
                short_group(SHORT - 1, 1)
                for j in range(2):
                    split_u(SHORT, j)
                gather(SHORT - 1, 0, 4)
                for j in range(2):
                    split_v(SHORT, 0, j)
                gather(SHORT - 1, 4, 2 * NT)
                group(SHORT, 0, before=False)
                with dve.Fori(SHORT // 2, (NG - 2) // 2) as i:
                    group(2 * i + 1, 1)
                    group(2 * i + 2, 0)
                group(NG - 1, 1, more=False)
                gather(NG - 1, 0, 2 * NT)

            @block.gpsimd
            def _(pool):
                pool.wait_ge(x1_in, 16 * NT)
                for t in range(NT):
                    nc.gpsimd.tensor_scalar(y[:, t, :], y[:, t, :], ALPHA, None, ALU.mult).then_inc(y_ready, 1)


def finish(nc, sem, io, cst, y, out):
    with ExitStack() as ctx:
        def sb(name, shape, dt=F32):
            return ctx.enter_context(nc.sbuf_tensor(name, shape, dt))

        lng = sb("f_g", [P, D])
        lnb = sb("f_b", [P, D])
        st = sb("f_st", [P, NT, 2, 6])
        mv = sb("f_mv", [P, NT, 2])
        rstd = sb("f_rstd", [P, NT])
        shift = sb("f_shift", [P, NT])
        side = sem("f_side")
        stored = sem("f_stored")
        stat, aggr, log, root, shifted, nrm, nrm_g, done = (
            sem(f"f_{n}") for n in "stat aggr log root shifted nrm nrm_g done".split())
        with nc.Block() as block:
            @block.sync
            def _(sp):
                sp.dma_start(lng[:], io["ln2_g"].partition_broadcast(P)).then_inc(side, 16)
                sp.dma_start(lnb[:], io["ln2_b"].partition_broadcast(P)).then_inc(side, 16)
                for t in range(NT):
                    sp.wait_ge(done, t + 1)
                    sp.dma_start(out[0, t * P:(t + 1) * P, :], y[:, t, :]).then_inc(stored, 16)
                sp.wait_ge(stored, 16 * NT)

            @block.scalar
            def _(act):
                def root_of(t):
                    act.wait_ge(aggr, t + 1)
                    nc.scalar.activation(rstd[:, t:t + 1], mv[:, t, 1:2], ACT.Ln, bias=cst[:, C_EPS:C_EPS + 1]).then_inc(log, 1)
                    act.wait_ge(log, t + 1)
                    nc.scalar.activation(rstd[:, t:t + 1], rstd[:, t:t + 1], ACT.Exp, scale=-0.5).then_inc(root, 1)

                def normalize(t):
                    act.wait_ge(root, t + 1)
                    act.wait_ge(shifted, t + 1)
                    nc.scalar.activation(y[:, t, :], y[:, t, :], ACT.Identity, scale=rstd[:, t:t + 1],
                                         bias=shift[:, t:t + 1]).then_inc(nrm, 1)

                root_of(0)
                for t in range(NT):
                    if t + 1 < NT:
                        root_of(t + 1)
                    normalize(t)

            @block.vector
            def _(dve):
                def statistics(t):
                    for n in range(2):
                        nc.vector.bn_stats(st[:, t, n, :], y[:, t, n * HALF:(n + 1) * HALF]).then_inc(stat, 1)
                    dve.wait_ge(stat, 2 * (t + 1))
                    nc.vector.bn_aggr(mv[:, t, :], st[:, t]).then_inc(aggr, 1)

                def shift_of(t):
                    dve.wait_ge(aggr, t + 1)
                    dve.wait_ge(root, t + 1)
                    nc.vector.scalar_tensor_tensor(shift[:, t:t + 1], mv[:, t, 0:1], -1.0, rstd[:, t:t + 1],
                                                   ALU.mult, ALU.mult).then_inc(shifted, 1)

                def weight(t):
                    dve.wait_ge(nrm, t + 1)
                    nc.vector.tensor_tensor(y[:, t, :], y[:, t, :], lng[:], ALU.mult).then_inc(nrm_g, 1)

                statistics(0)
                statistics(1)
                shift_of(0)
                dve.wait_ge(side, 32)
                for t in range(NT):
                    if t + 2 < NT:
                        statistics(t + 2)
                    if t + 1 < NT:
                        shift_of(t + 1)
                    weight(t)

            @block.gpsimd
            def _(pool):
                pool.wait_ge(side, 32)
                for t in range(NT):
                    pool.wait_ge(nrm_g, t + 1)
                    nc.gpsimd.tensor_tensor(y[:, t, :], y[:, t, :], lnb[:], ALU.add).then_inc(done, 1)


def build(nc, io, out):
    with ExitStack() as ctx:
        scr = {
            "ch": nc.dram_tensor("s_ch", (N_CH, P, T), F32).ap(),
            "sk": nc.dram_tensor("s_sk", (P, P + T), F32).ap(),
            "sv": nc.dram_tensor("s_sv", (P + T, P), F32).ap(),
            "z": nc.dram_tensor("s_z", (T, GH * P), F32).ap(),
            "x1": nc.dram_tensor("s_x1", (T, D), F32).ap(),
            "hidden": nc.dram_tensor("s_hidden", (AHEAD, P, T), F32).ap(),
            "G": nc.dram_tensor("s_G", (T // TG, P, NK, TG), F32).ap(),
        }
        psum = ctx.enter_context(nc.psum_tensor("psum", [P, 8, HALF], F32))
        cst = ctx.enter_context(nc.sbuf_tensor("cst", [P, C_N], F32))
        cst_in = ctx.enter_context(nc.semaphore("cst_in"))
        with nc.Block() as block:
            @block.sync
            def _(sp):
                sp.dma_start(cst[:], io["consts"]).then_inc(cst_in, 16)
                sp.wait_ge(cst_in, 16)
        with ExitStack() as mixer:
            ba = mixer.enter_context(nc.sbuf_tensor("ba", [P, NT, 2 * GH], F32))
            with stage_semaphores(nc) as sem:
                project(nc, sem, io, scr, ba, cst, psum)
            with stage_semaphores(nc) as sem:
                mix_tokens(nc, sem, io, scr, ba, cst, psum)
        x1h = ctx.enter_context(nc.sbuf_tensor("x1h", [P, KC, T], F32R))
        x1l = ctx.enter_context(nc.sbuf_tensor("x1l", [P, KC, T], F32R))
        with stage_semaphores(nc) as sem:
            split_x1(nc, sem, scr, cst, psum, x1h, x1l)
        with ExitStack() as picks:
            key1, key2, gate = (picks.enter_context(nc.sbuf_tensor(n, [P, NT, PH * TOPK], F32))
                                for n in ("key1", "key2", "gate"))
            with stage_semaphores(nc) as sem:
                retrieve(nc, sem, io, scr, cst, psum, x1h, x1l, key1, key2, gate)
            with stage_semaphores(nc) as sem:
                build_gates(nc, sem, io, scr, cst, psum, x1h, x1l, key1, key2, gate)
        with ExitStack() as sums:
            y = sums.enter_context(nc.sbuf_tensor("y", [P, NT, D], F32))
            with stage_semaphores(nc) as sem:
                experts(nc, sem, io, scr, psum, x1h, x1l, y)
            with stage_semaphores(nc) as sem:
                finish(nc, sem, io, cst, y, out)


def layout(inputs):
    a = {k: np.asarray(v) for k, v in inputs.items()}

    def blocks(w):
        return np.ascontiguousarray(w.reshape(KC, P, -1, P).transpose(2, 1, 0, 3))

    def rows(w):
        return np.ascontiguousarray(w.reshape(KC, P, -1).transpose(1, 0, 2))

    w = a["w_in"][0]
    q0 = 4 * GH * P + 2 * GH
    k0, v0 = q0 + AH * AD, q0 + AH * AD + 2 * AD
    order = np.concatenate([np.arange(AD) + (r * 4 + p) * AD for p in range(4) for r in range(2)])
    channels = np.concatenate([w[:, 0:3 * GH * P], w[:, q0 + order], w[:, k0:v0]], axis=1)
    keys = np.stack([a["peer_k1"][0], a["peer_k2"][0]], axis=1).transpose(0, 1, 3, 2).reshape(2 * PH, P, NK)
    return {
        "x": a["x"][0], "xT": np.ascontiguousarray(a["x"][0].T), "w_ch": blocks(channels),
        "w_tok": rows(np.concatenate([w[:, 3 * GH * P:4 * GH * P], w[:, v0:], w[:, 4 * GH * P:q0]], axis=1)),
        "conv_w": np.ascontiguousarray(a["gdn_conv_w"][0].reshape(4, N_CONV, P).transpose(2, 1, 0)),
        "a_log": a["gdn_a_log"][0], "dt_bias": a["gdn_dt_bias"][0], "norm_w": a["gdn_norm_w"][0],
        "sinks": a["swa_sinks"][0], "w_out": a["w_out"][0], "ln1_g": a["ln1_g"][0], "ln1_b": a["ln1_b"][0],
        "wq": blocks(a["peer_wq"][0]), "keysT": np.ascontiguousarray(keys),
        "uT": np.ascontiguousarray(a["peer_u"][0].reshape(NK, NK, KC, P).transpose(0, 3, 2, 1)),
        "v": a["peer_v"][0], "ln2_g": a["ln2_g"][0], "ln2_b": a["ln2_b"][0],
        "consts": constants(), "wmask": window_masks(),
    }


def kernel(**inputs):
    import concourse.bacc as bacc
    from concourse.bass_utils import run_bass_kernel_spmd

    nc = bacc.Bacc("TRN2", target_bir_lowering=False, num_devices=1)
    arrays = {f"in_{k}": v for k, v in layout(inputs).items()}
    io = {k[3:]: nc.dram_tensor(k, v.shape, mybir.dt.from_np(v.dtype), kind="ExternalInput").ap()
          for k, v in arrays.items()}
    out = nc.dram_tensor("out", (1, T, D), F32, kind="ExternalOutput").ap()
    build(nc, io, out)
    result = run_bass_kernel_spmd(nc, [arrays], core_ids=[0])
    return result.results[0]["out"]
```

```python
from contextlib import ExitStack, contextmanager

import concourse.bass as bass
import numpy as np
from concourse import mybir

F32 = mybir.dt.float32
F32R = mybir.dt.float32r
U32 = mybir.dt.uint32
ALU = mybir.AluOpType
ACT = mybir.ActivationFunctionType
AX = mybir.AxisListType.X

P = 128
T = 1024
D = 1024
NT = T // P
KC = D // P
GH = 4
AH = 8
AD = 64
N_CH = 16
N_CONV = 12
PH = 8
TOPK = 16
NK = 128
HALF = 512
TG = 64
ALPHA = 2.0 ** 0.25
LN_EPS = 1e-5
RMS_EPS = 1e-6
L2_EPS = 1e-6
MASKED = -1e30
REPLACED = -3e38
TAIL = 4
AHEAD_R = PH + TAIL
AHEAD_G = T // (2 * TG)
AHEAD = AHEAD_R + AHEAD_G
LEVELS = 7

C_ID, C_TRIU, C_NEG, C_ONES, C_LEVEL = 0, 128, 256, 384, 512
C_IOTA = C_LEVEL + LEVELS * 128
C_IOTA16 = C_IOTA + 128
C_EPS = C_IOTA16 + 16
C_N = C_EPS + 4


def constants():
    c = np.zeros((P, C_N), np.float32)
    i, j = np.arange(P)[:, None], np.arange(P)[None, :]
    c[:, C_ID:C_ID + 128] = i == j
    c[:, C_TRIU:C_TRIU + 128] = i <= j
    c[:, C_NEG:C_NEG + 128] = np.where(j >= i, 0.0, MASKED)
    c[:, C_ONES:C_ONES + 128] = 1.0
    for n in range(LEVELS):
        bi, bj = i >> n, j >> n
        c[:, C_LEVEL + 128 * n:C_LEVEL + 128 * (n + 1)] = np.where((bi % 2 == 1) & (bj == bi - 1), -1.0, 0.0)
    c[:, C_IOTA:C_IOTA + 128] = j
    c[:, C_IOTA16:C_IOTA16 + 16] = np.arange(16)
    c[:, C_EPS + 0] = LN_EPS
    c[:, C_EPS + 1] = RMS_EPS
    c[:, C_EPS + 2] = L2_EPS
    c[:, C_EPS + 3] = L2_EPS * P
    return c


def window_masks():
    q = np.arange(P)[:, None] // 64
    k = np.arange(2 * P)[None, :] // 64
    m = np.where((k == q + 1) | (k == q + 2), 0.0, MASKED).astype(np.float32)
    out = np.stack([m] * NT)
    out[0, :, :P] = MASKED
    return out


def ts(start, size):
    return bass.ds(start, size)


def wait_apart(engine, tick, semaphore, value):
    engine.wait_ge(semaphore, value)
    engine.sem_inc(tick, 1)


@contextmanager
def stage_semaphores(nc):
    used = []

    def sem(name):
        used.append(nc.alloc_semaphore(name))
        return used[-1]

    yield sem
    nc.clear_and_free_semaphores(used)
    nc.all_engine_barrier()


def project(nc, sem, io, scr, ba, cst, psum):
    with ExitStack() as ctx:
        def sb(name, shape, dt=F32):
            return ctx.enter_context(nc.sbuf_tensor(name, shape, dt))

        TOK = GH * P + P + 2 * GH
        xh = sb("p_xh", [P, KC, T], F32R)
        xl = sb("p_xl", [P, KC, T], F32R)
        part = [sb(f"p_part{s}", [P, T]) for s in range(2)]
        wr = [sb(f"p_wr{s}", [P, KC, P]) for s in range(2)]
        wh = [sb(f"p_wh{s}", [P, KC, P], F32R) for s in range(2)]
        wl = [sb(f"p_wl{s}", [P, KC, P], F32R) for s in range(2)]
        toh = sb("p_toh", [P, KC, TOK], F32R)
        tol = sb("p_tol", [P, KC, TOK], F32R)
        convw = sb("p_convw", [P, N_CONV, 4])
        normw = sb("p_normw", [P, P])
        raw = [sb(f"p_raw{s}", [P, 3 + T]) for s in range(2)]
        cv = [sb(f"p_cv{s}", [P, T]) for s in range(2)]
        out = [sb(f"p_out{s}", [P, T]) for s in range(2)]
        zt = [sb(f"p_zt{s}", [P, GH * P]) for s in range(2)]
        svt = [sb(f"p_sv{s}", [P, P]) for s in range(2)]
        zero = sb("p_zero", [P, P])
        squares = sb("p_squares", [P, 2 * GH, T])
        ps = [psum[:, 2 * s:2 * s + 2, :] for s in range(2)]

        part_in = [sem(f"part_in{s}") for s in range(2)]
        part_hi, part_lo = sem("part_hi"), sem("part_lo")
        w_hi = [sem(f"w_hi{s}") for s in range(2)]
        w_lo = [sem(f"w_lo{s}") for s in range(2)]
        side_in = sem("side_in")
        w_in = [sem(f"w_in{s}") for s in range(2)]
        mm = [sem(f"proj_mm{s}") for s in range(2)]
        evac = [sem(f"proj_evac{s}") for s in range(2)]
        zeroed = sem("proj_zeroed")
        squared = sem("squared")
        conv_step = sem("conv_step")
        conv_done = [sem(f"conv_done{s}") for s in range(2)]
        silu = [sem(f"silu{s}") for s in range(2)]
        stored = [sem(f"ch_stored{s}") for s in range(2)]
        gated = [sem(f"z_gated{s}") for s in range(2)]
        tok_stored = [sem(f"tok_stored{s}") for s in range(2)]
        pad_stored = sem("pad_stored")
        N_BLK = N_CH + 1
        with nc.Block() as block:
            @block.sync
            def _(sp):
                def load_w(n, s, b):
                    sp.wait_ge(w_lo[s], n)
                    sp.dma_start(wr[s][:], io["w_ch"][b]).then_inc(w_in[s], 16)

                load_w(0, 0, 0)
                for k in range(KC):
                    if k >= 2:
                        sp.wait_ge(part_lo, k - 1)
                    sp.dma_start(part[k % 2][:], io["xT"][k * P:(k + 1) * P, :]).then_inc(part_in[k % 2], 16)
                    if k == 2:
                        load_w(0, 1, 1)
                sp.dma_start(convw[:], io["conv_w"]).then_inc(side_in, 16)
                sp.dma_start(normw[:], io["norm_w"].partition_broadcast(P)).then_inc(side_in, 16)
                with sp.Fori(1, N_CH // 2) as i:
                    for s in range(2):
                        load_w(i, s, 2 * i + s)
                load_w(N_CH // 2, 0, N_CH)
                for k in range(KC):
                    sp.wait_ge(part_lo, KC + k - 1)
                    sp.dma_start(part[k % 2][:, 0:TOK], io["w_tok"][:, k, :]).then_inc(part_in[k % 2], 16)

            @block.tensor
            def _(pe):
                def channel_block(s, n, first=False):
                    pe.wait_ge(w_hi[s], n + 1)
                    pe.wait_ge(w_lo[s], n + 1)
                    pe.wait_ge(evac[s], n)
                    for k in range(KC):
                        if first:
                            pe.wait_ge(part_lo, k + 1)
                        for h in range(2):
                            c = slice(h * HALF, (h + 1) * HALF)
                            nc.tensor.matmul(ps[s][:, h, :], wh[s][:, k, :], xh[:, k, c], start=(k == 0), stop=False)
                            nc.tensor.matmul(ps[s][:, h, :], wh[s][:, k, :], xl[:, k, c], start=False, stop=False)
                            last = nc.tensor.matmul(ps[s][:, h, :], wl[s][:, k, :], xh[:, k, c], start=False,
                                                    stop=(k == KC - 1))
                    last.then_inc(mm[s], 1)

                channel_block(0, 0, first=True)
                channel_block(1, 0)
                with pe.Fori(1, N_CH // 2) as i:
                    for s in range(2):
                        channel_block(s, i)
                channel_block(0, N_CH // 2)
                pe.wait_ge(squared, 2 * GH)
                for t in range(NT):
                    for b in range(2 * GH):
                        nc.tensor.matmul(psum[:, 4, t * 2 * GH + b:t * 2 * GH + b + 1], squares[:, b, t * P:(t + 1) * P],
                                         cst[:, C_ONES:C_ONES + 1], start=True, stop=True)
                pe.wait_ge(part_lo, 2 * KC)
                for t in range(NT):
                    s = (t + 1) % 2
                    n = N_CH // 2 + (1 if s == 0 else 0) + t // 2
                    r = slice(t * P, (t + 1) * P)
                    pe.wait_ge(evac[s], n)
                    for k in range(KC):
                        for h in range(2):
                            c = slice(h * TOK // 2, (h + 1) * TOK // 2)
                            dst = ps[s][:, h, 0:TOK // 2]
                            nc.tensor.matmul(dst, xh[:, k, r], toh[:, k, c], start=(k == 0), stop=False)
                            nc.tensor.matmul(dst, xh[:, k, r], tol[:, k, c], start=False, stop=False)
                            last = nc.tensor.matmul(dst, xl[:, k, r], toh[:, k, c], start=False, stop=(k == KC - 1))
                    last.then_inc(mm[s], 1)

            @block.scalar
            def _(act):
                act.wait_ge(zeroed, 3)

                def split_w(n, s):
                    act.wait_ge(w_in[s], 16 * (n + 1))
                    act.wait_ge(mm[s], n)
                    nc.scalar.activation(wh[s][:], wr[s][:], ACT.Copy).then_inc(w_hi[s], 1)

                def split_part(q, dst):
                    act.wait_ge(part_in[q % 2], 16 * (q // 2 + 1))
                    nc.scalar.activation(dst, part[q % 2][:, 0:dst.shape[-1]], ACT.Copy).then_inc(part_hi, 1)

                split_w(0, 0)
                for k in range(KC):
                    split_part(k, xh[:, k, :])
                    if k == 3:
                        split_w(0, 1)

                def channels(i, s):
                    act.wait_ge(mm[s], i + 1)
                    act.wait_ge(conv_done[s], i)
                    nc.scalar.activation(raw[s][:, 3:3 + T], ps[s].rearrange("p h t -> p (h t)"),
                                         ACT.Copy).then_inc(evac[s], 1)
                    split_w(i + 1, s)
                    act.wait_ge(conv_done[s], i + 1)
                    act.wait_ge(stored[s], 16 * i)
                    nc.scalar.activation(out[s][:], cv[s][:], ACT.Silu).then_inc(silu[s], 1)

                with act.Fori(0, GH) as i:
                    for s in range(2):
                        channels(i, s)
                        act.wait_ge(silu[s], i + 1)
                        nc.scalar.activation(squares[:, ts(2 * i + s, 1), :].rearrange("p b t -> p (b t)"), out[s][:],
                                             ACT.Square).then_inc(squared, 1)
                with act.Fori(GH, N_CONV // 2) as i:
                    for s in range(2):
                        channels(i, s)
                for b in range(N_CONV, N_BLK):
                    s, n = b % 2, b // 2
                    act.wait_ge(mm[s], n + 1)
                    act.wait_ge(stored[s], 16 * n)
                    nc.scalar.activation(out[s][:], ps[s].rearrange("p h t -> p (h t)"), ACT.Copy).then_inc(evac[s], 1)
                    if b + 2 < N_BLK:
                        split_w(n + 1, s)
                    if b < N_CH:
                        for k in (2 * (b - N_CONV), 2 * (b - N_CONV) + 1):
                            split_part(KC + k, toh[:, k, :])
                for t in range(NT):
                    s = (t + 1) % 2
                    n = N_CH // 2 + (1 if s == 0 else 0) + t // 2
                    act.wait_ge(mm[s], n + 1)
                    if t >= 2:
                        act.wait_ge(tok_stored[s], 32 * (t // 2))
                    nc.scalar.activation(zt[s][:, 0:TOK // 2], ps[s][:, 0, 0:TOK // 2], ACT.Silu)
                    z1 = GH * P - TOK // 2
                    nc.scalar.activation(zt[s][:, TOK // 2:], ps[s][:, 1, 0:z1], ACT.Silu).then_inc(gated[s], 1)
                    nc.scalar.activation(svt[s][:], ps[s][:, 1, z1:z1 + P], ACT.Copy)
                    nc.scalar.activation(ba[:, t, :], ps[s][:, 1, z1 + P:TOK // 2], ACT.Copy).then_inc(evac[s], 1)

            @block.vector
            def _(dve):
                nc.vector.memset(raw[0][:, 0:3], 0.0).then_inc(zeroed, 1)
                nc.vector.memset(raw[1][:, 0:3], 0.0).then_inc(zeroed, 1)
                nc.vector.memset(zero[:], 0.0).then_inc(zeroed, 1)

                def split_w(n, s):
                    dve.wait_ge(w_hi[s], n + 1)
                    nc.vector.tensor_tensor(wl[s][:], wr[s][:], wh[s][:].bitcast(F32), ALU.subtract).then_inc(w_lo[s], 1)

                def split_part(q, hi, lo):
                    dve.wait_ge(part_hi, q + 1)
                    nc.vector.tensor_tensor(lo, part[q % 2][:, 0:hi.shape[-1]], hi.bitcast(F32),
                                            ALU.subtract).then_inc(part_lo, 1)

                split_w(0, 0)
                for k in range(KC):
                    split_part(k, xh[:, k, :], xl[:, k, :])
                    if k == 3:
                        split_w(0, 1)
                dve.wait_ge(side_in, 32)
                with dve.Fori(0, N_CONV // 2) as i:
                    for s in range(2):
                        b = 2 * i + s
                        dve.wait_ge(evac[s], i + 1)
                        dve.wait_ge(silu[s], i)
                        nc.vector.tensor_scalar(cv[s][:], raw[s][:, 0:T], convw[:, ts(b, 1), 0], None,
                                                ALU.mult).then_inc(conv_step, 1)
                        for k in range(1, 4):
                            dve.wait_ge(conv_step, b * 3 + k)
                            step = nc.vector.scalar_tensor_tensor(cv[s][:], raw[s][:, k:k + T], convw[:, ts(b, 1), k],
                                                                  cv[s][:], ALU.mult, ALU.add)
                            step.then_inc(conv_step if k < 3 else conv_done[s], 1)
                        split_w(i + 1, s)
                for b in range(N_CONV, N_CH):
                    if b + 2 <= N_CH:
                        split_w(b // 2 + 1, b % 2)
                    for k in (2 * (b - N_CONV), 2 * (b - N_CONV) + 1):
                        split_part(KC + k, toh[:, k, :], tol[:, k, :])
                for t in range(NT):
                    s = (t + 1) % 2
                    dve.wait_ge(gated[s], t // 2 + 1)
                    zv = zt[s].rearrange("p (h d) -> p h d", h=GH)
                    nc.vector.tensor_tensor(zv, zv, normw[:, :].unsqueeze(1).broadcast_to([P, GH, P]),
                                            ALU.mult).then_inc(silu[s], 1)

            @block.gpsimd
            def _(pool):
                pool.wait_ge(zeroed, 3)
                pool.dma_start(scr["sk"][:, 0:P], zero[:]).then_inc(pad_stored, 16)
                pool.dma_start(scr["sv"][0:P, :], zero[:]).then_inc(pad_stored, 16)
                with pool.Fori(0, N_CONV // 2) as i:
                    for s in range(2):
                        pool.wait_ge(silu[s], i + 1)
                        pool.dma_start(scr["ch"][2 * i + s], out[s][:]).then_inc(stored[s], 16)
                for b in range(N_CONV, N_CH):
                    s, n = b % 2, b // 2
                    pool.wait_ge(evac[s], n + 1)
                    pool.dma_start(scr["ch"][b], out[s][:]).then_inc(stored[s], 16)
                pool.wait_ge(evac[0], N_CH // 2 + 1)
                pool.dma_start(scr["sk"][:, P:P + T], out[0][:]).then_inc(stored[0], 16)
                for t in range(NT):
                    s = (t + 1) % 2
                    pool.wait_ge(silu[s], N_CONV // 2 + t // 2 + 1)
                    pool.dma_start(scr["z"][t * P:(t + 1) * P, :], zt[s][:]).then_inc(tok_stored[s], 16)
                    pool.wait_ge(evac[s], N_CH // 2 + (1 if s == 0 else 0) + t // 2 + 1)
                    pool.dma_start(scr["sv"][(t + 1) * P:(t + 2) * P, :], svt[s][:]).then_inc(tok_stored[s], 16)
                pool.wait_ge(pad_stored, 32)
                pool.wait_ge(stored[0], 16 * (N_CH // 2 + 1))
                pool.wait_ge(stored[1], 16 * (N_CH // 2))
                for s in range(2):
                    pool.wait_ge(tok_stored[s], 16 * NT)


def mix_tokens(nc, sem, io, scr, ba, cst, psum):
    with ExitStack() as ctx:
        def sb(name, shape, dt=F32):
            return ctx.enter_context(nc.sbuf_tensor(name, shape, dt))

        ident = cst[:, C_ID:C_ID + P]
        triu = cst[:, C_TRIU:C_TRIU + P]
        neg = cst[:, C_NEG:C_NEG + P]
        ones = cst[:, C_ONES:C_ONES + P]

        def heads(ap):
            return ap.unsqueeze(1).broadcast_to([P, GH, P])

        wout = [sb(f"m_wout_{part}", [P, KC, D], F32R) for part in ("hi", "lo")]
        wout_raw = [sb(f"m_wout_raw{s}", [P, D]) for s in range(2)]
        lng = sb("m_lng", [P, D])
        lnb = sb("m_lnb", [P, D])
        sinks = sb("m_sinks", [P, AH])
        dtb = sb("m_dtb", [P, GH])
        alog = sb("m_alog", [P, GH])
        ch = [sb(f"m_ch{s}", [P, N_CH, P]) for s in range(2)]
        kw = [sb(f"m_kw{s}", [P, 2 * P]) for s in range(2)]
        vw = [sb(f"m_vw{s}", [P, 2, P]) for s in range(2)]
        zw = [sb(f"m_zw{s}", [P, GH, P]) for s in range(2)]
        wm = [sb(f"m_wm{s}", [P, 2 * P]) for s in range(2)]
        xt = [sb(f"m_xt{s}", [P, D]) for s in range(2)]
        mag = sb("m_mag", [P, NT, 2 * GH])
        clip = sb("m_clip", [P, NT, 2 * GH])
        lr = sb("m_lr", [P, NT, 2 * GH])
        small = {n: sb(f"m_{n}", [P, NT, GH]) for n in ("lnbeta", "g", "gam", "nkey", "kdl", "kdec", "nbeg", "decay", "beta")}
        rows = sb("m_rows", [P, NT, 2, GH])
        gB = sb("m_gB", [P, 2 * GH, P])
        e0 = sb("m_e0", [P, GH, P])
        dm = sb("m_dm", [P, 2, GH, P])
        eg = sb("m_eg", [P, GH, P])
        aq = [sb(f"m_aq{s}", [P, 2, GH, P]) for s in range(2)]
        qd = [sb(f"m_qd{s}", [P, GH, P]) for s in range(2)]
        kd = sb("m_kd", [P, GH, P])
        vb = sb("m_vb", [P, GH, P])
        tu = sb("m_tu", [P, 2, GH, P])
        xs = sb("m_xs", [P, GH, P])
        uu = sb("m_uu", [P, GH, P])
        state = sb("m_state", [P, GH, P])
        faded = sb("m_faded", [P, GH, P])
        og = sb("m_og", [P, GH, P])
        rms = sb("m_rms", [P, 2, GH])
        mixT = [[sb(f"m_mixT{s}_{part}", [P, KC, P], F32R) for part in ("hi", "lo")] for s in range(2)]
        sc = sb("m_sc", [P, AH, 2 * P])
        pT = sb("m_pT", [P, AH, 2, P])
        on = sb("m_on", [P, AH, AD])
        mx = sb("m_mx", [P, 4, AH])
        h1 = sb("m_h1", [P, D])
        st = sb("m_st", [P, 2, 6])
        mv = sb("m_mv", [P, 4])

        def bank(b):
            return psum[:, b, :].rearrange("p (h d) -> p h d", h=GH)

        ATT = psum[:, 4:6, :].rearrange("p b k -> p (b k)")

        side_in = sem("mix_side_in")
        ln_in = sem("ln_in")
        wout_in = [sem(f"wout_in{s}") for s in range(2)]
        wout_hi, wout_lo = sem("wout_hi"), sem("wout_lo")
        tile_in = [[sem(f"tile_in{s}_{n}") for n in range(6)] for s in range(2)]
        x1_out = sem("x1_stored")
        tick = sem("m_tick")
        prep = {n: sem(f"prep_{n}") for n in "bias abs exp one ln g0 g sums gam kdl rows exps done".split()}
        names = ("gB e0 row_a row_q eg add_a e_add dmx kk kq aq_a aq qd tr kd xt0 xs0 t1 t1T u1 decayed ks kb r2 u_mm "
                 "u_ev ods st_up osq osum oroot orms og ogT mg mg_lo mask max mx nmx prob p_tr p_ev s_mm den rec o_mm o_n onT "
                 "ma ma_lo proj h1 stat aggr root rstd nrm nrm_g x1").split()
        S = {n: sem(f"m_{n}") for n in names}
        lx, lm, lt, lu, la, lb = (sem(f"level_{n}") for n in ("x", "masked", "t", "u", "t_add", "u_add"))
        LV = LEVELS - 1
        last_tile = NT - 1

        def load(sp, c, s):
            for n, (dst, src) in enumerate((
                    (ch[s][:], scr["ch"][:, :, ts(c * P, P)].rearrange("b p t -> p b t")),
                    (kw[s][:], scr["sk"][:, ts(c * P, 2 * P)]),
                    (vw[s][:], scr["sv"][ts(c * P, 2 * P), :].rearrange("(a p) d -> p a d", a=2)),
                    (zw[s][:], scr["z"][ts(c * P, P), :].rearrange("p (h d) -> p h d", h=GH)),
                    (wm[s][:], io["wmask"][ts(c, 1)].rearrange("a p k -> (a p) k")))):
                sp.dma_start(dst, src).then_inc(tile_in[s][n], 16)

        def load_x(sp, c, s):
            sp.dma_start(xt[s][:], io["x"][ts(c * P, P), :]).then_inc(tile_in[s][5], 16)

        def tiles(engine, body):
            body(0, 0, 0, False, True)
            with engine.Fori(0, NT // 2 - 1) as i:
                body(2 * i + 1, i, 1, True, True)
                body(2 * i + 2, i + 1, 0, True, True)
            body(last_tile, NT // 2 - 1, 1, True, False)

        with nc.Block() as block:
            @block.sync
            def _(sp):
                sp.dma_start(sinks[:], io["sinks"].partition_broadcast(P)).then_inc(side_in, 16)
                sp.dma_start(dtb[:], io["dt_bias"].partition_broadcast(P)).then_inc(side_in, 16)
                sp.dma_start(alog[:], io["a_log"].partition_broadcast(P)).then_inc(side_in, 16)
                for s in range(2):
                    load(sp, s, s)
                    load_x(sp, s, s)
                for k in range(KC):
                    if k >= 2:
                        sp.wait_ge(wout_lo, k - 1)
                    sp.dma_start(wout_raw[k % 2][:], io["w_out"][k * P:(k + 1) * P, :]).then_inc(wout_in[k % 2], 16)
                sp.dma_start(lng[:], io["ln1_g"].partition_broadcast(P)).then_inc(ln_in, 16)
                sp.dma_start(lnb[:], io["ln1_b"].partition_broadcast(P)).then_inc(ln_in, 16)

                def refill(c, s):
                    sp.wait_ge(S["og"], c + 1)
                    sp.wait_ge(S["o_mm"], c + 1)
                    load(sp, c + 2, s)

                def store(c, s, more=True):
                    sp.wait_ge(S["x1"], c + 1)
                    sp.dma_start(scr["x1"][ts(c * P, P), :], h1[:]).then_inc(x1_out, 16)
                    if more:
                        load_x(sp, c + 2, s)

                refill(0, 0)
                with sp.Fori(0, NT // 2 - 2) as i:
                    refill(2 * i + 1, 1)
                    store(2 * i, 0)
                    refill(2 * i + 2, 0)
                    store(2 * i + 1, 1)
                refill(NT - 3, 1)
                store(NT - 4, 0)
                store(NT - 3, 1)
                for s in range(2):
                    store(NT - 2 + s, s, more=False)
                sp.wait_ge(x1_out, 16 * NT)

            @block.tensor
            def _(pe):
                pe.wait_ge(prep["g"], 1)
                nc.tensor.matmul(psum[:, 0, 0:NT * GH], triu, small["g"].rearrange("p t h -> p (t h)"),
                                 start=True, stop=True)
                nc.tensor.matmul(psum[:, 0, NT * GH:2 * NT * GH], ones, small["g"].rearrange("p t h -> p (t h)"),
                                 start=True, stop=True).then_inc(prep["sums"], 1)
                pe.wait_ge(prep["done"], 1)

                def project_out(s, first, n):
                    for m in range(first, first + n):
                        half, k = divmod(m, KC)
                        c = slice(half * HALF, (half + 1) * HALF)
                        for n, (a, w) in enumerate(((0, 0), (0, 1), (1, 0))):
                            last = nc.tensor.matmul(psum[:, 6 + half, :], mixT[s][a][:, k, :], wout[w][:, k, c],
                                                    start=(k == 0 and n == 0), stop=(k == KC - 1 and n == 2))
                    return last

                def scores(s, half):
                    for n in range(4):
                        last = nc.tensor.matmul(ATT[:, n * 2 * P:(n + 1) * 2 * P],
                                                ch[s][64 * half:64 * half + 64, N_CONV + n, :],
                                                kw[s][64 * half:64 * half + 64, :], start=True, stop=True)
                    last.then_inc(S["s_mm"], 1)

                def transpose_probs(half):
                    for n in range(8):
                        last = nc.tensor.transpose(ATT[:, n * P:(n + 1) * P],
                                                   sc[:, 4 * half + n // 2, (n % 2) * P:(n % 2 + 1) * P], ident)
                    last.then_inc(S["p_tr"], 1)

                def ahead(d, i, s, step):
                    if step == 0:
                        pe.wait_ge(S["gB"], d + 1)
                        for h in range(GH):
                            last = nc.tensor.matmul(bank(1)[:, h, :], gB[:, h, :], ident, start=True, stop=True)
                        last.then_inc(S["row_a"], 1)
                    if step == 1:
                        pe.wait_ge(S["add_a"], d + 1)
                        for h in range(GH):
                            last = nc.tensor.matmul(bank(1)[:, h, :], gB[:, GH + h, :], ident, start=True, stop=True)
                        last.then_inc(S["row_q"], 1)
                    if step == 2:
                        pe.wait_ge(S["e_add"], d + 1)
                        pe.wait_ge(tile_in[s][0], 16 * (i + 1))
                        for h in range(GH):
                            last = nc.tensor.matmul(bank(1)[:, h, :], ch[s][:, GH + h, :], ch[s][:, GH + h, :],
                                                    start=True, stop=True)
                        last.then_inc(S["kk"], 1)
                    if step == 3:
                        pe.wait_ge(S["aq_a"], d + 1)
                        for h in range(GH):
                            last = nc.tensor.matmul(bank(1)[:, h, :], ch[s][:, GH + h, :], ch[s][:, h, :],
                                                    start=True, stop=True)
                        last.then_inc(S["kq"], 1)

                def begin_x(d, s):
                    pe.wait_ge(S["aq"], d + 1)
                    for h in range(GH):
                        last = nc.tensor.transpose(bank(0)[:, h, :], aq[s][:, 0, h, :], ident)
                    last.then_inc(S["xt0"], 1)

                def begin_u(d):
                    pe.wait_ge(S["t1"], d + 1)
                    for h in range(GH):
                        last = nc.tensor.transpose(bank(0)[:, h, :], tu[:, 0, h, :], ident)
                    last.then_inc(S["t1T"], 1)

                share = (2, 2, 2, 2, 3, 3, 2)

                def body(c, i, s, before, after):
                    now = c + 1
                    pe.wait_ge(tile_in[s][0], 16 * (i + 1))
                    for h in range(GH):
                        nc.tensor.transpose(bank(2)[:, h, :], ch[s][:, GH + h, :], ident)
                    for h in range(GH):
                        last = nc.tensor.transpose(bank(3)[:, h, :], ch[s][:, 2 * GH + h, :], ident)
                    last.then_inc(S["tr"], 1)
                    pe.wait_ge(tile_in[s][1], 16 * (i + 1))
                    if before:
                        pe.wait_ge(S["ma_lo"], c)
                    scores(s, 0)
                    if before:
                        pe.wait_ge(S["mg_lo"], c)
                        pe.wait_ge(wout_lo, KC)
                        pe.wait_ge(S["h1"], 2 * (c - 1))
                    pe.wait_ge(S["u1"], now)
                    for n in range(LV):
                        at_level = c * LV + n + 1
                        if n:
                            pe.wait_ge(la, c * (LV - 1) + n)
                        for h in range(GH):
                            last = nc.tensor.matmul(bank(0)[:, h, :], aq[s][:, 0, h, :], tu[:, 0, h, :],
                                                    start=True, stop=True)
                        last.then_inc(lx, 1)
                        if before:
                            project_out(1 - s, sum(share[:n]), share[n])
                        if n == 2:
                            pe.wait_ge(S["prob"], 2 * c + 1)
                            transpose_probs(0)
                        if n == 3:
                            pe.wait_ge(S["p_ev"], 2 * c + 1)
                            scores(s, 1)
                        if after and n in (0, 1, 2, 4):
                            ahead(c + 1, i + s, 1 - s, min(n, 3))
                        pe.wait_ge(lm, at_level)
                        if n == 0:
                            pe.wait_ge(S["kd"], now)
                        else:
                            pe.wait_ge(lb, c * LV + n)
                        if n < LV - 1:
                            for h in range(GH):
                                last = nc.tensor.matmul(bank(2)[:, h, :], tu[:, 1, h, :], xs[:, h, :], start=True, stop=True)
                            last.then_inc(lt, 1)
                        for h in range(GH):
                            last = nc.tensor.matmul(bank(3)[:, h, :], xs[:, h, :], tu[:, 1, h, :], start=True, stop=True)
                        last.then_inc(lu, 1)
                    if before:
                        pe.wait_ge(S["st_up"], c)
                    for h in range(GH):
                        last = nc.tensor.matmul(bank(0)[:, h, :], ch[s][:, GH + h, :], state[:, h, :], start=True, stop=True)
                    last.then_inc(S["ks"], 1)
                    if before:
                        project_out(1 - s, sum(share[:LV]), share[LV]).then_inc(S["proj"], 1)
                    pe.wait_ge(S["r2"], now)
                    pe.wait_ge(lb, now * LV)
                    if after:
                        pe.wait_ge(S["aq"], c + 2)
                    for h in range(GH):
                        last = nc.tensor.matmul(bank(1)[:, h, :], tu[:, 1, h, :], vb[:, h, :], start=True, stop=True)
                    last.then_inc(S["u_mm"], 1)
                    if after:
                        begin_x(c + 1, 1 - s)
                    pe.wait_ge(S["u_ev"], now)
                    for h in range(GH):
                        nc.tensor.matmul(bank(3)[:, h, :], kd[:, h, :], uu[:, h, :], start=True, stop=True)
                    for h in range(GH):
                        nc.tensor.matmul(bank(2)[:, h, :], aq[s][:, 1, h, :], uu[:, h, :], start=True, stop=False)
                        last = nc.tensor.matmul(bank(2)[:, h, :], qd[s][:, h, :], state[:, h, :], start=False, stop=True)
                    last.then_inc(S["ods"], 1)
                    pe.wait_ge(S["prob"], 2 * now)
                    transpose_probs(1)
                    if after:
                        begin_u(c + 1)
                    pe.wait_ge(S["p_ev"], 2 * now)
                    pe.wait_ge(tile_in[s][2], 16 * (i + 1))
                    for a in range(AH):
                        r = a // 4
                        for k in range(2):
                            last = nc.tensor.matmul(psum[:, 4, a * AD:(a + 1) * AD], pT[:, a, k, :],
                                                    vw[s][:, k, r * AD:(r + 1) * AD], start=(k == 0), stop=(k == 1))
                    last.then_inc(S["o_mm"], 1)
                    pe.wait_ge(S["og"], now)
                    for h in range(GH):
                        last = nc.tensor.transpose(bank(1)[:, h, :], og[:, h, :], ident)
                    last.then_inc(S["ogT"], 1)
                    pe.wait_ge(S["o_n"], now)
                    for p in range(4):
                        last = nc.tensor.transpose(bank(5)[:, p, :], on[:, 2 * p:2 * p + 2, :].rearrange("p a d -> p (a d)"),
                                                   ident)
                    last.then_inc(S["onT"], 1)

                for step in range(4):
                    ahead(0, 0, 0, step)
                begin_x(0, 0)
                begin_u(0)
                tiles(pe, body)
                pe.wait_ge(S["mg_lo"], NT)
                pe.wait_ge(S["ma_lo"], NT)
                pe.wait_ge(S["h1"], 2 * last_tile)
                project_out(last_tile % 2, 0, 2 * KC).then_inc(S["proj"], 1)

            @block.scalar
            def _(act):
                act.wait_ge(side_in, 48)
                act.wait_ge(prep["bias"], 1)
                nc.scalar.activation(mag[:], ba[:], ACT.Abs).then_inc(prep["abs"], 1)
                act.wait_ge(prep["abs"], 1)
                nc.scalar.activation(mag[:], mag[:], ACT.Exp, scale=-1.0).then_inc(prep["exp"], 1)
                nc.scalar.activation(alog[:], alog[:], ACT.Exp)
                lrv = lr.rearrange("p t (a h) -> p t a h", a=2)
                ss = psum[:, 4, 0:NT * 2 * GH].rearrange("p (t a h) -> p t a h", t=NT, a=2)
                nc.scalar.activation(lrv[:, :, 0, :], ss[:, :, 0, :], ACT.Ln, scale=float(P), bias=cst[:, C_EPS + 3:C_EPS + 4])
                nc.scalar.activation(lrv[:, :, 1, :], ss[:, :, 1, :], ACT.Ln, bias=cst[:, C_EPS + 2:C_EPS + 3])
                act.wait_ge(prep["one"], 1)
                nc.scalar.activation(mag[:], mag[:], ACT.Ln).then_inc(prep["ln"], 1)
                act.wait_ge(prep["rows"], 1)
                nc.scalar.activation(small["beta"][:], small["lnbeta"][:], ACT.Exp)
                nc.scalar.activation(small["kdec"][:], small["kdl"][:], ACT.Exp)
                nc.scalar.activation(small["nbeg"][:], rows[:, :, 0, :], ACT.Exp)
                nc.scalar.activation(small["decay"].rearrange("p t h -> p (t h)"), psum[:, 0, NT * GH:2 * NT * GH],
                                     ACT.Exp).then_inc(prep["exps"], 1)

                def exps(c, half):
                    act.wait_ge(S["nmx"], 2 * c + half + 1)
                    for a in range(4 * half, 4 * half + 4):
                        nc.scalar.activation(sc[:, a, :], sc[:, a, :], ACT.Exp, bias=mx[:, 1, a:a + 1],
                                             accum_out=mx[:, 3, a:a + 1])
                    a = slice(4 * half, 4 * half + 4)
                    nc.scalar.activation(mx[:, 2, a], mx[:, 2, a], ACT.Exp).then_inc(S["prob"], 1)

                def evacuate_probs(c, half):
                    act.wait_ge(S["p_tr"], 2 * c + half + 1)
                    nc.scalar.activation(pT[:, 4 * half:4 * half + 4].rearrange("p a k q -> p (a k q)"), ATT,
                                         ACT.Copy).then_inc(S["p_ev"], 1)

                def root(c):
                    act.wait_ge(S["aggr"], c + 1)
                    nc.scalar.activation(mv[:, 2:3], mv[:, 1:2], ACT.Sqrt, bias=cst[:, C_EPS:C_EPS + 1]).then_inc(S["root"], 1)

                def ahead(d):
                    act.wait_ge(S["row_q"], d + 1)
                    act.wait_ge(S["qd"], d)
                    nc.scalar.activation(eg[:], bank(1), ACT.Exp).then_inc(S["eg"], 1)
                    act.wait_ge(S["e_add"], d + 1)
                    nc.scalar.activation(dm[:], dm[:], ACT.Exp).then_inc(S["dmx"], 1)

                def begin_u(d):
                    act.wait_ge(S["t1T"], d + 1)
                    nc.scalar.activation(tu[:, 1], bank(0), ACT.Copy).then_inc(S["u1"], 1)

                def split_wout(k):
                    act.wait_ge(wout_in[k % 2], 16 * (k // 2 + 1))
                    nc.scalar.activation(wout[0][:, k, :], wout_raw[k % 2][:], ACT.Copy).then_inc(wout_hi, 1)

                def body(c, i, s, before, after):
                    now = c + 1
                    exps(c, 0)
                    if not before:
                        split_wout(0)
                    if after:
                        ahead(c + 1)
                    if not before:
                        split_wout(1)
                        split_wout(2)
                    evacuate_probs(c, 0)
                    if not before:
                        split_wout(3)
                        split_wout(4)
                    exps(c, 1)
                    if not before:
                        split_wout(5)
                        split_wout(6)
                        split_wout(7)
                    act.wait_ge(S["u_mm"], now)
                    nc.scalar.activation(uu[:], bank(1), ACT.Copy).then_inc(S["u_ev"], 1)
                    act.wait_ge(S["ods"], now)
                    nc.scalar.activation(og[:], bank(2), ACT.Square).then_inc(S["osq"], 1)
                    evacuate_probs(c, 1)
                    act.wait_ge(S["osum"], now)
                    nc.scalar.activation(rms[:, 0, :], rms[:, 0, :], ACT.Sqrt, scale=1.0 / P,
                                         bias=cst[:, C_EPS + 1:C_EPS + 2]).then_inc(S["oroot"], 1)
                    if before:
                        root(c - 1)
                    if after:
                        begin_u(c + 1)
                    act.wait_ge(S["ogT"], now)
                    nc.scalar.activation(mixT[s][0][:, 0:GH, :], bank(1), ACT.Copy).then_inc(S["mg"], 1)
                    act.wait_ge(S["onT"], now)
                    nc.scalar.activation(mixT[s][0][:, GH:, :], bank(5), ACT.Copy).then_inc(S["ma"], 1)

                act.wait_ge(prep["done"], 1)
                ahead(0)
                begin_u(0)
                tiles(act, body)
                root(last_tile)

            @block.vector
            def _(dve):
                dve.wait_ge(side_in, 48)
                nc.vector.tensor_tensor(ba[:, :, GH:2 * GH], ba[:, :, GH:2 * GH],
                                        dtb[:, :].unsqueeze(1).broadcast_to([P, NT, GH]), ALU.add).then_inc(prep["bias"], 1)
                dve.wait_ge(prep["exp"], 1)
                nc.vector.tensor_scalar(mag[:], mag[:], 1.0, None, ALU.add).then_inc(prep["one"], 1)
                nc.vector.tensor_scalar(clip[:, :, 0:GH], ba[:, :, 0:GH], 0.0, None, ALU.min)
                nc.vector.tensor_scalar(clip[:, :, GH:], ba[:, :, GH:], 0.0, None, ALU.max).then_inc(prep["g0"], 1)
                dve.wait_ge(prep["ln"], 1)
                dve.wait_ge(prep["g0"], 1)
                nc.vector.tensor_tensor(clip[:, :, GH:], clip[:, :, GH:], mag[:, :, GH:], ALU.add).then_inc(prep["g0"], 1)
                nc.vector.tensor_tensor(small["lnbeta"][:], clip[:, :, 0:GH], mag[:, :, 0:GH], ALU.subtract)
                nc.vector.tensor_scalar(lr[:], lr[:], -0.5, None, ALU.mult)
                dve.wait_ge(prep["g0"], 2)
                nc.vector.scalar_tensor_tensor(small["g"][:], clip[:, :, GH:], -1.0,
                                               alog[:, :].unsqueeze(1).broadcast_to([P, NT, GH]),
                                               ALU.mult, ALU.mult).then_inc(prep["g"], 1)
                dve.wait_ge(prep["g"], 1)
                dve.wait_ge(prep["sums"], 1)
                nc.vector.tensor_copy(small["gam"].rearrange("p t h -> p (t h)"),
                                      psum[:, 0, 0:NT * GH]).then_inc(prep["gam"], 1)
                dve.wait_ge(prep["gam"], 1)
                nc.vector.tensor_tensor(small["nkey"][:], lr[:, :, GH:], small["gam"][:], ALU.subtract).then_inc(prep["gam"], 1)
                nc.vector.tensor_tensor(rows[:, :, 1, :], small["gam"][:], lr[:, :, 0:GH], ALU.add)
                nc.vector.tensor_tensor(rows[:, :, 0, :], small["gam"][:], lr[:, :, GH:], ALU.add).then_inc(prep["kdl"], 1)
                dve.wait_ge(prep["gam"], 2)
                nc.vector.tensor_tensor(small["kdl"].rearrange("p t h -> p (t h)"), psum[:, 0, NT * GH:2 * NT * GH],
                                        small["nkey"].rearrange("p t h -> p (t h)"), ALU.add)
                dve.wait_ge(prep["kdl"], 1)
                nc.vector.tensor_tensor(rows[:, :, 0, :], rows[:, :, 0, :], small["lnbeta"][:],
                                        ALU.add).then_inc(prep["rows"], 1)
                nc.vector.memset(state[:], 0.0)
                dve.wait_ge(prep["rows"], 1)
                dve.wait_ge(prep["exps"], 1)
                nc.vector.tensor_scalar(small["nbeg"][:], small["nbeg"][:], -1.0, None, ALU.mult).then_inc(prep["done"], 1)
                dve.wait_ge(prep["done"], 1)

                def per_head(name, c):
                    return small[name][:, ts(c, 1), :].rearrange("p t h -> p (t h)").unsqueeze(2).broadcast_to([P, GH, P])

                def ahead(d, i, s, step):
                    e_heads = e0[:, :, :]
                    if step == 0:
                        dve.wait_ge(S["row_q"], d)
                        nc.vector.tensor_copy(gB[:], rows[:, ts(d, 1)].rearrange("p t a h -> p (t a h)").unsqueeze(2)
                                              .broadcast_to([P, 2 * GH, P])).then_inc(S["gB"], 1)
                        nc.vector.tensor_tensor(e0[:], heads(neg), per_head("nkey", d), ALU.add).then_inc(S["e0"], 1)
                    if step == 1:
                        dve.wait_ge(S["row_a"], d + 1)
                        dve.wait_ge(S["e0"], d + 1)
                        nc.vector.tensor_tensor(dm[:, 0], bank(1), e_heads, ALU.add).then_inc(S["add_a"], 1)
                    if step == 2:
                        dve.wait_ge(S["eg"], d + 1)
                        nc.vector.tensor_tensor(dm[:, 1], bank(1), e_heads, ALU.add).then_inc(S["e_add"], 1)
                    if step == 3:
                        dve.wait_ge(tile_in[s][0], 16 * (i + 1))
                        nc.vector.tensor_tensor(qd[s][:], ch[s][:, 0:GH, :], eg[:], ALU.mult).then_inc(S["qd"], 1)
                    if step == 4:
                        dve.wait_ge(S["dmx"], d + 1)
                        dve.wait_ge(S["kk"], d + 1)
                        nc.vector.tensor_tensor(aq[s][:, 0], bank(1), dm[:, 0], ALU.mult).then_inc(S["aq_a"], 1)
                    if step == 5:
                        dve.wait_ge(S["kq"], d + 1)
                        nc.vector.tensor_tensor(aq[s][:, 1], bank(1), dm[:, 1], ALU.mult).then_inc(S["aq"], 1)

                def begin_inverse(d):
                    dve.wait_ge(S["xt0"], d + 1)
                    nc.vector.tensor_tensor(xs[:], bank(0), heads(cst[:, C_LEVEL:C_LEVEL + P]), ALU.mult).then_inc(S["xs0"], 1)
                    dve.wait_ge(S["xs0"], d + 1)
                    nc.vector.tensor_tensor(tu[:, 0], xs[:], heads(ident), ALU.add).then_inc(S["t1"], 1)

                def softmax_scores(c, s, half):
                    n = 2 * c + half + 1
                    a = slice(4 * half, 4 * half + 4)
                    dve.wait_ge(S["s_mm"], n)
                    nc.vector.scalar_tensor_tensor(sc[:, a, :], ATT.rearrange("p (a k) -> p a k", a=4), AD ** -0.5,
                                                   wm[s][:, :].unsqueeze(1).broadcast_to([P, 4, 2 * P]),
                                                   ALU.mult, ALU.add).then_inc(S["mask"], 1)

                def softmax_max(c, half):
                    n = 2 * c + half + 1
                    a = slice(4 * half, 4 * half + 4)
                    dve.wait_ge(S["mask"], n)
                    nc.vector.tensor_reduce(mx[:, 0, a], sc[:, a, :], AX, ALU.max).then_inc(S["max"], 1)
                    dve.wait_ge(S["max"], n)
                    nc.vector.tensor_tensor(mx[:, 0, a], mx[:, 0, a], sinks[:, a], ALU.max).then_inc(S["mx"], 1)
                    dve.wait_ge(S["mx"], n)
                    nc.vector.tensor_tensor(mx[:, 2, a], sinks[:, a], mx[:, 0, a], ALU.subtract)
                    nc.vector.tensor_scalar(mx[:, 1, a], mx[:, 0, a], -1.0, None, ALU.mult).then_inc(S["nmx"], 1)

                def layer_norm(c, i, s):
                    dve.wait_ge(S["proj"], c + 1)
                    dve.wait_ge(tile_in[s][5], 16 * (i + 1))
                    dve.wait_ge(x1_out, 16 * c)
                    for n in range(2):
                        nc.vector.scalar_tensor_tensor(h1[:, n * HALF:(n + 1) * HALF],
                                                       xt[s][:, n * HALF:(n + 1) * HALF], ALPHA, psum[:, 6 + n, :],
                                                       ALU.mult, ALU.add).then_inc(S["h1"], 1)
                    for n in range(2):
                        dve.wait_ge(S["h1"], 2 * c + n + 1)
                        nc.vector.bn_stats(st[:, n, :], h1[:, n * HALF:(n + 1) * HALF]).then_inc(S["stat"], 1)
                    wait_apart(dve, tick, S["stat"], 2 * (c + 1))
                    nc.vector.bn_aggr(mv[:, 0:2], st[:]).then_inc(S["aggr"], 1)

                def normalize(c):
                    dve.wait_ge(S["root"], c + 1)
                    nc.vector.reciprocal(mv[:, 3:4], mv[:, 2:3]).then_inc(S["rstd"], 1)
                    dve.wait_ge(S["rstd"], c + 1)
                    nc.vector.tensor_scalar(h1[:], h1[:], mv[:, 0:1], mv[:, 3:4], ALU.subtract,
                                            ALU.mult).then_inc(S["nrm"], 1)

                def split_wout(k):
                    dve.wait_ge(wout_hi, k + 1)
                    nc.vector.tensor_tensor(wout[1][:, k, :], wout_raw[k % 2][:], wout[0][:, k, :].bitcast(F32),
                                            ALU.subtract).then_inc(wout_lo, 1)

                def body(c, i, s, before, after):
                    now = c + 1
                    dve.wait_ge(tile_in[s][4], 16 * (i + 1))
                    dve.wait_ge(S["tr"], now)
                    nc.vector.tensor_tensor(kd[:], bank(2), per_head("kdec", c), ALU.mult)
                    nc.vector.tensor_tensor(vb[:], bank(3), per_head("beta", c), ALU.mult).then_inc(S["kd"], 1)
                    softmax_scores(c, s, 0)
                    for n in range(LV):
                        dve.wait_ge(lx, c * LV + n + 1)
                        level = cst[:, C_LEVEL + (n + 1) * P:C_LEVEL + (n + 2) * P]
                        nc.vector.tensor_tensor(xs[:], bank(0), heads(level), ALU.mult).then_inc(lm, 1)
                        if after and n == 0:
                            ahead(c + 1, i + s, 1 - s, 0)
                        if after and n == 2:
                            ahead(c + 1, i + s, 1 - s, 3)
                        if n < LV - 1:
                            dve.wait_ge(lt, c * (LV - 1) + n + 1)
                            nc.vector.tensor_tensor(tu[:, 0], tu[:, 0], bank(2), ALU.add).then_inc(la, 1)
                        if n == 4:
                            softmax_max(c, 1)
                        if n == 5:
                            dve.wait_ge(S["st_up"], c)
                            nc.vector.tensor_tensor(faded[:], state[:], per_head("decay", c),
                                                    ALU.mult).then_inc(S["decayed"], 1)
                        dve.wait_ge(lu, c * LV + n + 1)
                        nc.vector.tensor_tensor(tu[:, 1], tu[:, 1], bank(3), ALU.add).then_inc(lb, 1)
                        if n == 0:
                            softmax_max(c, 0)
                        if n == 3:
                            softmax_scores(c, s, 1)
                        if after and n in (0, 1, 2, 4):
                            ahead(c + 1, i + s, 1 - s, {0: 1, 1: 2, 2: 4, 4: 5}[n])
                        if not before and n:
                            split_wout(n - 1)
                    dve.wait_ge(S["ks"], now)
                    nc.vector.tensor_tensor(xs[:], bank(0), per_head("nbeg", c), ALU.mult).then_inc(S["kb"], 1)
                    dve.wait_ge(S["kb"], now)
                    nc.vector.tensor_tensor(vb[:], vb[:], xs[:], ALU.add).then_inc(S["r2"], 1)
                    if not before:
                        split_wout(LV - 1)
                    if before:
                        layer_norm(c - 1, i - 1 + s, 1 - s)
                    if after:
                        begin_inverse(c + 1)
                    dve.wait_ge(S["ods"], now)
                    dve.wait_ge(S["decayed"], now)
                    nc.vector.tensor_tensor(state[:], faded[:], bank(3), ALU.add).then_inc(S["st_up"], 1)
                    if not before:
                        for k in range(LV, KC):
                            split_wout(k)
                    dve.wait_ge(S["osq"], now)
                    nc.vector.tensor_reduce(rms[:, 0, :], og[:], AX, ALU.add).then_inc(S["osum"], 1)
                    nc.vector.tensor_tensor(mx[:, 3, :], mx[:, 3, :], mx[:, 2, :], ALU.add).then_inc(S["den"], 1)
                    dve.wait_ge(S["den"], now)
                    nc.vector.reciprocal(mx[:, 3, :], mx[:, 3, :]).then_inc(S["rec"], 1)
                    dve.wait_ge(S["oroot"], now)
                    nc.vector.reciprocal(rms[:, 1, :], rms[:, 0, :]).then_inc(S["orms"], 1)
                    dve.wait_ge(S["orms"], now)
                    dve.wait_ge(tile_in[s][3], 16 * (i + 1))
                    for h in range(GH):
                        last = nc.vector.scalar_tensor_tensor(og[:, h, :], bank(2)[:, h, :], rms[:, 1, h:h + 1],
                                                              zw[s][:, h, :], ALU.mult, ALU.mult)
                    last.then_inc(S["og"], 1)
                    dve.wait_ge(S["rec"], now)
                    dve.wait_ge(S["o_mm"], now)
                    nc.vector.tensor_tensor(on[:], psum[:, 4, :].rearrange("p (a d) -> p a d", a=AH),
                                            mx[:, 3, :].unsqueeze(2).broadcast_to([P, AH, AD]),
                                            ALU.mult).then_inc(S["o_n"], 1)
                    if before:
                        normalize(c - 1)
                    for name, b, k in (("mg", 1, 0), ("ma", 5, GH)):
                        dve.wait_ge(S[name], now)
                        nc.vector.tensor_tensor(mixT[s][1][:, k:k + GH, :], bank(b), mixT[s][0][:, k:k + GH, :].bitcast(F32),
                                                ALU.subtract).then_inc(S[name + "_lo"], 1)

                for step in range(6):
                    ahead(0, 0, 0, step)
                begin_inverse(0)
                tiles(dve, body)
                layer_norm(last_tile, NT // 2 - 1, last_tile % 2)
                normalize(last_tile)

            @block.gpsimd
            def _(pool):
                pool.wait_ge(ln_in, 32)
                with pool.Fori(0, NT) as c:
                    pool.wait_ge(S["nrm"], c + 1)
                    nc.gpsimd.tensor_tensor(h1[:], h1[:], lng[:], ALU.mult).then_inc(S["nrm_g"], 1)
                    pool.wait_ge(S["nrm_g"], c + 1)
                    nc.gpsimd.tensor_tensor(h1[:], h1[:], lnb[:], ALU.add).then_inc(S["x1"], 1)


def split_x1(nc, sem, scr, cst, psum, x1h, x1l):
    with ExitStack() as ctx:
        xt = [ctx.enter_context(nc.sbuf_tensor(f"t_x{t}", [P, D], F32)) for t in range(NT)]
        x_in = [sem(f"t_in{t}") for t in range(NT)]
        tr = [sem(f"t_tr{s}") for s in range(2)]
        hi = [sem(f"t_hi{s}") for s in range(2)]
        lo = [sem(f"t_lo{s}") for s in range(2)]
        ps = [psum[:, 2 * s:2 * s + 2, :].rearrange("p b (k t) -> p (b k) t", t=P) for s in range(2)]
        with nc.Block() as block:
            @block.sync
            def _(sp):
                for t in range(NT):
                    sp.dma_start(xt[t][:], scr["x1"][t * P:(t + 1) * P, :]).then_inc(x_in[t], 16)

            @block.tensor
            def _(pe):
                for t in range(NT):
                    s = t % 2
                    pe.wait_ge(x_in[t], 16)
                    pe.wait_ge(lo[s], t // 2)
                    for k in range(KC):
                        last = nc.tensor.transpose(ps[s][:, k, :], xt[t][:, k * P:(k + 1) * P], cst[:, C_ID:C_ID + P])
                    last.then_inc(tr[s], 1)

            @block.scalar
            def _(act):
                with act.Fori(0, NT // 2) as i:
                    for s in range(2):
                        act.wait_ge(tr[s], i + 1)
                        nc.scalar.activation(x1h[:, :, ts((2 * i + s) * P, P)], ps[s], ACT.Copy).then_inc(hi[s], 1)

            @block.vector
            def _(dve):
                with dve.Fori(0, NT // 2) as i:
                    for s in range(2):
                        dve.wait_ge(hi[s], i + 1)
                        nc.vector.tensor_tensor(x1l[:, :, ts((2 * i + s) * P, P)], ps[s],
                                                x1h[:, :, ts((2 * i + s) * P, P)].bitcast(F32),
                                                ALU.subtract).then_inc(lo[s], 1)


def retrieve(nc, sem, io, scr, cst, psum, x1h, x1l, key1, key2, gate):
    with ExitStack() as ctx:
        def sb(name, shape, dt=F32):
            return ctx.enter_context(nc.sbuf_tensor(name, shape, dt))

        wr = [sb(f"r_w{s}", [P, KC, P]) for s in range(2)]
        wh = [sb(f"r_wh{s}", [P, KC, P], F32R) for s in range(2)]
        wl = [sb(f"r_wl{s}", [P, KC, P], F32R) for s in range(2)]
        qT = [sb(f"r_qT{s}", [P, T]) for s in range(2)]
        kk = [sb(f"r_kk{s}", [P, NK]) for s in range(2)]
        sc = [sb(f"r_sc{s}", [P, NT, NK]) for s in range(2)]
        rest = sb("r_rest", [P, NT, NK])
        top = [sb(f"r_top{s}", [P, NT, TOPK]) for s in range(2)]
        idx = [sb(f"r_idx{s}", [P, NT, TOPK], U32) for s in range(2)]
        idf = [[sb(f"r_idf{v}{s}", [P, NT, TOPK]) for s in range(2)] for v in range(2)]
        cand = sb("r_cand", [P, NT, TOPK * TOPK])
        crest = sb("r_crest", [P, NT, TOPK * TOPK])
        best = sb("r_best", [P, NT, TOPK])
        ex = sb("r_ex", [P, NT, TOPK])
        pos = sb("r_pos", [P, NT, TOPK], U32)
        pab = [sb(f"r_pab{s}", [P, NT, TOPK], U32) for s in range(2)]
        pf = [[sb(f"r_pf{v}{s}", [P, NT, TOPK]) for s in range(2)] for v in range(2)]
        gsum = sb("r_gsum", [P, NT])
        pick = [sb(f"r_pick{s}", [P, NT, TOPK, TOPK]) for s in range(2)]
        ur = sb("r_ur", [P, KC, P])
        uh = [sb(f"r_uh{v}", [P, KC, P], F32R) for v in range(2)]
        ul = [sb(f"r_ul{v}", [P, KC, P], F32R) for v in range(2)]
        act_out = [sb(f"r_gelu{n}", [P, HALF]) for n in range(2)]
        q_ps = [psum[:, 2 * s:2 * s + 2, :] for s in range(2)]
        s_ps = psum[:, 4:6, :]

        tick = sem("r_tick")
        w_in = [sem(f"r_w_in{s}") for s in range(2)]
        w_hi = [sem(f"r_w_hi{s}") for s in range(2)]
        w_lo = [sem(f"r_w_lo{s}") for s in range(2)]
        q_mm = [sem(f"r_q_mm{s}") for s in range(2)]
        q_ev = [sem(f"r_q_ev{s}") for s in range(2)]
        s_mm = [sem(f"r_s_mm{s}") for s in range(2)]
        s_ev = [sem(f"r_s_ev{s}") for s in range(2)]
        u_in, u_hi, u_lo = sem("r_u_in"), sem("r_u_hi"), sem("r_u_lo")
        h_mm = [sem(f"r_h_mm{n}") for n in range(2)]
        gelu = [sem(f"r_gelu{n}") for n in range(2)]
        h_out = [sem(f"r_h_out{n}") for n in range(2)]
        kk_in = [sem(f"r_kk{s}") for s in range(2)]
        half_done = [sem(f"r_half{s}") for s in range(2)]
        mx1, mi1, mr, mx2 = sem("r_max1"), sem("r_index1"), sem("r_replace"), sem("r_max2")
        c_new, c1, c2, c3, c4, c5 = (sem(f"r_cand{n}") for n in range(6))
        g_sub, g_exp, g_sum, g_rec, g_out = (sem(f"r_gate{n}") for n in range(5))
        p_bits = sem("r_bits")
        p_ready = [sem(f"r_pos_ready{v}") for v in range(2)]
        pool_step = sem("r_pick_step")
        last_step = sem("r_last_step")
        p_square = sem("r_pick_square")
        p_diff = [sem(f"r_pick_diff{s}") for s in range(2)]
        p_match = [sem(f"r_pick_match{s}") for s in range(2)]
        picked_all = [sem(f"r_picked{v}") for v in range(2)]

        with nc.Block() as block:
            @block.sync
            def _(sp):
                def load_u(b):
                    sp.wait_ge(u_lo, b)
                    sp.dma_start(ur[:], io["uT"][b]).then_inc(u_in, 16)

                def store_hidden(b):
                    for n in range(2):
                        sp.wait_ge(gelu[n], b + 1)
                        sp.dma_start(scr["hidden"][ts(b, 1), :, n * HALF:(n + 1) * HALF].rearrange("a p t -> (a p) t"),
                                     act_out[n][:]).then_inc(h_out[n], 16)

                def head(h):
                    for s in range(2):
                        sp.wait_ge(w_lo[s], h)
                        sp.dma_start(wr[s][:], io["wq"][2 * h + s]).then_inc(w_in[s], 16)
                    load_u(h)
                    for s in range(2):
                        sp.wait_ge(s_mm[s], h)
                        sp.dma_start(kk[s][:], io["keysT"][2 * h + s]).then_inc(kk_in[s], 16)

                head(0)
                with sp.Fori(1, PH) as h:
                    head(h)
                    store_hidden(h - 1)
                load_u(PH)
                store_hidden(PH - 1)
                for b in range(PH + 1, AHEAD_R):
                    load_u(b)
                    if b > PH + 1:
                        store_hidden(b - 2)
                for b in range(AHEAD_R - 2, AHEAD_R):
                    store_hidden(b)
                for n in range(2):
                    sp.wait_ge(h_out[n], 16 * AHEAD_R)

            @block.tensor
            def _(pe):
                def query(h, s):
                    pe.wait_ge(w_hi[s], h + 1)
                    pe.wait_ge(w_lo[s], h + 1)
                    pe.wait_ge(q_ev[s], h)
                    for n in range(2):
                        for k in range(KC):
                            c = slice(n * HALF, (n + 1) * HALF)
                            nc.tensor.matmul(q_ps[s][:, n, :], wh[s][:, k, :], x1h[:, k, c],
                                             start=(k == 0), stop=False)
                            nc.tensor.matmul(q_ps[s][:, n, :], wh[s][:, k, :], x1l[:, k, c],
                                             start=False, stop=False)
                            last = nc.tensor.matmul(q_ps[s][:, n, :], wl[s][:, k, :], x1h[:, k, c],
                                                    start=False, stop=(k == KC - 1))
                    last.then_inc(q_mm[s], 1)

                def hidden(b, v, n):
                    pe.wait_ge(u_hi, b + 1)
                    pe.wait_ge(u_lo, b + 1)
                    pe.wait_ge(gelu[n], b)
                    c = slice(n * HALF, (n + 1) * HALF)
                    for k in range(KC):
                        nc.tensor.matmul(psum[:, 6 + n, :], uh[v][:, k, :], x1h[:, k, c], start=(k == 0), stop=False)
                        nc.tensor.matmul(psum[:, 6 + n, :], uh[v][:, k, :], x1l[:, k, c], start=False, stop=False)
                        last = nc.tensor.matmul(psum[:, 6 + n, :], ul[v][:, k, :], x1h[:, k, c], start=False,
                                                stop=(k == KC - 1))
                    last.then_inc(h_mm[n], 1)

                def score(h, s):
                    pe.wait_ge(q_ev[s], h + 1)
                    pe.wait_ge(kk_in[s], 16 * (h + 1))
                    pe.wait_ge(s_ev[1 - s], h + s)
                    for t in range(NT):
                        last = nc.tensor.matmul(s_ps[:, t // 4, (t % 4) * P:(t % 4 + 1) * P],
                                                qT[s][:, t * P:(t + 1) * P], kk[s][:], start=True, stop=True)
                    last.then_inc(s_mm[s], 1)

                with pe.Fori(0, PH // 2) as i:
                    for v in range(2):
                        h = 2 * i + v
                        query(h, 0)
                        query(h, 1)
                        hidden(h, v, 0)
                        score(h, 0)
                        hidden(h, v, 1)
                        score(h, 1)
                for b in range(PH, AHEAD_R):
                    for n in range(2):
                        hidden(b, b % 2, n)

            @block.scalar
            def _(act):
                def weights(h):
                    for s in range(2):
                        act.wait_ge(w_in[s], 16 * (h + 1))
                        act.wait_ge(q_mm[s], h)
                        nc.scalar.activation(wh[s][:], wr[s][:], ACT.Copy).then_inc(w_hi[s], 1)

                def split_u(b, v):
                    act.wait_ge(u_in, 16 * (b + 1))
                    if not isinstance(b, int) or b >= 2:
                        act.wait_ge(h_mm[1], b - 1)
                    nc.scalar.activation(uh[v][:], ur[:], ACT.Copy).then_inc(u_hi, 1)

                def activate(b, n):
                    act.wait_ge(h_mm[n], b + 1)
                    act.wait_ge(h_out[n], 16 * b)
                    nc.scalar.activation(act_out[n][:], psum[:, 6 + n, :], ACT.Gelu).then_inc(gelu[n], 1)

                def scores(h, v, more=True):
                    for s in range(2):
                        act.wait_ge(q_mm[s], h + 1)
                        act.wait_ge(s_mm[s], h)
                        nc.scalar.activation(qT[s][:], q_ps[s].rearrange("p b t -> p (b t)"), ACT.Copy).then_inc(q_ev[s], 1)
                    if more:
                        weights(h + 1)
                    split_u(h + 1, 1 - v)
                    for s in range(2):
                        activate(h, s)
                        act.wait_ge(s_mm[s], h + 1)
                        act.wait_ge(half_done[s], h)
                        nc.scalar.activation(sc[s].rearrange("p t n -> p (t n)"),
                                             s_ps.rearrange("p b n -> p (b n)"), ACT.Copy).then_inc(s_ev[s], 1)

                def picks(h):
                    for s in range(2):
                        act.wait_ge(p_diff[s], h + 1)
                        nc.scalar.activation(pick[s][:], pick[s][:], ACT.Square).then_inc(p_square, 1)
                        act.wait_ge(p_square, 2 * h + s + 1)
                        nc.scalar.activation(pick[s][:], pick[s][:], ACT.Relu, scale=-1.0,
                                             bias=cst[:, C_ONES:C_ONES + 1]).then_inc(p_match[s], 1)

                def gates(h):
                    act.wait_ge(g_sub, h + 1)
                    nc.scalar.activation(ex[:], ex[:], ACT.Exp).then_inc(g_exp, 1)

                weights(0)
                split_u(0, 0)
                scores(0, 0)
                scores(1, 1)
                gates(0)

                def steady(h, v, more=True):
                    picks(h - 1)
                    scores(h + 1, v, more)
                    gates(h)

                with act.Fori(0, PH // 2 - 2) as i:
                    steady(2 * i + 1, 0)
                    steady(2 * i + 2, 1)
                steady(PH - 3, 0)
                steady(PH - 2, 1, more=False)
                split_u(PH + 1, 1)
                picks(PH - 2)
                for n in range(2):
                    activate(PH, n)
                split_u(PH + 2, 0)
                for n in range(2):
                    activate(PH + 1, n)
                gates(PH - 1)
                split_u(PH + 3, 1)
                for n in range(2):
                    activate(PH + 2, n)
                picks(PH - 1)
                for n in range(2):
                    activate(PH + 3, n)

            @block.vector
            def _(dve):
                def split_u(b, v):
                    dve.wait_ge(u_hi, b + 1)
                    nc.vector.tensor_tensor(ul[v][:], ur[:], uh[v][:].bitcast(F32), ALU.subtract).then_inc(u_lo, 1)

                def head(i, v, more=True):
                    h = 2 * i + v
                    for s in range(2):
                        n = 2 * h + s
                        wait_apart(dve, tick, s_ev[s], h + 1)
                        for t in range(NT):
                            last = nc.vector.max(top[s][:, t, 0:8], sc[s][:, t, :])
                        last.then_inc(mx1, 1)
                        wait_apart(dve, tick, mx1, n + 1)
                        for t in range(NT):
                            last = nc.vector.match_replace(rest[:, t, :], top[s][:, t, 0:8], sc[s][:, t, :], REPLACED)
                        last.then_inc(mr, 1)
                        for t in range(NT):
                            last = nc.vector.max_index(idx[s][:, t, 0:8], top[s][:, t, 0:8], sc[s][:, t, :])
                        last.then_inc(half_done[s], 1)
                        wait_apart(dve, tick, mr, n + 1)
                        for t in range(NT):
                            last = nc.vector.max(top[s][:, t, 8:16], rest[:, t, :])
                        last.then_inc(mx2, 1)
                        wait_apart(dve, tick, mx2, n + 1)
                        for t in range(NT):
                            last = nc.vector.max_index(idx[s][:, t, 8:16], top[s][:, t, 8:16], rest[:, t, :])
                        last.then_inc(mi1, 1)
                    dve.wait_ge(mi1, 2 * h + 2)
                    dve.wait_ge(picked_all[v], i)
                    for s in range(2):
                        nc.vector.tensor_copy(idf[v][s][:], idx[s][:])
                    nc.vector.tensor_tensor(cand.rearrange("p t (a b) -> p t a b", a=TOPK),
                                            top[0][:, :, :].unsqueeze(3).broadcast_to([P, NT, TOPK, TOPK]),
                                            top[1][:, :, :].unsqueeze(2).broadcast_to([P, NT, TOPK, TOPK]),
                                            ALU.add).then_inc(c_new, 1)
                    dve.wait_ge(c_new, h + 1)
                    wait_apart(dve, tick, g_out, h)
                    for t in range(NT):
                        last = nc.vector.max(best[:, t, 0:8], cand[:, t, :])
                    last.then_inc(c1, 1)
                    if more:
                        split_u(h + 2, v)
                    wait_apart(dve, tick, c1, h + 1)
                    for t in range(NT):
                        last = nc.vector.match_replace(crest[:, t, :], best[:, t, 0:8], cand[:, t, :], REPLACED)
                    last.then_inc(c2, 1)
                    for t in range(NT):
                        nc.vector.max_index(pos[:, t, 0:8], best[:, t, 0:8], cand[:, t, :])
                    wait_apart(dve, tick, c2, h + 1)
                    for t in range(NT):
                        last = nc.vector.max(best[:, t, 8:16], crest[:, t, :])
                    last.then_inc(c3, 1)
                    wait_apart(dve, tick, c3, h + 1)
                    for t in range(NT):
                        last = nc.vector.max_index(pos[:, t, 8:16], best[:, t, 8:16], crest[:, t, :])
                    last.then_inc(c4, 1)
                    dve.wait_ge(c4, h + 1)
                    nc.vector.tensor_scalar(pab[0][:], pos[:], 4, None, ALU.logical_shift_right)
                    nc.vector.tensor_scalar(pab[1][:], pos[:], 15, None, ALU.bitwise_and).then_inc(p_bits, 1)
                    nc.vector.tensor_tensor(ex[:], best[:], best[:, :, 0:1].broadcast_to([P, NT, TOPK]),
                                            ALU.subtract).then_inc(g_sub, 1)
                    dve.wait_ge(p_bits, h + 1)
                    nc.vector.tensor_copy(pf[v][0][:], pab[0][:])
                    nc.vector.tensor_copy(pf[v][1][:], pab[1][:]).then_inc(p_ready[v], 1)
                    dve.wait_ge(g_exp, h + 1)
                    nc.vector.tensor_reduce(gsum[:], ex[:], AX, ALU.add).then_inc(g_sum, 1)
                    dve.wait_ge(g_sum, h + 1)
                    nc.vector.reciprocal(gsum[:], gsum[:]).then_inc(g_rec, 1)
                    dve.wait_ge(g_rec, h + 1)
                    nc.vector.tensor_tensor(gate[:, :, ts(h * TOPK, TOPK)], ex[:],
                                            gsum[:, :].unsqueeze(2).broadcast_to([P, NT, TOPK]),
                                            ALU.mult).then_inc(g_out, 1)

                split_u(1, 1)
                with dve.Fori(0, PH // 2 - 1) as i:
                    for v in range(2):
                        head(i, v)
                head(PH // 2 - 1, 0)
                head(PH // 2 - 1, 1, more=False)
                flat = pick[1].rearrange("p t k j -> p (t k) j")
                dve.wait_ge(p_ready[1], PH // 2)
                dve.wait_ge(picked_all[0], PH // 2)
                nc.vector.tensor_tensor(
                    flat, pf[1][1].rearrange("p t k -> p (t k)").unsqueeze(2).broadcast_to([P, NT * TOPK, TOPK]),
                    cst[:, C_IOTA16:C_IOTA16 + TOPK].unsqueeze(1).broadcast_to([P, NT * TOPK, TOPK]),
                    ALU.subtract).then_inc(p_diff[1], 1)
                split_u(AHEAD_R - 1, 1)
                dve.wait_ge(p_match[1], PH)
                nc.vector.tensor_tensor(pick[1][:], pick[1][:],
                                        idf[1][1][:, :, :].unsqueeze(2).broadcast_to([P, NT, TOPK, TOPK]),
                                        ALU.mult).then_inc(last_step, 1)
                for step, n in enumerate((8, 4, 2)):
                    dve.wait_ge(last_step, step + 1)
                    nc.vector.tensor_tensor(flat[:, :, 0:n], flat[:, :, 0:n], flat[:, :, n:2 * n],
                                            ALU.add).then_inc(last_step, 1)
                dve.wait_ge(last_step, 4)
                nc.vector.tensor_tensor(key2[:, :, (PH - 1) * TOPK:], pick[1][:, :, :, 0], pick[1][:, :, :, 1], ALU.add)

            @block.gpsimd
            def _(pool):
                def weights(h):
                    for s in range(2):
                        pool.wait_ge(w_hi[s], h + 1)
                        nc.gpsimd.tensor_tensor(wl[s][:], wr[s][:], wh[s][:].bitcast(F32), ALU.subtract).then_inc(w_lo[s], 1)

                def split_u(b, v):
                    pool.wait_ge(u_hi, b + 1)
                    nc.gpsimd.tensor_tensor(ul[v][:], ur[:], uh[v][:].bitcast(F32), ALU.subtract).then_inc(u_lo, 1)

                def picks(h, v, i, halves=2):
                    ranks = cst[:, C_IOTA16:C_IOTA16 + TOPK].unsqueeze(1).broadcast_to([P, NT * TOPK, TOPK])
                    pool.wait_ge(p_ready[v], i + 1)
                    pool.wait_ge(pool_step, 10 * h)
                    for s in range(halves):
                        nc.gpsimd.tensor_tensor(
                            pick[s].rearrange("p t k j -> p (t k) j"),
                            pf[v][s].rearrange("p t k -> p (t k)").unsqueeze(2).broadcast_to([P, NT * TOPK, TOPK]),
                            ranks, ALU.subtract).then_inc(p_diff[s], 1)
                    for s, dst in enumerate((key1, key2)[:halves]):
                        n = 10 * h + 5 * s
                        flat = pick[s].rearrange("p t k j -> p (t k) j")
                        pool.wait_ge(p_match[s], h + 1)
                        nc.gpsimd.tensor_tensor(pick[s][:], pick[s][:],
                                                idf[v][s][:, :, :].unsqueeze(2).broadcast_to([P, NT, TOPK, TOPK]),
                                                ALU.mult).then_inc(pool_step, 1)
                        pool.wait_ge(pool_step, n + 1)
                        for step, m in enumerate((8, 4, 2)):
                            nc.gpsimd.tensor_tensor(flat[:, :, 0:m], flat[:, :, 0:m], flat[:, :, m:2 * m],
                                                    ALU.add).then_inc(pool_step, 1)
                            pool.wait_ge(pool_step, n + 2 + step)
                        nc.gpsimd.tensor_tensor(dst[:, :, ts(h * TOPK, TOPK)], pick[s][:, :, :, 0],
                                                pick[s][:, :, :, 1], ALU.add).then_inc(pool_step, 1)
                    pool.wait_ge(pool_step, 10 * h + 5 * halves)
                    pool.sem_inc(picked_all[v], 1)

                weights(0)
                split_u(0, 0)
                weights(1)
                with pool.Fori(0, PH // 2 - 1) as i:
                    for v in range(2):
                        weights(2 * i + v + 2)
                        picks(2 * i + v, v, i)
                split_u(PH + 1, 1)
                picks(PH - 2, 0, PH // 2 - 1)
                split_u(PH + 2, 0)
                picks(PH - 1, 1, PH // 2 - 1, halves=1)


def build_gates(nc, sem, io, scr, cst, psum, x1h, x1l, key1, key2, gate):
    with ExitStack() as ctx:
        def sb(name, shape, dt=F32):
            return ctx.enter_context(nc.sbuf_tensor(name, shape, dt))

        R = 16
        pickT = sb("g_pickT", [P, 3, T])
        one1 = [sb(f"g_one{s}", [P, R, NK]) for s in range(2)]
        one2 = [sb(f"g_two{s}", [P, R, NK]) for s in range(2)]
        gt = [sb(f"g_tile{s}", [P, NK, TG]) for s in range(2)]
        iota = cst[:, C_IOTA:C_IOTA + NK].unsqueeze(1).broadcast_to([P, R, NK])
        ur = sb("g_ur", [P, KC, P])
        uh = sb("g_uh", [P, KC, P], F32R)
        ul = sb("g_ul", [P, KC, P], F32R)
        act_out = [sb(f"g_gelu{n}", [P, HALF]) for n in range(2)]
        u_in, u_hi, u_lo = sem("g_u_in"), sem("g_u_hi"), sem("g_u_lo")
        h_mm = [sem(f"g_h_mm{n}") for n in range(2)]
        gelu = [sem(f"g_gelu{n}") for n in range(2)]
        h_out = [sem(f"g_h_out{n}") for n in range(2)]
        PAIRS = 2 * TG // (2 * R)
        tr, tr_ev = sem("g_tr"), sem("g_tr_ev")
        hot1 = [sem(f"g_hot1{s}") for s in range(2)]
        hot2 = [sem(f"g_hot2{s}") for s in range(2)]
        gated = [sem(f"g_gated{s}") for s in range(2)]
        mm = [sem(f"g_mm{s}") for s in range(2)]
        evac = [sem(f"g_evac{n}") for n in range(4)]
        stored = [sem(f"g_stored{s}") for s in range(2)]

        def picks_of(n, t):
            return pickT[:, n, ts(t, R)].unsqueeze(2).broadcast_to([P, R, NK])

        with nc.Block() as block:
            @block.tensor
            def _(pe):
                for t in range(NT):
                    if t >= 2:
                        pe.wait_ge(tr_ev, t - 1)
                    for n, src in enumerate((key1, key2, gate)):
                        last = nc.tensor.transpose(psum[:, t % 2, n * P:(n + 1) * P], src[:, t, :], cst[:, C_ID:C_ID + P])
                    last.then_inc(tr, 1)
                pe.wait_ge(tr_ev, NT)
                with pe.Fori(0, AHEAD_G) as i:
                    for r in range(PAIRS):
                        for s in range(2):
                            pair = PAIRS * i + r
                            pe.wait_ge(hot1[s], pair + 1)
                            pe.wait_ge(gated[s], pair + 1)
                            for n in range(R):
                                if n % 4 == 0:
                                    pe.wait_ge(evac[n // 4], 2 * pair + s)
                                last = nc.tensor.matmul(psum[:, n // 4, (n % 4) * NK:(n % 4 + 1) * NK],
                                                        one2[s][:, n, :], one1[s][:, n, :], start=True, stop=True)
                                if n % 4 == 3:
                                    last.then_inc(mm[s], 1)
                        n, first = r // 2, r % 2 * (KC // 2)
                        if r == 0:
                            pe.wait_ge(u_hi, i + 1)
                            pe.wait_ge(u_lo, i + 1)
                        if first == 0:
                            pe.wait_ge(gelu[n], i)
                        c = slice(n * HALF, (n + 1) * HALF)
                        for k in range(first, first + KC // 2):
                            nc.tensor.matmul(psum[:, 6 + n, :], uh[:, k, :], x1h[:, k, c], start=(k == 0), stop=False)
                            nc.tensor.matmul(psum[:, 6 + n, :], uh[:, k, :], x1l[:, k, c], start=False, stop=False)
                            last = nc.tensor.matmul(psum[:, 6 + n, :], ul[:, k, :], x1h[:, k, c], start=False,
                                                    stop=(k == KC - 1))
                        if first:
                            last.then_inc(h_mm[n], 1)

            @block.vector
            def _(dve):
                dve.wait_ge(tr_ev, NT)
                with dve.Fori(0, T // R // 2) as i:
                    for s in range(2):
                        t = (2 * i + s) * R
                        dve.wait_ge(mm[s], 4 * i)
                        nc.vector.tensor_tensor(one2[s][:], iota, picks_of(1, t), ALU.is_equal).then_inc(hot2[s], 1)
                        nc.vector.tensor_tensor(one1[s][:], iota, picks_of(0, t), ALU.is_equal).then_inc(hot1[s], 1)

            @block.gpsimd
            def _(pool):
                with pool.Fori(0, AHEAD_G) as i:
                    for r in range(PAIRS):
                        for s in range(2):
                            pair = PAIRS * i + r
                            pool.wait_ge(hot2[s], pair + 1)
                            nc.gpsimd.tensor_tensor(one2[s][:], one2[s][:], picks_of(2, (2 * pair + s) * R),
                                                    ALU.mult).then_inc(gated[s], 1)
                        if r == 0:
                            pool.wait_ge(u_hi, i + 1)
                            nc.gpsimd.tensor_tensor(ul[:], ur[:], uh[:].bitcast(F32), ALU.subtract).then_inc(u_lo, 1)

            @block.scalar
            def _(act):
                for t in range(NT):
                    act.wait_ge(tr, t + 1)
                    nc.scalar.activation(pickT[:, :, t * P:(t + 1) * P],
                                         psum[:, t % 2, 0:3 * P].rearrange("p (n t) -> p n t", n=3),
                                         ACT.Copy).then_inc(tr_ev, 1)
                with act.Fori(0, T // TG // 2) as i:
                    act.wait_ge(u_in, 16 * (i + 1))
                    act.wait_ge(h_mm[1], i)
                    nc.scalar.activation(uh[:], ur[:], ACT.Copy).then_inc(u_hi, 1)
                    for b in range(2):
                        act.wait_ge(stored[b], 16 * i)
                        for r in range(TG // R):
                            s = r % 2
                            for n in range(4):
                                act.wait_ge(mm[s], ((2 * i + b) * (TG // R // 2) + r // 2) * 4 + n + 1)
                                nc.scalar.activation(gt[b][:, :, r * R + 4 * n:r * R + 4 * n + 4].rearrange("p k t -> p t k"),
                                                     psum[:, n, :].rearrange("p (t k) -> p t k", t=4),
                                                     ACT.Copy).then_inc(evac[n], 1)
                        act.wait_ge(h_mm[b], i + 1)
                        act.wait_ge(h_out[b], 16 * i)
                        nc.scalar.activation(act_out[b][:], psum[:, 6 + b, :], ACT.Gelu).then_inc(gelu[b], 1)

            @block.sync
            def _(sp):
                def stores(i, more):
                    if more:
                        sp.wait_ge(u_lo, i + 1)
                        sp.dma_start(ur[:], io["uT"][i + (AHEAD_R + 1)]).then_inc(u_in, 16)
                    for b in range(2):
                        sp.wait_ge(evac[3], (2 * i + b + 1) * (TG // R))
                        sp.dma_start(scr["G"][ts(2 * i + b, 1)].rearrange("a p k t -> (a p) k t"),
                                     gt[b][:]).then_inc(stored[b], 16)
                        sp.wait_ge(gelu[b], i + 1)
                        sp.dma_start(scr["hidden"][ts(i + AHEAD_R, 1), :, b * HALF:(b + 1) * HALF]
                                     .rearrange("a p t -> (a p) t"), act_out[b][:]).then_inc(h_out[b], 16)

                sp.dma_start(ur[:], io["uT"][AHEAD_R]).then_inc(u_in, 16)
                with sp.Fori(0, AHEAD_G - 1) as i:
                    stores(i, True)
                stores(AHEAD_G - 1, False)
                for b in range(2):
                    sp.wait_ge(stored[b], 16 * (T // TG // 2))
                    sp.wait_ge(h_out[b], 16 * AHEAD_G)


def experts(nc, sem, io, scr, cst, psum, x1h, x1l, y, out):
    with ExitStack() as ctx:
        def sb(name, shape, dt=F32):
            return ctx.enter_context(nc.sbuf_tensor(name, shape, dt))

        NG = NK // 2
        SHORT = AHEAD // 2
        ur = [sb(f"e_ur{j}", [P, KC, P]) for j in range(2)]
        vr = sb("e_vr", [P, D])
        uh = [sb(f"e_uh{j}", [P, KC, P], F32R) for j in range(2)]
        ul = [sb(f"e_ul{j}", [P, KC, P], F32R) for j in range(2)]
        vh = [[sb(f"e_vh{s}{j}", [P, D], F32R) for j in range(2)] for s in range(2)]
        vl = [[sb(f"e_vl{s}{j}", [P, D], F32R) for j in range(2)] for s in range(2)]
        ah = [[sb(f"e_ah{s}{j}", [P, T], F32R) for j in range(2)] for s in range(2)]
        al = [[sb(f"e_al{s}{j}", [P, T], F32R) for j in range(2)] for s in range(2)]
        gt = [sb(f"e_g{j}", [P, T // TG, TG]) for j in range(2)]
        av = [sb(f"e_a{n}", [P, HALF]) for n in range(2)]

        u_in = [sem(f"u_in{j}") for j in range(2)]
        v_in = [sem(f"v_in{j}") for j in range(2)]
        g_in = [sem(f"g_in{j}") for j in range(2)]
        u_hi = [sem(f"u_hi{j}") for j in range(2)]
        u_lo = [sem(f"u_lo{j}") for j in range(2)]
        v_hi = [sem(f"v_hi{j}") for j in range(2)]
        v_lo = [sem(f"v_lo{j}") for j in range(2)]
        h_mm = [[sem(f"h_mm{j}{n}") for n in range(2)] for j in range(2)]
        gelu = [[sem(f"gelu{j}{n}") for n in range(2)] for j in range(2)]
        a_mul = [[sem(f"a_mul{j}{n}") for n in range(2)] for j in range(2)]
        a_hi = [[sem(f"a_hi{j}{n}") for n in range(2)] for j in range(2)]
        a_lo = [[sem(f"a_lo{j}{n}") for n in range(2)] for j in range(2)]
        y_mm = sem("y_mm")
        y_add = [sem(f"y_add{b}") for b in range(4)]
        x1_in = sem("x1_in")
        y_ready = sem("y_ready")
        st = sb("f_st", [P, NT, 2, 6])
        mv = sb("f_mv", [P, NT, 2])
        root = sb("f_root", [P, NT])
        rstd = sb("f_rstd", [P, NT])
        shift = sb("f_shift", [P, NT])
        lng, lnb = (ur[j].rearrange("p k e -> p (k e)") for j in range(2))
        ln_in = 16 * (NG + 1)
        stored = sem("f_stored")
        stat, aggr, rooted, inverted, shifted, nrm, nrm_g, done = (
            sem(f"f_{n}") for n in "stat aggr rooted inverted shifted nrm nrm_g done".split())

        with nc.Block() as block:
            @block.sync
            def _(sp):
                def load_v(g, j):
                    sp.wait_ge(v_lo[1 - j], g + j)
                    sp.dma_start(vr[:], io["v"][ts((2 * g + j) * NK, NK), :]).then_inc(v_in[j], 16)

                def load_gates(g, j):
                    sp.wait_ge(a_mul[j][1], g)
                    sp.dma_start(gt[j][:], scr["G"][:, :, 2 * g + j, :].rearrange("t p q -> p t q")).then_inc(g_in[j], 16)

                def short_group(g):
                    for j in range(2):
                        load_gates(g, j)
                        sp.dma_start(ur[j].rearrange("p k e -> p (k e)"),
                                     scr["hidden"][2 * g + j]).then_inc(u_in[j], 16)
                    for j in range(2):
                        load_v(g, j)
                short_group(0)
                for t in range(NT):
                    sp.dma_start(y[:, t, :], scr["x1"][t * P:(t + 1) * P, :]).then_inc(x1_in, 16)
                with sp.Fori(1, SHORT) as g:
                    short_group(g)
                with sp.Fori(SHORT, NG) as g:
                    for j in range(2):
                        sp.wait_ge(u_lo[j], g - SHORT)
                        sp.wait_ge(a_mul[j][1], SHORT)
                        sp.dma_start(ur[j][:], io["uT"][2 * g + j]).then_inc(u_in[j], 16)
                        load_v(g, j)
                        load_gates(g, j)
                for j, src in enumerate(("ln2_g", "ln2_b")):
                    sp.wait_ge(u_lo[j], NG - SHORT)
                    sp.dma_start(ur[j].rearrange("p k e -> p (k e)"), io[src].partition_broadcast(P)).then_inc(u_in[j], 16)
                for t in range(NT):
                    sp.wait_ge(done, t + 1)
                    sp.dma_start(out[0, t * P:(t + 1) * P, :], y[:, t, :]).then_inc(stored, 16)
                sp.wait_ge(stored, 16 * NT)

            @block.tensor
            def _(pe):
                def hidden(g):
                    for j in range(2):
                        pe.wait_ge(u_hi[j], g - SHORT + 1)
                        pe.wait_ge(u_lo[j], g - SHORT + 1)
                        for n in range(2):
                            pe.wait_ge(gelu[j][n], g - SHORT)
                            out = psum[:, 2 * j + n, :]
                            c = slice(n * HALF, (n + 1) * HALF)
                            for k in range(KC):
                                nc.tensor.matmul(out, uh[j][:, k, :], x1h[:, k, c], start=(k == 0), stop=False)
                                nc.tensor.matmul(out, uh[j][:, k, :], x1l[:, k, c], start=False, stop=False)
                                last = nc.tensor.matmul(out, ul[j][:, k, :], x1h[:, k, c], start=False,
                                                        stop=(k == KC - 1))
                            last.then_inc(h_mm[j][n], 1)

                def values(g, s):
                    for j in range(2):
                        pe.wait_ge(v_hi[j], g + 1)
                        pe.wait_ge(v_lo[j], g + 1)
                        for n in range(2):
                            pe.wait_ge(a_lo[j][n], g + 1)
                    for q in range(2 * NT):
                        t, n = divmod(q, 2)
                        pe.wait_ge(y_add[q % 4], 4 * g + q // 4)
                        out = psum[:, 4 + q % 4, :]
                        c = slice(n * HALF, (n + 1) * HALF)
                        r = slice(t * P, (t + 1) * P)
                        for j in range(2):
                            nc.tensor.matmul(out, ah[s][j][:, r], vh[s][j][:, c], start=(j == 0), stop=False)
                            nc.tensor.matmul(out, ah[s][j][:, r], vl[s][j][:, c], start=False, stop=False)
                            last = nc.tensor.matmul(out, al[s][j][:, r], vh[s][j][:, c], start=False, stop=(j == 1))
                        last.then_inc(y_mm, 1)

                with pe.Fori(0, SHORT // 2) as i:
                    values(2 * i, 0)
                    values(2 * i + 1, 1)
                hidden(SHORT)
                with pe.Fori(SHORT // 2, (NG - 2) // 2) as i:
                    hidden(2 * i + 1)
                    values(2 * i, 0)
                    hidden(2 * i + 2)
                    values(2 * i + 1, 1)
                hidden(NG - 1)
                values(NG - 2, 0)
                values(NG - 1, 1)

            @block.scalar
            def _(act):
                def split_u(g, j):
                    act.wait_ge(u_in[j], 16 * (g + 1))
                    act.wait_ge(h_mm[j][1], g - SHORT)
                    nc.scalar.activation(uh[j][:], ur[j][:], ACT.Copy).then_inc(u_hi[j], 1)

                def split_v(g, s, j, used):
                    act.wait_ge(v_in[j], 16 * (g + 1))
                    act.wait_ge(y_mm, used)
                    nc.scalar.activation(vh[s][j][:], vr[:], ACT.Copy).then_inc(v_hi[j], 1)

                def split_a(g, s, j, used):
                    act.wait_ge(y_mm, used)
                    for n in range(2):
                        act.wait_ge(a_mul[j][n], g + 1)
                        nc.scalar.activation(ah[s][j][:, n * HALF:(n + 1) * HALF], av[n][:], ACT.Copy).then_inc(a_hi[j][n], 1)

                def activate(g, j):
                    for n in range(2):
                        act.wait_ge(h_mm[j][n], g - SHORT + 1)
                        if j == 1:
                            act.wait_ge(a_lo[0][n], g + 1)
                        else:
                            act.wait_ge(a_lo[1][n], g)
                        nc.scalar.activation(av[n][:], psum[:, 2 * j + n, :], ACT.Gelu).then_inc(gelu[j][n], 1)

                def short_group(g, s, used):
                    for j in range(2):
                        split_a(g, s, j, used)
                    for j in range(2):
                        split_v(g, s, j, used)

                def group(g, s, used, used_next, more=True):
                    for j in range(2):
                        activate(g, j)
                        split_a(g, s, j, used)
                        if more:
                            split_u(g + 1, j)
                    if more:
                        for j in range(2):
                            split_v(g + 1, 1 - s, j, used_next)

                short_group(0, 0, 0)
                with act.Fori(0, SHORT // 2 - 1) as i:
                    short_group(2 * i + 1, 1, 32 * i)
                    short_group(2 * i + 2, 0, 32 * i + 16)
                short_group(SHORT - 1, 1, 16 * (SHORT - 2))
                for j in range(2):
                    split_u(SHORT, j)
                for j in range(2):
                    split_v(SHORT, 0, j, 16 * (SHORT - 1))
                group(SHORT, 0, 16 * (SHORT - 1), 16 * SHORT)
                with act.Fori(SHORT // 2, (NG - 2) // 2) as i:
                    group(2 * i + 1, 1, 32 * i, 32 * i + 16)
                    group(2 * i + 2, 0, 32 * i + 16, 32 * i + 32)
                group(NG - 1, 1, 16 * (NG - 2), 0, more=False)

                def root_of(t):
                    act.wait_ge(aggr, t + 1)
                    nc.scalar.activation(root[:, t:t + 1], mv[:, t, 1:2], ACT.Sqrt,
                                         bias=cst[:, C_EPS:C_EPS + 1]).then_inc(rooted, 1)

                root_of(0)
                for t in range(NT):
                    if t + 1 < NT:
                        root_of(t + 1)
                    act.wait_ge(shifted, t + 1)
                    nc.scalar.activation(y[:, t, :], y[:, t, :], ACT.Identity, scale=rstd[:, t:t + 1],
                                         bias=shift[:, t:t + 1]).then_inc(nrm, 1)

            @block.vector
            def _(dve):
                def split_u(g, j):
                    dve.wait_ge(u_hi[j], g - SHORT + 1)
                    nc.vector.tensor_tensor(ul[j][:], ur[j][:], uh[j][:].bitcast(F32), ALU.subtract).then_inc(u_lo[j], 1)

                def split_v(g, s, j):
                    dve.wait_ge(v_hi[j], g + 1)
                    nc.vector.tensor_tensor(vl[s][j][:], vr[:], vh[s][j][:].bitcast(F32),
                                            ALU.subtract).then_inc(v_lo[j], 1)

                def weigh(g, s, j, short=True):
                    dve.wait_ge(g_in[j], 16 * (g + 1))
                    if short:
                        dve.wait_ge(u_in[j], 16 * (g + 1))
                    for n in range(2):
                        if short:
                            dve.wait_ge(a_lo[1 - j][n], g + j)
                            src = ur[j].rearrange("p k e -> p (k e)")[:, n * HALF:(n + 1) * HALF]
                        else:
                            dve.wait_ge(gelu[j][n], g - SHORT + 1)
                            src = av[n][:]
                        nc.vector.tensor_tensor(av[n][:], src,
                                                gt[j][:, n * HALF // TG:(n + 1) * HALF // TG, :].rearrange("p t q -> p (t q)"),
                                                ALU.mult).then_inc(a_mul[j][n], 1)
                    for n in range(2):
                        dve.wait_ge(a_hi[j][n], g + 1)
                        c = slice(n * HALF, (n + 1) * HALF)
                        nc.vector.tensor_tensor(al[s][j][:, c], av[n][:], ah[s][j][:, c].bitcast(F32),
                                                ALU.subtract).then_inc(a_lo[j][n], 1)

                def gather(g, q0, q1, first=False):
                    for q in range(q0, q1):
                        t, n = divmod(q, 2)
                        c = slice(n * HALF, (n + 1) * HALF)
                        dve.wait_ge(y_mm, 16 * g + q + 1)
                        if first:
                            dve.wait_ge(y_ready, t + 1)
                        nc.vector.tensor_tensor(y[:, t, c], y[:, t, c], psum[:, 4 + q % 4, :], ALU.add).then_inc(y_add[q % 4], 1)

                def short_group(g, s, before=True, first=False):
                    for n, prepare in enumerate((weigh, weigh, split_v, split_v)):
                        prepare(g, s, n % 2)
                        if before:
                            gather(g - 1, 4 * n, 4 * n + 4, first)

                def group(g, s, more=True, before=True):
                    weigh(g, s, 0, short=False)
                    if more:
                        split_u(g + 1, 0)
                    weigh(g, s, 1, short=False)
                    if before:
                        gather(g - 1, 0, 4)
                    if more:
                        split_u(g + 1, 1)
                    if before:
                        gather(g - 1, 4, 2 * NT)
                    if more:
                        for j in range(2):
                            split_v(g + 1, 1 - s, j)

                short_group(0, 0, before=False)
                short_group(1, 1, first=True)
                short_group(2, 0)
                with dve.Fori(1, SHORT // 2 - 1) as i:
                    short_group(2 * i + 1, 1)
                    short_group(2 * i + 2, 0)
                short_group(SHORT - 1, 1)
                for j in range(2):
                    split_u(SHORT, j)
                gather(SHORT - 1, 0, 4)
                for j in range(2):
                    split_v(SHORT, 0, j)
                gather(SHORT - 1, 4, 2 * NT)
                group(SHORT, 0, before=False)
                with dve.Fori(SHORT // 2, (NG - 2) // 2) as i:
                    group(2 * i + 1, 1)
                    group(2 * i + 2, 0)
                group(NG - 1, 1, more=False)

                def statistics(t):
                    for n in range(2):
                        q = 2 * t + n
                        dve.wait_ge(y_add[q % 4], 4 * (NG - 1) + q // 4 + 1)
                        nc.vector.bn_stats(st[:, t, n, :], y[:, t, n * HALF:(n + 1) * HALF]).then_inc(stat, 1)
                    dve.wait_ge(stat, 2 * (t + 1))
                    nc.vector.bn_aggr(mv[:, t, :], st[:, t]).then_inc(aggr, 1)

                def shift_of(t):
                    dve.wait_ge(rooted, t + 1)
                    nc.vector.reciprocal(rstd[:, t:t + 1], root[:, t:t + 1]).then_inc(inverted, 1)
                    dve.wait_ge(aggr, t + 1)
                    dve.wait_ge(inverted, t + 1)
                    nc.vector.scalar_tensor_tensor(shift[:, t:t + 1], mv[:, t, 0:1], -1.0, rstd[:, t:t + 1],
                                                   ALU.mult, ALU.mult).then_inc(shifted, 1)

                def weight(t):
                    dve.wait_ge(nrm, t + 1)
                    dve.wait_ge(u_in[0], ln_in)
                    nc.vector.tensor_tensor(y[:, t, :], y[:, t, :], lng, ALU.mult).then_inc(nrm_g, 1)

                for t in range(NT + 2):
                    if t < NT:
                        gather(NG - 1, 2 * t, 2 * t + 2)
                        statistics(t)
                    if 1 <= t <= NT:
                        shift_of(t - 1)
                    if t >= 2:
                        weight(t - 2)

            @block.gpsimd
            def _(pool):
                pool.wait_ge(x1_in, 16 * NT)
                for t in range(NT):
                    nc.gpsimd.tensor_scalar(y[:, t, :], y[:, t, :], ALPHA, None, ALU.mult).then_inc(y_ready, 1)
                pool.wait_ge(u_in[1], ln_in)
                for t in range(NT):
                    pool.wait_ge(nrm_g, t + 1)
                    nc.gpsimd.tensor_tensor(y[:, t, :], y[:, t, :], lnb, ALU.add).then_inc(done, 1)


def build(nc, io, out):
    with ExitStack() as ctx:
        scr = {
            "ch": nc.dram_tensor("s_ch", (N_CH, P, T), F32).ap(),
            "sk": nc.dram_tensor("s_sk", (P, P + T), F32).ap(),
            "sv": nc.dram_tensor("s_sv", (P + T, P), F32).ap(),
            "z": nc.dram_tensor("s_z", (T, GH * P), F32).ap(),
            "x1": nc.dram_tensor("s_x1", (T, D), F32).ap(),
            "hidden": nc.dram_tensor("s_hidden", (AHEAD, P, T), F32).ap(),
            "G": nc.dram_tensor("s_G", (T // TG, P, NK, TG), F32).ap(),
        }
        psum = ctx.enter_context(nc.psum_tensor("psum", [P, 8, HALF], F32))
        cst = ctx.enter_context(nc.sbuf_tensor("cst", [P, C_N], F32))
        cst_in = ctx.enter_context(nc.semaphore("cst_in"))
        with nc.Block() as block:
            @block.sync
            def _(sp):
                sp.dma_start(cst[:], io["consts"]).then_inc(cst_in, 16)
                sp.wait_ge(cst_in, 16)
        with ExitStack() as mixer:
            ba = mixer.enter_context(nc.sbuf_tensor("ba", [P, NT, 2 * GH], F32))
            with stage_semaphores(nc) as sem:
                project(nc, sem, io, scr, ba, cst, psum)
            with stage_semaphores(nc) as sem:
                mix_tokens(nc, sem, io, scr, ba, cst, psum)
        x1h = ctx.enter_context(nc.sbuf_tensor("x1h", [P, KC, T], F32R))
        x1l = ctx.enter_context(nc.sbuf_tensor("x1l", [P, KC, T], F32R))
        with stage_semaphores(nc) as sem:
            split_x1(nc, sem, scr, cst, psum, x1h, x1l)
        with ExitStack() as picks:
            key1, key2, gate = (picks.enter_context(nc.sbuf_tensor(n, [P, NT, PH * TOPK], F32))
                                for n in ("key1", "key2", "gate"))
            with stage_semaphores(nc) as sem:
                retrieve(nc, sem, io, scr, cst, psum, x1h, x1l, key1, key2, gate)
            with stage_semaphores(nc) as sem:
                build_gates(nc, sem, io, scr, cst, psum, x1h, x1l, key1, key2, gate)
        with ExitStack() as sums:
            y = sums.enter_context(nc.sbuf_tensor("y", [P, NT, D], F32))
            with stage_semaphores(nc) as sem:
                experts(nc, sem, io, scr, cst, psum, x1h, x1l, y, out)


def layout(inputs):
    a = {k: np.asarray(v) for k, v in inputs.items()}

    def blocks(w):
        return np.ascontiguousarray(w.reshape(KC, P, -1, P).transpose(2, 1, 0, 3))

    def rows(w):
        return np.ascontiguousarray(w.reshape(KC, P, -1).transpose(1, 0, 2))

    w = a["w_in"][0]
    q0 = 4 * GH * P + 2 * GH
    k0, v0 = q0 + AH * AD, q0 + AH * AD + 2 * AD
    order = np.concatenate([np.arange(AD) + (r * 4 + p) * AD for p in range(4) for r in range(2)])
    channels = np.concatenate([w[:, 0:3 * GH * P], w[:, q0 + order], w[:, k0:v0]], axis=1)
    keys = np.stack([a["peer_k1"][0], a["peer_k2"][0]], axis=1).transpose(0, 1, 3, 2).reshape(2 * PH, P, NK)
    return {
        "x": a["x"][0], "xT": np.ascontiguousarray(a["x"][0].T), "w_ch": blocks(channels),
        "w_tok": rows(np.concatenate([w[:, 3 * GH * P:4 * GH * P], w[:, v0:], w[:, 4 * GH * P:q0]], axis=1)),
        "conv_w": np.ascontiguousarray(a["gdn_conv_w"][0].reshape(4, N_CONV, P).transpose(2, 1, 0)),
        "a_log": a["gdn_a_log"][0], "dt_bias": a["gdn_dt_bias"][0], "norm_w": a["gdn_norm_w"][0],
        "sinks": a["swa_sinks"][0], "w_out": a["w_out"][0], "ln1_g": a["ln1_g"][0], "ln1_b": a["ln1_b"][0],
        "wq": blocks(a["peer_wq"][0]), "keysT": np.ascontiguousarray(keys),
        "uT": np.ascontiguousarray(a["peer_u"][0].reshape(NK, NK, KC, P).transpose(0, 3, 2, 1)),
        "v": a["peer_v"][0], "ln2_g": a["ln2_g"][0], "ln2_b": a["ln2_b"][0],
        "consts": constants(), "wmask": window_masks(),
    }


def kernel(**inputs):
    import concourse.bacc as bacc
    from concourse.bass_utils import run_bass_kernel_spmd

    nc = bacc.Bacc("TRN2", target_bir_lowering=False, num_devices=1)
    arrays = {f"in_{k}": v for k, v in layout(inputs).items()}
    io = {k[3:]: nc.dram_tensor(k, v.shape, mybir.dt.from_np(v.dtype), kind="ExternalInput").ap()
          for k, v in arrays.items()}
    out = nc.dram_tensor("out", (1, T, D), F32, kind="ExternalOutput").ap()
    build(nc, io, out)
    result = run_bass_kernel_spmd(nc, [arrays], core_ids=[0])
    return result.results[0]["out"]
```
